# Optimizing a Trainium2 kernel written in Bass

```python
import jax, jax.numpy as jnp
from jax import lax
import numpy as np

D_MODEL = 1024
BATCH = 1
SEQ = 1024
DEPTH = 1

D_MIX = D_MODEL
D_HGRN = D_MIX // 2
HGRN_HEAD_DIM = 128
HGRN_HEADS = D_HGRN // HGRN_HEAD_DIM
HGRN_CHUNK = 64
D_RG = D_MIX - D_HGRN
RG_BLOCKS = 8
RG_BLOCK_DIM = D_RG // RG_BLOCKS
CONV_WIDTH = 4
RG_C = 8.0
D_IN = 4 * D_HGRN + 2 * D_RG
N_GROUPS = 4
EXPERTS_PER_GROUP = 8
N_EXPERTS = N_GROUPS * EXPERTS_PER_GROUP
TOP_K = 2
D_EXPERT = D_MODEL // 2
MOE_BLOCK = 256
EPS = 1e-6

kernel_name = "hybrid_hgrn2_rglru_hmoe_block"

def rmsnorm(x, g):
    xf = x.astype(jnp.float32)
    y = xf * lax.rsqrt(jnp.mean(xf * xf, axis=-1, keepdims=True) + EPS)
    return (y * g.astype(jnp.float32)).astype(x.dtype)

def hgrn2_chunkwise(q, k, v, log_f):
    B, S, H, K = q.shape
    V = v.shape[-1]
    N = S // HGRN_CHUNK

    def to_chunks(t):
        return t.reshape(B, N, HGRN_CHUNK, H, t.shape[-1]).transpose(1, 0, 3, 2, 4)

    mask = jnp.tril(jnp.ones((HGRN_CHUNK, HGRN_CHUNK), dtype=bool))[:, :, None]

    def step(state, inp):
        qc, kc, vc, gc = inp
        b = jnp.cumsum(gc, axis=-2)
        diff = b[:, :, :, None, :] - b[:, :, None, :, :]
        decay = jnp.exp(jnp.where(mask, diff, -jnp.inf))
        scores = jnp.einsum('bhtk,bhtsk,bhsk->bhts', qc, decay, kc)
        o = jnp.einsum('bhts,bhsv->bhtv', scores, vc) + jnp.einsum('bhtk,bhkv->bhtv', qc * jnp.exp(b), state)
        b_last = b[:, :, -1:, :]
        new_state = jnp.exp(b_last[:, :, 0, :, None]) * state + jnp.einsum('bhsk,bhsv->bhkv', kc * jnp.exp(b_last - b), vc)
        return new_state, o

    s0 = jnp.zeros((B, H, K, V), jnp.float32)
    _, o = lax.scan(step, s0, (to_chunks(q), to_chunks(k), to_chunks(v), to_chunks(log_f)))
    return o.transpose(1, 0, 3, 2, 4).reshape(B, S, H, V)

def causal_dwconv(x, w, b):
    y = lax.conv_general_dilated(x, w[:, None, :].astype(x.dtype), window_strides=(1,),
                                 padding=[(CONV_WIDTH - 1, 0)],
                                 dimension_numbers=('NWC', 'WIO', 'NWC'),
                                 feature_group_count=x.shape[-1])
    return y + b.astype(x.dtype)

def rg_lru(xc, w_r, b_r, w_i, b_i, lam):
    B, S, R = xc.shape
    xh = xc.reshape(B, S, RG_BLOCKS, RG_BLOCK_DIM)
    r = jax.nn.sigmoid(jnp.einsum('bshi,hij->bshj', xh, w_r.astype(jnp.float32)).reshape(B, S, R) + b_r.astype(jnp.float32))
    i = jax.nn.sigmoid(jnp.einsum('bshi,hij->bshj', xh, w_i.astype(jnp.float32)).reshape(B, S, R) + b_i.astype(jnp.float32))
    log_a = RG_C * r * jax.nn.log_sigmoid(lam.astype(jnp.float32))
    a = jnp.exp(log_a)
    u = jnp.sqrt(-jnp.expm1(2.0 * log_a)) * (i * xc)

    def combine(lhs, rhs):
        a1, b1 = lhs
        a2, b2 = rhs
        return a1 * a2, a2 * b1 + b2

    _, h = lax.associative_scan(combine, (a, u), axis=1)
    return h

def hier_moe(h, w_rg, b_rg, w_re, b_re, w1, w3, w2):
    T, D = h.shape
    logits_g = (h @ w_rg + b_rg).astype(jnp.float32)
    p_g = jax.nn.softmax(logits_g, axis=-1)
    g_star = jnp.argmax(p_g, axis=-1)
    gate_g = jnp.max(p_g, axis=-1)
    logits_e = (h @ w_re + b_re).astype(jnp.float32).reshape(T, N_GROUPS, EXPERTS_PER_GROUP)
    sel = jnp.take_along_axis(logits_e, g_star[:, None, None], axis=1)[:, 0]
    p_e = jax.nn.softmax(sel, axis=-1)
    top_v, top_i = lax.top_k(p_e, TOP_K)
    w_tok = top_v / jnp.sum(top_v, axis=-1, keepdims=True) * gate_g[:, None]

    eid = (g_star[:, None] * EXPERTS_PER_GROUP + top_i).reshape(-1).astype(jnp.int32)
    tok = jnp.repeat(jnp.arange(T, dtype=jnp.int32), TOP_K)
    wflat = w_tok.reshape(-1)
    A = T * TOP_K
    n_blocks = -(-A // MOE_BLOCK) + N_EXPERTS
    P = n_blocks * MOE_BLOCK

    order = jnp.argsort(eid)
    s_eid = eid[order]
    counts = jnp.zeros((N_EXPERTS,), jnp.int32).at[eid].add(1)
    starts = jnp.cumsum(counts) - counts
    pcounts = (counts + MOE_BLOCK - 1) // MOE_BLOCK * MOE_BLOCK
    pends = jnp.cumsum(pcounts)
    pstarts = pends - pcounts
    dest = pstarts[s_eid] + (jnp.arange(A, dtype=jnp.int32) - starts[s_eid])
    buf_tok = jnp.full((P,), T, jnp.int32).at[dest].set(tok[order])
    buf_w = jnp.zeros((P,), jnp.float32).at[dest].set(wflat[order])
    blk_e = jnp.minimum(jnp.searchsorted(pends, jnp.arange(n_blocks, dtype=jnp.int32) * MOE_BLOCK, side='right'),
                        N_EXPERTS - 1).astype(jnp.int32)

    h_pad = jnp.concatenate([h, jnp.zeros((1, D), h.dtype)], axis=0)
    xb = h_pad[buf_tok].reshape(n_blocks, MOE_BLOCK, D)

    def expert_block(args):
        xblk, e = args
        return (jax.nn.silu(xblk @ w1[e]) * (xblk @ w3[e])) @ w2[e]

    yb = lax.map(expert_block, (xb, blk_e)).reshape(P, D)
    out = jnp.zeros((T + 1, D), yb.dtype).at[buf_tok].add(yb * buf_w[:, None].astype(yb.dtype))
    return out[:T]

def setup_inputs(seed: int = 0) -> dict:
    key = jax.random.key(seed)
    ks = jax.random.split(key, 28)
    f32 = jnp.float32

    def nrm(k, shape, fan_in):
        return jax.random.normal(k, shape, f32) * (fan_in ** -0.5)

    def gain(k, n):
        return 1.0 + 0.05 * jax.random.normal(k, (DEPTH, n), f32)

    def small(k, shape):
        return 0.01 * jax.random.normal(k, shape, f32)

    u = jax.random.uniform(ks[17], (DEPTH, D_RG), f32, minval=0.9, maxval=0.999)
    s = u ** (1.0 / RG_C)
    rg_lambda = jnp.log(s) - jnp.log1p(-s)
    return {
        "x": jax.random.normal(ks[0], (BATCH, SEQ, D_MODEL), f32),
        "c": jax.random.normal(ks[1], (BATCH, D_MODEL), f32),
        "w_ada": 0.5 * nrm(ks[2], (DEPTH, D_MODEL, 6 * D_MODEL), D_MODEL),
        "b_ada": small(ks[3], (DEPTH, 6 * D_MODEL)),
        "g_pre_mix": gain(ks[4], D_MODEL),
        "g_post_mix": gain(ks[5], D_MODEL),
        "g_pre_ffn": gain(ks[6], D_MODEL),
        "g_post_ffn": gain(ks[7], D_MODEL),
        "w_in": nrm(ks[8], (DEPTH, D_MODEL, D_IN), D_MODEL),
        "hgrn_gamma": jax.random.normal(ks[9], (DEPTH + 1, D_HGRN), f32),
        "hgrn_norm_g": gain(ks[10], D_HGRN),
        "conv_w": nrm(ks[11], (DEPTH, CONV_WIDTH, D_RG), CONV_WIDTH),
        "conv_b": small(ks[12], (DEPTH, D_RG)),
        "rg_w_r": nrm(ks[13], (DEPTH, RG_BLOCKS, RG_BLOCK_DIM, RG_BLOCK_DIM), RG_BLOCK_DIM),
        "rg_b_r": small(ks[14], (DEPTH, D_RG)),
        "rg_w_i": nrm(ks[15], (DEPTH, RG_BLOCKS, RG_BLOCK_DIM, RG_BLOCK_DIM), RG_BLOCK_DIM),
        "rg_b_i": small(ks[16], (DEPTH, D_RG)),
        "rg_lambda": rg_lambda,
        "rg_norm_g": gain(ks[18], D_RG),
        "w_out": nrm(ks[19], (DEPTH, D_MIX, D_MODEL), D_MIX),
        "w_router_group": nrm(ks[20], (DEPTH, D_MODEL, N_GROUPS), D_MODEL),
        "b_router_group": small(ks[21], (DEPTH, N_GROUPS)),
        "w_router_expert": nrm(ks[22], (DEPTH, D_MODEL, N_EXPERTS), D_MODEL),
        "b_router_expert": small(ks[23], (DEPTH, N_EXPERTS)),
        "w1": nrm(ks[24], (DEPTH, N_EXPERTS, D_MODEL, D_EXPERT), D_MODEL),
        "w3": nrm(ks[25], (DEPTH, N_EXPERTS, D_MODEL, D_EXPERT), D_MODEL),
        "w2": nrm(ks[26], (DEPTH, N_EXPERTS, D_EXPERT, D_MODEL), D_EXPERT),
    }

def reference(x, c, w_ada, b_ada, g_pre_mix, g_post_mix, g_pre_ffn, g_post_ffn, w_in, hgrn_gamma,
              hgrn_norm_g, conv_w, conv_b, rg_w_r, rg_b_r, rg_w_i, rg_b_i, rg_lambda, rg_norm_g, w_out,
              w_router_group, b_router_group, w_router_expert, b_router_expert, w1, w3, w2):
    B, S, D = x.shape
    lb_table = jnp.cumsum(jax.nn.softmax(hgrn_gamma.astype(jnp.float32), axis=0), axis=0)
    for l in range(DEPTH):
        mod = jax.nn.silu(c) @ w_ada[l] + b_ada[l]
        sh1, sc1, gt1, sh2, sc2, gt2 = [m[:, None, :] for m in jnp.split(mod, 6, axis=-1)]

        h = rmsnorm(x, g_pre_mix[l]) * (1.0 + sc1) + sh1
        proj = h @ w_in[l]
        q, fz, iv, gz, xr, yr = jnp.split(proj, [D_HGRN, 2 * D_HGRN, 3 * D_HGRN, 4 * D_HGRN, 4 * D_HGRN + D_RG], axis=-1)

        lb = lb_table[l]
        fz32 = fz.astype(jnp.float32)
        f = lb + (1.0 - lb) * jax.nn.sigmoid(fz32)
        k_in = (1.0 - lb) * jax.nn.sigmoid(-fz32)
        hs = (B, S, HGRN_HEADS, HGRN_HEAD_DIM)
        o_a = hgrn2_chunkwise(jax.nn.silu(q.astype(jnp.float32)).reshape(hs), k_in.reshape(hs),
                              iv.astype(jnp.float32).reshape(hs), jnp.log(f).reshape(hs))
        o_a = rmsnorm(o_a, hgrn_norm_g[l].reshape(HGRN_HEADS, HGRN_HEAD_DIM)).reshape(B, S, D_HGRN)
        o_a = (o_a * jax.nn.silu(gz.astype(jnp.float32))).astype(x.dtype)

        xc = causal_dwconv(xr, conv_w[l], conv_b[l]).astype(jnp.float32)
        hr = rg_lru(xc, rg_w_r[l], rg_b_r[l], rg_w_i[l], rg_b_i[l], rg_lambda[l])
        o_b = rmsnorm(hr * jax.nn.gelu(yr.astype(jnp.float32)), rg_norm_g[l]).astype(x.dtype)

        mix = jnp.concatenate([o_a, o_b], axis=-1) @ w_out[l]
        x = x + gt1 * rmsnorm(mix, g_post_mix[l])

        h = rmsnorm(x, g_pre_ffn[l]) * (1.0 + sc2) + sh2
        y = hier_moe(h.reshape(B * S, D), w_router_group[l], b_router_group[l], w_router_expert[l],
                     b_router_expert[l], w1[l], w3[l], w2[l]).reshape(B, S, D)
        x = x + gt2 * rmsnorm(y, g_post_ffn[l])
    return x


_drawn_inputs = setup_inputs


def setup_inputs(seed=0):
    import zlib

    import numpy as np

    out = dict(_drawn_inputs(seed))
    spreads = {}
    factors = {'g_post_ffn': 4.133, 'rg_b_r': 8.0, 'rg_b_i': 8.0, 'b_router_group': 6.279}
    for name, (base, spread) in spreads.items():
        noise = np.random.default_rng([zlib.crc32(name.encode()), seed]).standard_normal(out[name].shape)
        drawn = base * np.exp(spread * noise) if base else spread * noise
        out[name] = __import__('jax').numpy.asarray(drawn.astype(out[name].dtype))
    for name, factor in factors.items():
        out[name] = (out[name] * factor).astype(out[name].dtype)
    return out
```

```python
import numpy as np
import concourse.bass as bass
from concourse import mybir

F32 = mybir.dt.float32
I32 = mybir.dt.int32
ALU = mybir.AluOpType
ACT = mybir.ActivationFunctionType
AX = mybir.AxisListType

P = 128
D = 1024
T = 1024
KD = D // P
NT = T // P
HALF = 512
CH = 512
HEADS = 4
CT = CH // P
NG, EPG = 4, 8
NE = NG * EPG
FE = D // 2
KF = FE // P
NCHUNK = T // P
LEVELS = (2, 4, 8, 16, 32, 64)
N_OVER = (2 * T - NE) // P
N_BLOCKS = NE + N_OVER
EPS = 1e-6

PARAM = {}
_at = 0
for _name, _n in (("c", 8), ("g_pre", 8), ("b_ada", 16), ("gam0", 4), ("gam1", 4), ("hg", 4), ("cw0", 4), ("cw1", 4),
                  ("cw2", 4), ("cw3", 4), ("cb", 4), ("br", 4), ("bi", 4), ("lam", 4), ("rgg", 4), ("rbias", 36)):
    PARAM[_name] = (_at, _n)
    _at += _n
N_PARAM = _at
CONST = {}
_at = 0
for _name, _n in (("ident", P), ("ones", P), ("upper", P), ("iota128", P), ("iota47", N_BLOCKS), ("iota32", NE),
                  ("iota15", N_OVER), ("tok", NT), ("rev4", 4), ("rev8", 8)):
    CONST[_name] = (_at, _n)
    _at += _n
N_CONST = _at
MASK_BASE = P


def mixer_steps():
    steps = []
    ada = iter(range(16))

    def fill(name, ct, half):
        steps.append(("proj", name, ct, half))

    for ct in range(CT):
        fill("xr", ct, 0)
        if ct:
            steps.append(("gate", ct - 1))
            steps.append(("scan", ct - 1))
        fill("xr", ct, 1)
        steps.append(("conv", ct))
    fill("yr", 0, 0)
    steps.append(("gate", CT - 1))
    steps.append(("scan", CT - 1))
    fill("yr", 0, 1)
    steps.append(("gelu_mul", 0))
    pending = []

    def ada_step():
        u = next(ada, None)
        if pending:
            steps.append(("row", pending.pop(0)))
        if u is not None:
            steps.append(("ada", u))
            pending.append(u)

    for ct in range(1, CT):
        fill("yr", ct, 0)
        ada_step()
        fill("yr", ct, 1)
        steps.append(("gelu_mul", ct))
    for h in range(HEADS):
        fill("q", h, 0)
        ada_step()
        fill("q", h, 1)
        if h == 0:
            steps.append(("rg_norm",))
    for h in range(HEADS):
        fill("f", h, 0)
        ada_step()
        fill("f", h, 1)
        steps.append(("prep", h))
    level_steps = [("base", h) for h in range(HEADS)] + [("level", m, h) for m in LEVELS for h in range(HEADS)]
    fills = [("iv", i, 0) for i in range(NT)] + [("gz", h, half) for h in range(HEADS) for half in range(2)]
    n = 0
    for i, f in enumerate(fills):
        fill(*f)
        if i % 2 == 0 or pending:
            ada_step()
        for _ in range(2 if i % 4 != 3 else 1):
            if n < len(level_steps):
                steps.append(level_steps[n])
                n += 1
    while pending:
        ada_step()
    steps += level_steps[n:]
    return steps


STEPS = mixer_steps()
GROUPS = {s[1:]: n for n, s in enumerate([s for s in STEPS if s[0] == "proj"])}
LEVEL_ORDER = {s: n for n, s in enumerate([s for s in STEPS if s[0] in ("base", "level")])}
PIECES = ["xr", "yr", "q", "f", "iv", "gz"]
PIECE_COL = {"q": 0, "f": 512, "iv": 1024, "gz": 1536, "xr": 2048, "yr": 2560}


def build(nc, x, x_t, params, consts, masks, w_ada, mod_rows, w_in, w_r, w_i, w_out, w_route, w1, w3, w2, out):
    KB = 256
    arena = nc.alloc_sbuf_tensor("arena", [P, 207 * KB], F32)
    ps = nc.alloc_psum_tensor("banks", [P, 8, HALF], F32)
    h2_rows = nc.dram_tensor("h2_rows", [T, D], F32).ap()
    y_rows = nc.dram_tensor("y_rows", [N_BLOCKS * P, D], F32).ap()
    mod_raw = nc.dram_tensor("mod_raw", [8, HALF], F32).ap()
    mod_done = nc.dram_tensor("mod_done", [8, HALF], F32).ap()

    def region(kb, cols, dtype=None):
        a = arena[:, int(kb * KB):int(kb * KB) + cols]
        return a if dtype is None else a.bitcast(dtype)

    def region3(kb, a, b):
        return region(kb, a * b).rearrange("p (a b) -> p a b", a=a)

    ring = [region3(kb, KD, HALF) for kb in (0, 16)]
    hT = region3(32, KD, T)
    fbuf = region3(64, HEADS, T)
    qbuf = region3(80, HEADS, T)
    kbuf = region3(96, HEADS, T)
    pbuf = region3(112, HEADS, T)
    vbuf = region3(128, NCHUNK, CH)
    gzbuf = region3(144, HEADS, T)
    rgbuf = region3(160, CT, T)
    t2buf = region3(176, HEADS, HALF)
    early = [region3(kb, KD, HALF) for kb in (64, 80, 128, 144)]
    sq = region3(96, 2, T)
    rbc = region(104, T)
    acc_early = region3(108, 2, HALF)
    gy = region3(128, CT, T)
    xc, rgate, igate, th = (region(112 + 4 * n, T) for n in range(4))
    k_nat, states = region3(32, 2, T), region3(40, 2, T)
    osq, orr = region3(48, 2, T), region3(56, 2, T)
    modbc = region(128, 4 * T).rearrange("p (a b) -> p a b", a=4)
    x1 = region(96, NT * T).rearrange("p (a b) -> p a b", a=NT)
    xtile = region3(176, 2, T)
    h2 = region3(32, 2, T)
    junk = region(88, T)
    h2T = region3(80, 2, T)
    x_ring = region3(144, 2, D)
    xT_e = region3(152, 2, D)
    sil = region(160, FE)
    gbuf = region(162, FE)
    gT = region(164, FE)
    y_sb = region3(166, 2, D)
    m_slots = [region3(kb, KD, HALF) for kb in (32, 48, 0, 16, 64, 80)]
    m_slots2 = [region3(kb, KF, D) for kb in (32, 48, 0, 16, 64, 80)]

    at = [184 * KB]

    def small(cols, dtype=None):
        a = arena[:, at[0]:at[0] + cols]
        at[0] += cols
        return a if dtype is None else a.bitcast(dtype)

    con = small(N_CONST)
    par = small(N_PARAM)
    msk = small(MASK_BASE + 64 * len(LEVELS), I32)
    wrt = small(KD * 36).rearrange("p (a b) -> p a b", a=KD)
    bd = small(2 * CT * P).rearrange("p (g c j) -> p g c j", g=2, c=CT)
    A1, SH1 = small(8), small(8)
    lb, omlb, cl = small(4), small(4), small(4)
    eps = small(1)
    cs = small(8)
    tiny = small(4 * 12).rearrange("p (a b) -> p a b", a=12)
    ptot = small(HEADS * 8).rearrange("p (a b) -> p a b", a=HEADS)
    ssq = small(3 * 8).rearrange("p (a b) -> p a b", a=3)
    rst = small(3 * 8).rearrange("p (a b) -> p a b", a=3)
    acc = small(2 * 256).rearrange("p (a b) -> p a b", a=2)
    ada_at = at[0]
    ada_half = small(KD * 256).rearrange("p (a b) -> p a b", a=KD)
    rowt = small(2 * 256).rearrange("p (a b) -> p a b", a=2)
    assert at[0] <= 207 * KB, at[0] / KB
    m_all, m_pre = region3(76, NT, NE), region3(77, NT + 1, NE)
    modfix = region3(64, 4, HALF)
    rat = [ada_at]

    def keep(cols, dtype=None):
        a = arena[:, rat[0]:rat[0] + cols]
        rat[0] += cols
        assert rat[0] <= at[0]
        return a if dtype is None else a.bitcast(dtype)

    wtok = keep(16).rearrange("p (j t) -> p j t", j=2)
    yidx = keep(16, I32).rearrange("p (j t) -> p j t", j=2)
    tbl = keep(N_BLOCKS, I32)
    over = keep(16, I32)
    xidx = keep(2, I32)
    a_oh = keep(2 * P).rearrange("p (a b) -> p a b", a=2)
    b_oh = keep(2 * N_BLOCKS).rearrange("p (a b) -> p a b", a=2)

    def C(name, rows=P):
        o, n = CONST[name]
        return con[0:rows, o:o + n]

    def PR(name, i=None):
        o, n = PARAM[name]
        return par[:, o:o + n] if i is None else par[:, o + i:o + i + 1]

    ident, ones = C("ident"), C("ones")

    def sem(name):
        return nc.alloc_semaphore(name)

    ld_par, ld_con, ld_msk, ld_wrt, ld_bd, ld_fix, ld_mod = (sem(n) for n in
        ("ld_par", "ld_con", "ld_msk", "ld_wrt", "ld_bd", "ld_fix", "ld_mod"))
    ld_x = [sem(f"ld_x{i}") for i in range(2)]
    ld_early = [sem(f"ld_early{i}") for i in range(4)]
    ld_ring = [sem(f"ld_ring{i}") for i in range(2)]
    ld_ada = sem("ld_ada")
    ld_xt = [sem(f"ld_xtile{i}") for i in range(2)]
    ld_m = [sem(f"ld_expert{i}") for i in range(6)]
    ld_g = [sem(f"ld_gather{i}") for i in range(2)]
    (bd_zero, cs_ready, sq_ready, sq_summed, rms_ready, xs_ready, acc_ready, modc_ready, a1_ready, h_ready,
     proj_done, evac_done, conv_done, gate_mm, gates_ready, sqrt_in, sqrt_out, scan_done, gmul_done, rgsq_ready,
     rgsq_summed, rgrms_ready, ob_ready, row_mm, row_ready, row_sent, p_zero, prep_done, step_mm, merged, updated,
     kt_mm, kt_ready, ds_mm, st_ready, o_mm, osq_ready, os_mm, orr_ready, oa_ready, fix_ready, fix_sent,
     mix_mm, ss_ready, sd_ready, r1_ready, x1_ready, r2_ready, h2_ready, h2_sent, h2t_mm, h2t_ready, logit_mm,
     lg_ready, ex_ready, mm_ready, rank_mm, ab_ready, tab_mm, route_ready, dve_chain, act_chain, pool_chain,
     lbin_ready, lbexp_ready) = (sem(n) for n in
        ("bd_zero cs_ready sq_ready sq_summed rms_ready xs_ready acc_ready modc_ready a1_ready h_ready "
         "proj_done evac_done conv_done gate_mm gates_ready sqrt_in sqrt_out scan_done gmul_done rgsq_ready "
         "rgsq_summed rgrms_ready ob_ready row_mm row_ready row_sent p_zero prep_done step_mm merged updated "
         "kt_mm kt_ready ds_mm st_ready o_mm osq_ready os_mm orr_ready oa_ready fix_ready fix_sent "
         "mix_mm ss_ready sd_ready r1_ready x1_ready r2_ready h2_ready h2_sent h2t_mm h2t_ready logit_mm "
         "lg_ready ex_ready mm_ready rank_mm ab_ready tab_mm route_ready dve_chain act_chain pool_chain "
         "lbin_ready lbexp_ready").split())
    (xg_tr, xt_ready, h1_mm, h3_mm, sil_ready, g_ready, g_tr, gt_ready, y_mm, y_act, y_dve, out_sent) = (sem(n) for n in
        "xg_tr xt_ready h1_mm h3_mm sil_ready g_ready g_tr gt_ready y_mm y_act y_dve out_sent".split())
    y_sent = [sem(f"y_sent{i}") for i in range(2)]
    ld_ov, ov_x, ov_xt, ov_h, ov_sil, ov_g, ov_gtr, ov_gt, ov_y, ov_ysb, ov_sent = (sem(n) for n in
        "ld_ov ov_x ov_xt ov_h ov_sil ov_g ov_gtr ov_gt ov_y ov_ysb ov_sent".split())
    ov_xtr = sem("ov_xtr")
    ld_y = [sem(f"ld_y{i}") for i in range(2)]
    fin_a, fin_b, fin_s, fin_sd, fin_r, fin_g, fin_o = (sem(n) for n in "fin_a fin_b fin_s fin_sd fin_r fin_g fin_o".split())
    o_sent = [sem(f"o_sent{i}") for i in range(2)]
    ada_v = w_ada.rearrange("(k p) c -> p k c", p=P)
    win_v = w_in.rearrange("(k p) c -> p k c", p=P)
    wout_v = w_out.rearrange("(k p) c -> p k c", p=P)
    xt_v = x_t.rearrange("(k p) t -> p k t", p=P)
    w1_v = w1.rearrange("e (k p) c -> e p k c", p=P)
    w3_v = w3.rearrange("e (k p) c -> e p k c", p=P)
    w2_v = w2.rearrange("e (k p) c -> e p k c", p=P)

    def chain_of(eng, s):
        count = [0]

        def link(ins):
            count[0] += 1
            ins.then_inc(s, 1)
            eng.wait_ge(s, count[0])
        return link

    y_init = sem("y_init")
    passed = sem("passed")

    def stand(eng, s, value):
        eng.wait_ge(s, value)
        eng.sem_inc(passed, 1)

    def pairs(buf, m):
        return buf.rearrange("p (b two m) -> p b two m", two=2, m=m)

    def block_products(h, m):
        if m == 1:
            return fbuf[:, h, :]
        if m == 2:
            return t2buf[:, h, :]
        if m == P:
            return ptot[:, h, :]
        o = 512 - 1024 // m * 2
        return fbuf[:, h, o:o + T // m]

    def level_bank(s):
        n = LEVEL_ORDER[s]
        if s[0] == "base":
            return 4 + 2 * (n % 2), max(n - 1, 0)
        return 4 + n % 4, (max(n - 3, 0) if n >= 8 else (3 if n < 6 else 4))

    block_cm = nc.Block()
    with block_cm as block:

        @block.sync
        def _(sp):
            sp.dma_start(par, params).then_inc(ld_par, 16)
            for i in range(2):
                sp.dma_start(hT[:, 4 * i:4 * i + 4, :], xt_v[:, 4 * i:4 * i + 4, :]).then_inc(ld_x[i], 16)
            sp.dma_start(con, consts).then_inc(ld_con, 16)
            for n in range(4):
                sp.dma_start(early[n], ada_v[:, :, n * HALF:(n + 1) * HALF]).then_inc(ld_early[n], 16)
            for n in range(2):
                c = PIECE_COL[PIECES[n]]
                sp.dma_start(ring[n], win_v[:, :, c:c + HALF]).then_inc(ld_ring[n], 16)
            sp.wait_ge(bd_zero, 1)
            for g, w in enumerate((w_r, w_i)):
                wv = w.rearrange("(c two) i j -> two i c j", two=2)
                for two in range(2):
                    sp.dma_start(bd[64 * two:64 * two + 64, g, :, 64 * two:64 * two + 64], wv[two]).then_inc(ld_bd, 16)
            sp.dma_start(msk, masks).then_inc(ld_msk, 16)
            sp.dma_start(wrt, w_route).then_inc(ld_wrt, 16)
            sp.dma_start(y_rows[NE * P:NE * P + T, :], x).then_inc(y_init, 16)
            sp.dma_start(y_rows[NE * P + T:, :], x[0:N_OVER * P - T, :]).then_inc(y_init, 16)
            for n in range(2, 8):
                last = {0: ("xr", 3, 1), 1: ("yr", 3, 1), 2: ("q", 3, 1), 3: ("f", 3, 1), 4: ("iv", 7, 0), 5: ("gz", 3, 1)}[n - 2]
                sp.wait_ge(proj_done, GROUPS[last] + 1)
                if n < 6:
                    c = PIECE_COL[PIECES[n]]
                    src = win_v[:, :, c:c + HALF]
                else:
                    src = wout_v[:, :, (n - 6) * HALF:(n - 5) * HALF]
                sp.dma_start(ring[n % 2], src).then_inc(ld_ring[n % 2], 16)
            sp.wait_ge(row_sent, 16 * 16)
            sp.wait_ge(updated, len(LEVEL_ORDER))
            sp.dma_start(modfix[0:8, 0, :], mod_raw).then_inc(ld_fix, 16)
            sp.dma_start(modfix[0:8, 1:4, :], mod_rows).then_inc(ld_fix, 16)
            sp.wait_ge(fix_ready, 1)
            sp.dma_start(mod_done, modfix[0:8, 0, :]).then_inc(fix_sent, 16)
            sp.wait_ge(fix_sent, 16)
            sp.wait_ge(o_mm, HEADS)
            sp.dma_start(modbc, mod_done.rearrange("a b -> (a b)").partition_broadcast(P)
                         .rearrange("p (a b) -> p a b", a=4)).then_inc(ld_mod, 16)
            for i in range(NT):
                if i >= 2:
                    sp.wait_ge(x1_ready, i - 1)
                sp.dma_start(xtile[:, i % 2, :], x[i * P:(i + 1) * P, :]).then_inc(ld_xt[i % 2], 16)
            sp.wait_ge(mix_mm, NT)
            sp.dma_start(m_slots[2], w1_v[1]).then_inc(ld_m[2], 16)
            sp.dma_start(m_slots[3], w3_v[1]).then_inc(ld_m[3], 16)
            for i in range(2):
                sp.wait_ge(h2_sent, 16 * NT)
                sp.wait_ge(h2t_mm, NT)
                sp.dma_start(m_slots[i], (w1_v, w3_v)[i][0]).then_inc(ld_m[i], 16)
            sp.wait_ge(route_ready, 1)
            sp.dma_start(m_slots2[4], w2_v[0]).then_inc(ld_m[4], 16)
            sp.dma_start(m_slots[5], w1_v[2]).then_inc(ld_m[5], 16)
            sp.wait_ge(h1_mm, 1)
            sp.dma_start(m_slots[0], w3_v[2]).then_inc(ld_m[0], 16)
            sp.wait_ge(h3_mm, 1)
            sp.dma_start(m_slots2[1], w2_v[1]).then_inc(ld_m[1], 16)
            with sp.Fori(0, (NE - 4) // 2) as i:
                for odd in range(2):
                    b = 2 * i + (3 + odd)
                    s1, s3, s2 = (2, 3, 4) if odd == 0 else (5, 0, 1)
                    sp.wait_ge(h1_mm, b - 1)
                    sp.dma_start(m_slots[s1], w1_v[b]).then_inc(ld_m[s1], 16)
                    sp.wait_ge(h3_mm, b - 1)
                    sp.dma_start(m_slots[s3], w3_v[b]).then_inc(ld_m[s3], 16)
                    sp.wait_ge(y_mm, b - 2)
                    sp.dma_start(m_slots2[s2], w2_v[b - 1]).then_inc(ld_m[s2], 16)
            b = NE - 1
            sp.wait_ge(h1_mm, b - 1)
            sp.dma_start(m_slots[2], w1_v[b]).then_inc(ld_m[2], 16)
            sp.wait_ge(h3_mm, b - 1)
            sp.dma_start(m_slots[3], w3_v[b]).then_inc(ld_m[3], 16)
            sp.wait_ge(y_mm, b - 2)
            sp.dma_start(m_slots2[4], w2_v[b - 1]).then_inc(ld_m[4], 16)
            sp.wait_ge(h1_mm, b)
            sp.dma_start(m_slots2[5], w2_v[b]).then_inc(ld_m[5], 16)
            n_over = sp.value_load(over[0:1, 15:16], min_val=0, max_val=N_OVER)
            sp.wait_ge(y_mm, NE)
            with sp.Fori(0, N_OVER) as o:
                with sp.If(o < n_over):
                    e = sp.value_load(over[0:1, bass.ds(o, 1)], min_val=0, max_val=NE - 1)
                    sp.dma_start(m_slots[0], w1_v[bass.ds(e, 1)].rearrange("a p k c -> (a p) k c")).then_inc(ld_ov, 16)
                    sp.dma_start(m_slots[1], w3_v[bass.ds(e, 1)].rearrange("a p k c -> (a p) k c")).then_inc(ld_ov, 16)
                    sp.dma_start(m_slots2[2], w2_v[bass.ds(e, 1)].rearrange("a p k c -> (a p) k c")).then_inc(ld_ov, 16)
                    stand(sp, ov_sent, 16 * (o + 1))
            for i in range(NT):
                sp.wait_ge(fin_o, i + 1)
                sp.dma_start(out[i * P:(i + 1) * P, :], xtile[:, i % 2, :]).then_inc(o_sent[i % 2], 16)
            for i in range(2):
                sp.wait_ge(o_sent[i], 16 * NT // 2)

        @block.gpsimd
        def _(pool):
            link = chain_of(pool, pool_chain)
            link(pool.memset(eps, EPS))
            pool.memset(bd.rearrange("p g c j -> p (g c j)"), 0.0).then_inc(bd_zero, 1)
            for u in range(16):
                if u:
                    pool.wait_ge(acc_ready, 4 + u)
                c = 4 * HALF + u * 256
                pool.dma_start(ada_half, ada_v[:, :, c:c + 256]).then_inc(ld_ada, 16)
                if u == 3:
                    pool.wait_ge(ob_ready, CT)
                    pool.memset(pbuf.rearrange("p a b -> p (a b)"), 0.0).then_inc(p_zero, 1)
            for i in range(NT):
                pool.wait_ge(h2_ready, i + 1)
                pool.dma_start(h2_rows[i * P:(i + 1) * P, :], h2[:, i % 2, :]).then_inc(h2_sent, 16)
                pool.wait_ge(h2_sent, 16 * (i + 1))
            pool.wait_ge(route_ready, 1)

            pool_idx = sem("pool_idx")
            for b in range(2):
                pool.tensor_copy(xidx[:, b:b + 1], tbl[:, b:b + 1]).then_inc(pool_idx, 1)
                stand(pool, pool_idx, b + 1)
                pool.indirect_dma_start(x_ring[:, b, :], None, h2_rows,
                                        bass.IndirectOffsetOnAxis(ap=xidx[:, b:b + 1], axis=0)).then_inc(ld_g[b], 16)
            with pool.Fori(0, (NE - 2) // 2) as i:
                for q in range(2):
                    b = 2 * i + (2 + q)
                    pool.wait_ge(xg_tr, b - 1)
                    pool.tensor_copy(xidx[:, q:q + 1], tbl[:, bass.ds(b, 1)]).then_inc(pool_idx, 1)
                    stand(pool, pool_idx, b + 1)
                    pool.indirect_dma_start(x_ring[:, q, :], None, h2_rows,
                                            bass.IndirectOffsetOnAxis(ap=xidx[:, q:q + 1], axis=0)).then_inc(ld_g[q], 16)
            n_over = pool.value_load(over[0:1, 15:16], min_val=0, max_val=N_OVER)
            pool.wait_ge(xg_tr, NE)
            with pool.Fori(0, N_OVER) as o:
                with pool.If(o < n_over):
                    pool.tensor_copy(xidx[:, 0:1], tbl[:, bass.ds(o + NE, 1)]).then_inc(pool_idx, 1)
                    stand(pool, pool_idx, o + (NE + 1))
                    pool.indirect_dma_start(x_ring[:, 0, :], None, h2_rows,
                                            bass.IndirectOffsetOnAxis(ap=xidx[:, 0:1], axis=0)).then_inc(ov_x, 16)
                    stand(pool, ov_sent, 16 * (o + 1))
            pool.wait_ge(y_init, 32)
            for i in range(2):
                pool.wait_ge(y_sent[i], 16 * NE // 2)
            for i in range(NT):
                if i >= 2:
                    pool.wait_ge(fin_b, i - 1)
                for j in range(2):
                    k = 2 * (i % 2) + j
                    dst = (x_ring[:, 0, :], x_ring[:, 1, :], xT_e[:, 0, :], xT_e[:, 1, :])[k]
                    pool.indirect_dma_start(dst, None, y_rows,
                                            bass.IndirectOffsetOnAxis(ap=yidx[:, j, i:i + 1], axis=0)).then_inc(ld_y[i % 2], 16)

        @block.scalar
        def _(act):
            link = chain_of(act, act_chain)
            act.wait_ge(ld_par, 16)
            act.activation(cs, PR("c"), ACT.Silu).then_inc(cs_ready, 1)
            for k in range(KD):
                act.wait_ge(ld_x[k // 4], 16)
                if k >= 2:
                    act.wait_ge(sq_summed, k - 1)
                act.activation(sq[:, k % 2, :], hT[:, k, :], ACT.Square).then_inc(sq_ready, 1)
            act.wait_ge(lbin_ready, 1)
            act.activation(tiny[:, 0:3, :], tiny[:, 0:3, :], ACT.Exp).then_inc(lbexp_ready, 1)
            act.wait_ge(pool_chain, 1)
            act.wait_ge(sq_summed, KD)
            act.activation(rbc, ps[:, 0:2, :].rearrange("p a b -> p (a b)"), ACT.Sqrt, bias=eps, scale=1.0 / D).then_inc(rms_ready, 1)
            act.wait_ge(a1_ready, 1)
            for k in range(KD):
                act.wait_ge(xs_ready, k + 1)
                act.activation(hT[:, k, :], hT[:, k, :], ACT.Identity, bias=SH1[:, k:k + 1], scale=A1[:, k:k + 1]).then_inc(h_ready, 1)
            act.wait_ge(ld_bd, 64)
            n_row = 0
            for step in STEPS:
                kind = step[0]
                if kind == "proj":
                    _, name, a, half = step
                    g = GROUPS[step[1:]]
                    src = ps[:, g % 3, :]
                    cols = slice(half * HALF, (half + 1) * HALF)
                    act.wait_ge(proj_done, g + 1)
                    if name == "xr":
                        ins = act.activation(rgbuf[:, a, cols], src, ACT.Copy)
                    elif name == "yr":
                        act.wait_ge(a1_ready, 1)
                        ins = act.activation(gy[:, a, cols], src, ACT.Gelu_apprx_tanh)
                    elif name == "q":
                        ins = act.activation(qbuf[:, a, cols], src, ACT.Silu)
                    elif name == "f":
                        act.activation(fbuf[:, a, cols], src, ACT.Sigmoid)
                        ins = act.activation(kbuf[:, a, cols], src, ACT.Sigmoid, scale=-1.0)
                    elif name == "iv":
                        if a == 0:
                            act.wait_ge(ob_ready, CT)
                        ins = act.activation(vbuf[:, a, :], src, ACT.Copy)
                    else:
                        ins = act.activation(gzbuf[:, a, cols], src, ACT.Silu)
                    ins.then_inc(evac_done, 1)
                elif kind == "gate":
                    ct = step[1]
                    act.wait_ge(gate_mm, ct + 1)
                    if ct:
                        act.wait_ge(scan_done, ct)
                    act.activation(rgate, ps[:, 4:6, :].rearrange("p a b -> p (a b)"), ACT.Sigmoid, bias=PR("br", ct)).then_inc(gates_ready, 1)
                    act.activation(igate, ps[:, 6:8, :].rearrange("p a b -> p (a b)"), ACT.Sigmoid, bias=PR("bi", ct)).then_inc(gates_ready, 1)
                    act.wait_ge(gates_ready, 4 * ct + 1)
                    act.activation(th, rgate, ACT.Tanh, scale=cl[:, ct:ct + 1]).then_inc(gates_ready, 1)
                    act.wait_ge(gates_ready, 4 * ct + 3)
                    act.activation(rgate, rgate, ACT.Exp, scale=cl[:, ct:ct + 1]).then_inc(gates_ready, 1)
                elif kind == "scan":
                    ct = step[1]
                    act.wait_ge(sqrt_in, ct + 1)
                    act.activation(xc, xc, ACT.Sqrt, scale=-1.0).then_inc(sqrt_out, 1)
                elif kind == "rg_norm":
                    act.wait_ge(scan_done, CT)
                    for ct in range(CT):
                        act.wait_ge(gmul_done, ct + 1)
                        if ct >= 2:
                            act.wait_ge(rgsq_summed, ct - 1)
                        act.activation((xc, rgate)[ct % 2], rgbuf[:, ct, :], ACT.Square).then_inc(rgsq_ready, 1)
                    act.wait_ge(rgsq_summed, CT)
                    act.activation(igate, ps[:, 4:6, :].rearrange("p a b -> p (a b)"), ACT.Sqrt, bias=eps, scale=1.0 / CH).then_inc(rgrms_ready, 1)
                elif kind == "row":
                    u = step[1]
                    act.wait_ge(row_mm, u + 1)
                    if u >= 2:
                        act.wait_ge(row_sent, 16 * (u - 1))
                    act.activation(rowt[0:1, u % 2, :], ps[0:1, 3, (u % 2) * 256:(u % 2) * 256 + 256], ACT.Copy).then_inc(row_ready, 1)
                    act.wait_ge(row_ready, u + 1)
                    if u:
                        act.wait_ge(row_sent, 16 * u)
                    act.dma_start(mod_raw[u // 2:u // 2 + 1, (u % 2) * 256:(u % 2) * 256 + 256], rowt[0:1, u % 2, :]).then_inc(row_sent, 16)
            def k_out(h):
                act.wait_ge(kt_mm, h + 1)
                if h >= 2:
                    act.wait_ge(ds_mm, h - 1)
                act.activation(k_nat[:, h % 2, :], ps[:, 0:2, :].rearrange("p a b -> p (a b)"), ACT.Copy).then_inc(kt_ready, 1)

            def o_out(h):
                act.wait_ge(o_mm, h + 1)
                if h >= 2:
                    act.wait_ge(os_mm, h - 1)
                act.activation(osq[:, h % 2, :], ps[:, 4:6, :].rearrange("p a b -> p (a b)"), ACT.Square).then_inc(osq_ready, 1)
                act.wait_ge(os_mm, h + 1)
                if h >= 2:
                    act.wait_ge(oa_ready, h - 1)
                act.activation(orr[:, h % 2, :], ps[:, 6:8, :].rearrange("p a b -> p (a b)"), ACT.Sqrt, bias=eps, scale=1.0 / P).then_inc(orr_ready, 1)

            k_out(0)
            for h in range(HEADS):
                if h + 1 < HEADS:
                    k_out(h + 1)
                o_out(h)
            def h2_out(i):
                act.wait_ge(h2t_mm, i + 1)
                if i >= 2:
                    act.wait_ge(logit_mm, i - 1)
                act.activation(h2T[:, i % 2, :], ps[:, 4:6, :].rearrange("p a b -> p (a b)"), ACT.Copy).then_inc(h2t_ready, 1)

            for i in range(NT):
                act.wait_ge(mix_mm, i + 1)
                link(act.activation(junk, ps[:, 2 * (i % 2):2 * (i % 2) + 2, :].rearrange("p a b -> p (a b)"), ACT.Square, accum_out=ssq[:, 0, i:i + 1]))
                act.activation(ssq[:, 0, i:i + 1], ssq[:, 0, i:i + 1], ACT.Sqrt, bias=eps, scale=1.0 / D).then_inc(ss_ready, 1)
                if i:
                    h2_out(i - 1)
                act.wait_ge(x1_ready, i + 1)
                link(act.activation(junk, x1[:, i, :], ACT.Square, accum_out=ssq[:, 1, i:i + 1]))
                act.activation(ssq[:, 1, i:i + 1], ssq[:, 1, i:i + 1], ACT.Sqrt, bias=eps, scale=1.0 / D).then_inc(sd_ready, 1)
            h2_out(NT - 1)
            act.wait_ge(lg_ready, 1)
            lg = fbuf[:, 0, 0:NT * 36]
            act.activation(lg, lg, ACT.Exp).then_inc(ex_ready, 1)

            def x_out(b, q):
                act.wait_ge(xg_tr, b + 1)
                act.activation(xT_e[:, q, :], ps[:, 6:8, :].rearrange("p a b -> p (a b)"), ACT.Copy).then_inc(xt_ready, 1)

            def silu_out(b):
                act.wait_ge(h1_mm, b + 1)
                act.activation(sil, ps[:, 0, :], ACT.Silu).then_inc(sil_ready, 1)

            def y_out(b, q):
                act.wait_ge(y_mm, b + 1)
                act.activation(y_sb[:, q, 0:HALF], ps[:, 3, :], ACT.Copy).then_inc(y_act, 1)
                act.wait_ge(y_act, b + 1)
                act.wait_ge(y_dve, b + 1)
                act.dma_start(y_rows[bass.ds(b * P, P), :], y_sb[:, q, :]).then_inc(y_sent[q], 16)

            act.wait_ge(route_ready, 1)
            x_out(0, 0)
            silu_out(0)
            x_out(1, 1)
            for b in (1, 2):
                act.wait_ge(g_ready, b)
                silu_out(b)
                act.wait_ge(h3_mm, b)
                x_out(b + 1, (b + 1) % 2)
                y_out(b - 1, (b - 1) % 2)
            with act.Fori(0, (NE - 4) // 2) as i:
                for q in range(2):
                    b = 2 * i + (3 + q)
                    act.wait_ge(g_ready, b)
                    silu_out(b)
                    act.wait_ge(h3_mm, b)
                    x_out(b + 1, q)
                    act.wait_ge(y_sent[q], 16 * (i + 1))
                    y_out(b - 1, q)
            b = NE - 1
            act.wait_ge(g_ready, b)
            silu_out(b)
            act.wait_ge(y_sent[0], 16 * (NE // 2 - 1))
            y_out(b - 1, 0)
            act.wait_ge(y_sent[1], 16 * (NE // 2 - 1))
            y_out(b, 1)
            act.wait_ge(y_init, 32)
            n_over = act.value_load(over[0:1, 15:16], min_val=0, max_val=N_OVER)
            for q in range(2):
                act.wait_ge(y_sent[q], 16 * NE // 2)
            with act.Fori(0, N_OVER) as o:
                with act.If(o < n_over):
                    act.wait_ge(ov_xtr, o + 1)
                    act.activation(xT_e[:, 0, :], ps[:, 6:8, :].rearrange("p a b -> p (a b)"), ACT.Copy).then_inc(ov_xt, 1)
                    act.wait_ge(ov_h, o + 1)
                    act.activation(sil, ps[:, 0, :], ACT.Silu).then_inc(ov_sil, 1)
                    act.wait_ge(ov_y, o + 1)
                    act.activation(y_sb[:, 0, :], ps[:, 3:5, :].rearrange("p a b -> p (a b)"), ACT.Copy).then_inc(ov_ysb, 1)
                    act.wait_ge(ov_ysb, o + 1)
                    act.dma_start(y_rows[bass.ds((o + NE) * P, P), :], y_sb[:, 0, :]).then_inc(ov_sent, 16)
                    stand(act, ov_sent, 16 * (o + 1))
            for i in range(NT):
                act.wait_ge(ld_y[i % 2], 32 * (i // 2 + 1))
                r1 = x_ring[:, 0, :] if i % 2 == 0 else xT_e[:, 0, :]
                if i >= 2:
                    act.wait_ge(fin_g, i - 1)
                act.activation(y_sb[:, i % 2, :], r1, ACT.Copy, scale=wtok[:, 0, i:i + 1]).then_inc(fin_a, 1)
                act.wait_ge(fin_b, i + 1)
                link(act.activation(junk, y_sb[:, i % 2, :], ACT.Square, accum_out=ssq[:, 2, i:i + 1]))
                act.activation(ssq[:, 2, i:i + 1], ssq[:, 2, i:i + 1], ACT.Sqrt, bias=eps, scale=1.0 / D).then_inc(fin_s, 1)

        @block.vector
        def _(dve):
            link = chain_of(dve, dve_chain)
            dve.wait_ge(ld_par, 16)
            mx, e0, e1, ab, s0, s1, s2 = (tiny[:, n, :] for n in (3, 0, 1, 2, 4, 5, 6))
            link(dve.tensor_tensor(mx, PR("gam0"), PR("gam1"), ALU.max))
            dve.tensor_tensor(e0, PR("gam0"), mx, ALU.subtract)
            dve.tensor_tensor(e1, PR("gam1"), mx, ALU.subtract)
            link(dve.tensor_scalar(s0, PR("lam"), -1.0, None, ALU.mult))
            dve.tensor_tensor(ab, PR("lam"), s0, ALU.min).then_inc(lbin_ready, 1)
            dve.wait_ge(lbexp_ready, 1)
            link(dve.tensor_tensor(s0, e0, e1, ALU.add))
            link(dve.reciprocal(s1, s0))
            dve.tensor_tensor(lb, e0, s1, ALU.mult)
            dve.tensor_tensor(omlb, e1, s1, ALU.mult)
            link(dve.tensor_scalar(s0, ab, 2.0, None, ALU.add))
            link(dve.reciprocal(s0, s0))
            link(dve.tensor_tensor(s0, ab, s0, ALU.mult))
            link(dve.tensor_tensor(s1, s0, s0, ALU.mult))
            link(dve.memset(s2, 1.0 / 19.0))
            for n in range(17, 0, -2):
                link(dve.tensor_tensor(s2, s2, s1, ALU.mult))
                link(dve.tensor_scalar(s2, s2, 1.0 / n, None, ALU.add))
            link(dve.tensor_tensor(s2, s2, s0, ALU.mult))
            link(dve.tensor_scalar(s1, PR("lam"), 0.0, 8.0, ALU.min, ALU.mult))
            link(dve.scalar_tensor_tensor(cl, s2, -16.0, s1, ALU.mult, ALU.add))

            def ada_acc(dst, src, n):
                link(dve.tensor_scalar(dst, src[:, 0, :], cs[:, 0:1], None, ALU.mult))
                for k in range(1, KD):
                    ins = dve.scalar_tensor_tensor(dst, src[:, k, :], cs[:, k:k + 1], dst, ALU.mult, ALU.add)
                    if k < KD - 1:
                        link(ins)
                ins.then_inc(acc_ready, 1)

            dve.wait_ge(cs_ready, 1)
            for n in range(4):
                dve.wait_ge(ld_early[n], 16)
                if n >= 2:
                    dve.wait_ge(modc_ready, n - 1)
                ada_acc(acc_early[:, n % 2, :], early[n], n)
            dve.wait_ge(rms_ready, 1)
            link(dve.reciprocal(rbc, rbc))
            dve.wait_ge(modc_ready, 4)
            o = PARAM["b_ada"][0]
            dve.tensor_tensor(SH1, ps[:, 2, 0:8], par[:, o:o + 8], ALU.add)
            link(dve.tensor_tensor(A1, ps[:, 2, 8:16], par[:, o + 8:o + 16], ALU.add))
            dve.scalar_tensor_tensor(A1, A1, 1.0, PR("g_pre"), ALU.add, ALU.mult).then_inc(a1_ready, 1)
            for k in range(KD):
                dve.tensor_tensor(hT[:, k, :], hT[:, k, :], rbc, ALU.mult).then_inc(xs_ready, 1)
            for step in STEPS:
                kind = step[0]
                if kind == "conv":
                    ct = step[1]
                    dve.wait_ge(evac_done, GROUPS[("xr", ct, 1)] + 1)
                    if ct:
                        dve.wait_ge(scan_done, ct)
                    link(dve.tensor_scalar(xc, rgbuf[:, ct, :], PR("cw3", ct), PR("cb", ct), ALU.mult, ALU.add))
                    for j in range(1, 4):
                        ins = dve.scalar_tensor_tensor(xc[:, j:T], rgbuf[:, ct, 0:T - j], PR(f"cw{3 - j}", ct), xc[:, j:T], ALU.mult, ALU.add)
                        if j < 3:
                            link(ins)
                    ins.then_inc(conv_done, 1)
                elif kind == "gate":
                    ct = step[1]
                    dve.wait_ge(gates_ready, 4 * ct + 4)
                    dve.wait_ge(gate_mm, ct + 1)
                    link(dve.tensor_tensor(igate, igate, xc, ALU.mult))
                    link(dve.tensor_tensor(xc, rgate, rgate, ALU.mult))
                    dve.scalar_tensor_tensor(xc, xc, 1.0, th, ALU.add, ALU.mult).then_inc(sqrt_in, 1)
                    dve.wait_ge(sqrt_out, ct + 1)
                    link(dve.tensor_tensor(igate, igate, xc, ALU.mult))
                    dve.tensor_tensor_scan(rgbuf[:, ct, :], rgate, igate, 0.0, ALU.mult, ALU.add).then_inc(scan_done, 1)
                elif kind == "gelu_mul":
                    ct = step[1]
                    dve.wait_ge(evac_done, GROUPS[("yr", ct, 1)] + 1)
                    dve.wait_ge(scan_done, ct + 1)
                    dve.tensor_tensor(rgbuf[:, ct, :], rgbuf[:, ct, :], gy[:, ct, :], ALU.mult).then_inc(gmul_done, 1)
                elif kind == "ada":
                    u = step[1]
                    dve.wait_ge(ld_ada, 16 * (u + 1))
                    if u >= 2:
                        dve.wait_ge(row_mm, u - 1)
                    ada_acc(acc[:, u % 2, :], ada_half, u)
                elif kind == "rg_norm":
                    dve.wait_ge(rgrms_ready, 1)
                    link(dve.reciprocal(igate, igate))
                    for ct in range(CT):
                        dve.scalar_tensor_tensor(rgbuf[:, ct, :], rgbuf[:, ct, :], PR("rgg", ct), igate, ALU.mult, ALU.mult).then_inc(ob_ready, 1)
                elif kind == "prep":
                    h = step[1]
                    dve.wait_ge(evac_done, GROUPS[("f", h, 1)] + 1)
                    fo = pairs(fbuf[:, h, :], 1)[:, :, 1, :]
                    qo, ko = pairs(qbuf[:, h, :], 1)[:, :, 1, :], pairs(kbuf[:, h, :], 1)[:, :, 1, :]
                    rec = t2buf[:, h, :].unsqueeze(2)
                    dve.tensor_scalar(kbuf[:, h, :], kbuf[:, h, :], omlb[:, h:h + 1], None, ALU.mult)
                    link(dve.tensor_scalar(fbuf[:, h, :], fbuf[:, h, :], omlb[:, h:h + 1], lb[:, h:h + 1], ALU.mult, ALU.add))
                    dve.tensor_tensor(qo, qo, fo, ALU.mult)
                    link(dve.reciprocal(rec, fo))
                    dve.tensor_tensor(ko, ko, rec, ALU.mult).then_inc(prep_done, 1)
                elif kind == "base":
                    h = step[1]
                    n = LEVEL_ORDER[step]
                    bank, _ = level_bank(step)
                    dve.wait_ge(step_mm, n + 1)
                    if h == 0:
                        dve.wait_ge(p_zero, 1)
                        dve.wait_ge(ld_msk, 16)
                    v3 = lambda a: a.rearrange("p (c t) -> p c t", t=P)
                    dve.copy_predicated(v3(pbuf[:, h, :]), msk[:, 0:P].unsqueeze(1).to_broadcast([P, NCHUNK, P]),
                                        v3(ps[:, bank:bank + 2, :].rearrange("p a b -> p (a b)"))).then_inc(merged, 1)
                    q2, k2, f2 = (b[:, h, :].rearrange("p (b two) -> p b two", two=2) for b in (qbuf, kbuf, fbuf))
                    dve.tensor_tensor(q2, q2, f2[:, :, 0:1].to_broadcast([P, T // 2, 2]), ALU.mult)
                    dve.tensor_tensor(k2, k2, f2[:, :, 1:2].to_broadcast([P, T // 2, 2]), ALU.mult)
                    dve.tensor_tensor(t2buf[:, h, :].unsqueeze(2), f2[:, :, 0:1], f2[:, :, 1:2], ALU.mult).then_inc(updated, 1)
                elif kind == "level":
                    _, m, h = step
                    n = LEVEL_ORDER[step]
                    bank, _ = level_bank(step)
                    dve.wait_ge(step_mm, n + 1)
                    j = P // (2 * m)
                    o = MASK_BASE + 64 * LEVELS.index(m)
                    dst = pbuf[:, h, :].rearrange("p (c j two m) -> p c j two m", c=NCHUNK, two=2, m=m)[:, :, :, 1, :]
                    mk = msk[:, o:o + 64].rearrange("p (j m) -> p j m", m=m).unsqueeze(1).to_broadcast([P, NCHUNK, j, m])
                    dve.copy_predicated(dst, mk, ps[:, bank, :].rearrange("p (c j m) -> p c j m", c=NCHUNK, m=m)).then_inc(merged, 1)
                    tm = block_products(h, m).rearrange("p (b two) -> p b two", two=2)
                    qo, ke = pairs(qbuf[:, h, :], m)[:, :, 1, :], pairs(kbuf[:, h, :], m)[:, :, 0, :]
                    nb = T // (2 * m)
                    dve.wait_ge(updated, n - 3)
                    dve.tensor_tensor(qo, qo, tm[:, :, 0:1].to_broadcast([P, nb, m]), ALU.mult)
                    dve.tensor_tensor(ke, ke, tm[:, :, 1:2].to_broadcast([P, nb, m]), ALU.mult)
                    dve.tensor_tensor(block_products(h, 2 * m).unsqueeze(2), tm[:, :, 0:1], tm[:, :, 1:2], ALU.mult).then_inc(updated, 1)
            def fix_rows():
                dve.wait_ge(ld_fix, 32)
                r, b_, a_, g_ = (modfix[0:8, n, :] for n in range(4))
                link(dve.tensor_tensor(r, r, b_, ALU.add))
                link(dve.tensor_tensor(r, r, a_, ALU.add))
                dve.tensor_tensor(r, r, g_, ALU.mult).then_inc(fix_ready, 1)

            fix_rows()

            def state_chain(h):
                dve.wait_ge(ds_mm, h + 1)
                if h >= 2:
                    dve.wait_ge(o_mm, h - 1)
                if h == 0:
                    dve.wait_ge(updated, len(LEVEL_ORDER))
                st = states[:, h % 2, :].rearrange("p (c v) -> p c v", v=P)
                ds = ps[:, 2:4, :].rearrange("p a b -> p (a b)").rearrange("p (c v) -> p c v", v=P)
                ins = dve.tensor_copy(st[:, 1, :], ds[:, 0, :])
                for c in range(1, NCHUNK - 1):
                    link(ins)
                    ins = dve.scalar_tensor_tensor(st[:, c + 1, :], st[:, c, :], ptot[:, h, c:c + 1], ds[:, c, :], ALU.mult, ALU.add)
                ins.then_inc(st_ready, 1)

            def head_norm(h):
                dve.wait_ge(orr_ready, h + 1)
                r = orr[:, h % 2, :]
                link(dve.reciprocal(r, r))
                link(dve.scalar_tensor_tensor(r, ps[:, 4:6, :].rearrange("p a b -> p (a b)"), PR("hg", h), r, ALU.mult, ALU.mult))
                dve.tensor_tensor(gzbuf[:, h, :], gzbuf[:, h, :], r, ALU.mult).then_inc(oa_ready, 1)

            state_chain(0)
            for h in range(HEADS):
                if h + 1 < HEADS:
                    state_chain(h + 1)
                head_norm(h)
            dve.wait_ge(ld_mod, 16)
            gate1, shift2, scale2 = modbc[:, 0, :], modbc[:, 1, :], modbc[:, 2, :]
            for i in range(NT):
                dve.wait_ge(ss_ready, i + 1)
                link(dve.reciprocal(rst[:, 0, i:i + 1], ssq[:, 0, i:i + 1]))
                mix = ps[:, 2 * (i % 2):2 * (i % 2) + 2, :].rearrange("p a b -> p (a b)")
                link(dve.scalar_tensor_tensor(x1[:, i, :], mix, rst[:, 0, i:i + 1], gate1, ALU.mult, ALU.mult))
                dve.wait_ge(ld_xt[i % 2], 16 * (i // 2 + 1))
                dve.tensor_tensor(x1[:, i, :], x1[:, i, :], xtile[:, i % 2, :], ALU.add).then_inc(x1_ready, 1)
                dve.wait_ge(sd_ready, i + 1)
                link(dve.reciprocal(rst[:, 1, i:i + 1], ssq[:, 1, i:i + 1]))
                if i >= 2:
                    dve.wait_ge(h2_sent, 16 * (i - 1))
                    dve.wait_ge(h2t_mm, i - 1)
                link(dve.scalar_tensor_tensor(h2[:, i % 2, :], x1[:, i, :], rst[:, 1, i:i + 1], scale2, ALU.mult, ALU.mult))
                dve.tensor_tensor(h2[:, i % 2, :], h2[:, i % 2, :], shift2, ALU.add).then_inc(h2_ready, 1)

            rt = [64 * KB]

            def tmp(*shape):
                n = int(np.prod(shape))
                a = arena[:, rt[0]:rt[0] + n]
                rt[0] += n
                assert rt[0] <= 76 * KB
                if len(shape) == 2:
                    a = a.rearrange("p (a b) -> p a b", a=shape[0])
                elif len(shape) == 3:
                    a = a.rearrange("p (a b c) -> p a b c", a=shape[0], b=shape[1])
                return a

            lg = tmp(NT, 36)
            dve.wait_ge(logit_mm, NT)
            o = PARAM["rbias"][0]
            link(dve.tensor_tensor(lg, ps[:, 6, 0:NT * 36].rearrange("p (t e) -> p t e", t=NT),
                                   par[:, o:o + 36].unsqueeze(1).to_broadcast([P, NT, 36]), ALU.add))
            lgg = lg[:, :, 0:NG]
            lge = lg[:, :, NG:].rearrange("p t (g e) -> p t g e", g=NG)
            gmax, emax = tmp(NT, 1), tmp(NT, NG, 1)
            dve.tensor_reduce(gmax, lgg, AX.X, ALU.max)
            link(dve.tensor_reduce(emax, lge, AX.X, ALU.max))
            dve.tensor_tensor(lgg, lgg, gmax.to_broadcast([P, NT, NG]), ALU.subtract)
            dve.tensor_tensor(lge, lge, emax.to_broadcast([P, NT, NG, EPG]), ALU.subtract).then_inc(lg_ready, 1)
            dve.wait_ge(ex_ready, 1)

            def top(vals, n, rev):
                m, w, wm, oh = tmp(NT, 1), tmp(NT, n), tmp(NT, 1), tmp(NT, n)
                link(dve.tensor_reduce(m, vals, AX.X, ALU.max))
                link(dve.tensor_tensor(w, vals, m.to_broadcast([P, NT, n]), ALU.is_equal))
                link(dve.tensor_tensor(w, w, C(rev).unsqueeze(1).to_broadcast([P, NT, n]), ALU.mult))
                link(dve.tensor_reduce(wm, w, AX.X, ALU.max))
                link(dve.tensor_tensor(oh, w, wm.to_broadcast([P, NT, n]), ALU.is_equal))
                return m, oh

            gsum = tmp(NT, 1)
            link(dve.tensor_reduce(gsum, lgg, AX.X, ALU.add))
            link(dve.reciprocal(gsum, gsum))
            gm, ohg = top(lgg, NG, "rev4")
            gate = tmp(NT, 1)
            link(dve.tensor_tensor(gate, gm, gsum, ALU.mult))
            picked = tmp(NT, EPG, NG)
            se = tmp(NT, EPG)
            link(dve.tensor_tensor(picked, lge.rearrange("p t g e -> p t e g"), ohg.unsqueeze(2).to_broadcast([P, NT, EPG, NG]), ALU.mult))
            link(dve.tensor_reduce(se.unsqueeze(3), picked, AX.X, ALU.add))
            esum = tmp(NT, 1)
            link(dve.tensor_reduce(esum, se, AX.X, ALU.add))
            link(dve.reciprocal(esum, esum))
            m1, oh1 = top(se, EPG, "rev8")
            se2 = tmp(NT, EPG)
            link(dve.scalar_tensor_tensor(se2, oh1, -2.0, se, ALU.mult, ALU.add))
            m2, oh2 = top(se2, EPG, "rev8")
            p1, p2, den = tmp(NT, 1), tmp(NT, 1), tmp(NT, 1)
            dve.tensor_tensor(p1, m1, esum, ALU.mult)
            link(dve.tensor_tensor(p2, m2, esum, ALU.mult))
            link(dve.tensor_tensor(den, p1, p2, ALU.add))
            link(dve.reciprocal(den, den))
            link(dve.tensor_tensor(den, den, gate, ALU.mult))
            dve.tensor_tensor(wtok[:, 0, :].unsqueeze(2), p1, den, ALU.mult)
            dve.tensor_tensor(wtok[:, 1, :].unsqueeze(2), p2, den, ALU.mult)
            m_j = [tmp(NT, NE) for _ in range(2)]
            for j, oh in enumerate((oh1, oh2)):
                link(dve.tensor_tensor(m_j[j].rearrange("p t (g e) -> p t g e", g=NG), ohg.unsqueeze(3).to_broadcast([P, NT, NG, EPG]),
                                       oh.unsqueeze(2).to_broadcast([P, NT, NG, EPG]), ALU.mult))
            dve.memset(m_pre[:, 0, :], 0.0)
            link(dve.tensor_tensor(m_all, m_j[0], m_j[1], ALU.add))
            for i in range(NT):
                ins = dve.tensor_tensor(m_pre[:, i + 1, :], m_pre[:, i, :], m_all[:, i, :], ALU.add)
                if i < NT - 1:
                    link(ins)
            ins.then_inc(mm_ready, 1)
            dve.wait_ge(rank_mm, 1)
            rank, cnt = ps[:, 0, 0:NT * NE].rearrange("p (t e) -> p t e", t=NT), ps[:, 1, 0:NE]
            n_i, n_f, end, beg = tmp(NE).bitcast(I32), tmp(NE), tmp(NE), tmp(NE)
            link(dve.tensor_scalar(n_f, cnt, 1.0, -1.0, ALU.max, ALU.add))
            link(dve.tensor_copy(n_i, n_f))
            link(dve.tensor_scalar(n_i, n_i, 7, None, ALU.logical_shift_right))
            link(dve.tensor_copy(n_f, n_i))
            link(dve.tensor_tensor_scan(end, C("ones")[:, 0:NE], n_f, 0.0, ALU.mult, ALU.add))
            link(dve.tensor_tensor(beg, end, n_f, ALU.subtract))
            rj, ej, oj = tmp(2, NT, 1), tmp(2, NT, 1), tmp(2, NT, 1)
            prod = tmp(NT, NE)
            for j in range(2):
                for dst, src in ((rj, rank), (ej, C("iota32").unsqueeze(1).to_broadcast([P, NT, NE])),
                                 (oj, beg.unsqueeze(1).to_broadcast([P, NT, NE]))):
                    link(dve.tensor_tensor(prod, m_j[j], src, ALU.mult))
                    link(dve.tensor_reduce(dst[:, j], prod, AX.X, ALU.add))
            r_i, b_i, s_i = (tmp(16).bitcast(I32) for _ in range(3))
            b_f, s_f, is_o, blk = (tmp(16) for _ in range(4))
            rj, ej, oj = (a.rearrange("p j t o -> p (j t o)") for a in (rj, ej, oj))
            link(dve.tensor_copy(r_i, rj))
            dve.tensor_scalar(b_i, r_i, 7, None, ALU.logical_shift_right)
            link(dve.tensor_scalar(s_i, r_i, 127, None, ALU.bitwise_and))
            dve.tensor_copy(s_f, s_i)
            link(dve.tensor_copy(b_f, b_i))
            link(dve.tensor_scalar(is_o, b_f, 1.0, None, ALU.min))
            link(dve.tensor_tensor(blk, oj, b_f, ALU.add))
            link(dve.scalar_tensor_tensor(blk, blk, float(NE - 1), ej, ALU.add, ALU.subtract))
            link(dve.tensor_tensor(blk, blk, is_o, ALU.mult))
            link(dve.tensor_tensor(blk, blk, ej, ALU.add))
            yi = yidx.rearrange("p j t -> p (j t)")
            link(dve.scalar_tensor_tensor(b_f, blk, float(P), s_f, ALU.mult, ALU.add))
            dve.tensor_copy(yi, b_f)
            for n in range(16):
                if n >= 2:
                    dve.wait_ge(tab_mm, n - 1)
                dve.tensor_scalar(a_oh[:, n % 2, :], C("iota128"), s_f[:, n:n + 1], None, ALU.is_equal)
                o = CONST["tok"][0] + n % NT
                dve.tensor_scalar(b_oh[:, n % 2, :], C("iota47"), blk[:, n:n + 1], con[:, o:o + 1], ALU.is_equal, ALU.mult).then_inc(ab_ready, 1)
            cmp = tmp(N_OVER, NE)
            ov = tmp(16)
            link(dve.tensor_tensor(cmp, end.unsqueeze(1).to_broadcast([P, N_OVER, NE]), C("iota15").unsqueeze(2).to_broadcast([P, N_OVER, NE]), ALU.is_le))
            link(dve.tensor_reduce(ov[:, 0:N_OVER].unsqueeze(2), cmp, AX.X, ALU.add))
            link(dve.tensor_scalar(ov[:, 0:N_OVER], ov[:, 0:N_OVER], float(NE - 1), None, ALU.min))
            link(dve.tensor_copy(ov[:, 15:16], end[:, NE - 1:NE]))
            link(dve.tensor_copy(over, ov))
            dve.wait_ge(tab_mm, 16)
            dve.tensor_copy(tbl, ps[:, 2, 0:N_BLOCKS]).then_inc(route_ready, 1)

            def g_out(b):
                dve.wait_ge(sil_ready, b + 1)
                dve.wait_ge(h3_mm, b + 1)
                dve.tensor_tensor(gbuf, sil, ps[:, 1, :], ALU.mult).then_inc(g_ready, 1)

            def gt_out(b):
                dve.wait_ge(g_tr, b + 1)
                dve.tensor_copy(gT, ps[:, 2, :]).then_inc(gt_ready, 1)

            def y_half(b, q):
                dve.wait_ge(y_mm, b + 1)
                dve.tensor_copy(y_sb[:, q, HALF:D], ps[:, 4, :]).then_inc(y_dve, 1)

            g_out(0)
            for b in (1, 2):
                if b == 2:
                    dve.wait_ge(y_mm, 1)
                gt_out(b - 1)
                g_out(b)
                y_half(b - 1, (b - 1) % 2)
            with dve.Fori(0, (NE - 4) // 2) as i:
                for q in range(2):
                    b = 2 * i + (3 + q)
                    dve.wait_ge(y_mm, b - 1)
                    gt_out(b - 1)
                    g_out(b)
                    dve.wait_ge(y_sent[q], 16 * (i + 1))
                    y_half(b - 1, q)
            b = NE - 1
            dve.wait_ge(y_mm, b - 1)
            gt_out(b - 1)
            g_out(b)
            dve.wait_ge(y_sent[0], 16 * (NE // 2 - 1))
            y_half(b - 1, 0)
            dve.wait_ge(y_mm, b)
            gt_out(b)
            dve.wait_ge(y_sent[1], 16 * (NE // 2 - 1))
            y_half(b, 1)
            n_over = dve.value_load(over[0:1, 15:16], min_val=0, max_val=N_OVER)
            with dve.Fori(0, N_OVER) as o:
                with dve.If(o < n_over):
                    dve.wait_ge(ov_sil, o + 1)
                    dve.tensor_tensor(gbuf, sil, ps[:, 1, :], ALU.mult).then_inc(ov_g, 1)
                    dve.wait_ge(ov_gtr, o + 1)
                    dve.tensor_copy(gT, ps[:, 2, :]).then_inc(ov_gt, 1)
                    stand(dve, ov_sent, 16 * (o + 1))
            for i in range(NT):
                dve.wait_ge(fin_a, i + 1)
                dve.wait_ge(ld_y[i % 2], 32 * (i // 2 + 1))
                r2 = x_ring[:, 1, :] if i % 2 == 0 else xT_e[:, 1, :]
                y = y_sb[:, i % 2, :]
                dve.scalar_tensor_tensor(y, r2, wtok[:, 1, i:i + 1], y, ALU.mult, ALU.add).then_inc(fin_b, 1)
                dve.wait_ge(fin_s, i + 1)
                link(dve.reciprocal(rst[:, 2, i:i + 1], ssq[:, 2, i:i + 1]))
                if i >= 2:
                    dve.wait_ge(o_sent[i % 2], 16 * (i // 2))
                dve.scalar_tensor_tensor(xtile[:, i % 2, :], y, rst[:, 2, i:i + 1], modbc[:, 3, :], ALU.mult, ALU.mult).then_inc(fin_g, 1)
                dve.wait_ge(fin_g, i + 1)
                dve.tensor_tensor(xtile[:, i % 2, :], xtile[:, i % 2, :], x1[:, i, :], ALU.add).then_inc(fin_o, 1)

        @block.tensor
        def _(pe):
            mm = nc.tensor.matmul
            pe.wait_ge(ld_con, 16)
            for k in range(KD):
                pe.wait_ge(sq_ready, k + 1)
                for half in range(2):
                    ins = mm(ps[:, half, :], ones, sq[:, k % 2, half * HALF:(half + 1) * HALF], start=k == 0, stop=k == KD - 1)
                ins.then_inc(sq_summed, 1)
            for n in range(4):
                pe.wait_ge(acc_ready, n + 1)
                for j in range(4):
                    ins = mm(ps[:, 2, 4 * n + j:4 * n + j + 1], acc_early[:, n % 2, j * P:(j + 1) * P], ones[:, 0:1], start=True, stop=True)
                ins.then_inc(modc_ready, 1)
            seen = set()
            for step in STEPS:
                kind = step[0]
                if kind == "proj":
                    _, name, a, half = step
                    g = GROUPS[step[1:]]
                    if g < 3:
                        pe.wait_ge(rms_ready, 1)
                        pe.wait_ge(a1_ready, 1)
                    else:
                        pe.wait_ge(evac_done, g - 2)
                    if name not in seen:
                        seen.add(name)
                        n = PIECES.index(name)
                        pe.wait_ge(ld_ring[n % 2], 16 * (n // 2 + 1))
                    w = ring[PIECES.index(name) % 2]
                    for k in range(KD):
                        if g == 0:
                            pe.wait_ge(h_ready, k + 1)
                        if name == "iv":
                            lhs, rhs = hT[:, k, a * P:(a + 1) * P], w[:, k, :]
                        else:
                            lhs, rhs = w[:, k, a * P:(a + 1) * P], hT[:, k, half * HALF:(half + 1) * HALF]
                        ins = mm(ps[:, g % 3, :], lhs, rhs, start=k == 0, stop=k == KD - 1)
                    ins.then_inc(proj_done, 1)
                elif kind == "gate":
                    ct = step[1]
                    pe.wait_ge(conv_done, ct + 1)
                    pe.wait_ge(ld_bd, 64)
                    if ct:
                        pe.wait_ge(gates_ready, 4 * ct)
                    for g in range(2):
                        for half in range(2):
                            ins = mm(ps[:, 4 + 2 * g + half, :], bd[:, g, ct, :], xc[:, half * HALF:(half + 1) * HALF], start=True, stop=True)
                    ins.then_inc(gate_mm, 1)
                elif kind == "rg_norm":
                    pe.wait_ge(gates_ready, 4 * CT)
                    for ct in range(CT):
                        pe.wait_ge(rgsq_ready, ct + 1)
                        for half in range(2):
                            ins = mm(ps[:, 4 + half, :], ones, (xc, rgate)[ct % 2][:, half * HALF:(half + 1) * HALF], start=ct == 0, stop=ct == CT - 1)
                        ins.then_inc(rgsq_summed, 1)
                elif kind == "row":
                    u = step[1]
                    pe.wait_ge(acc_ready, 4 + u + 1)
                    if u:
                        pe.wait_ge(row_ready, u)
                    mm(ps[0:1, 3, (u % 2) * 256:(u % 2) * 256 + 256], ones[:, 0:1], acc[:, u % 2, :], start=True, stop=True).then_inc(row_mm, 1)
                elif kind in ("base", "level"):
                    n = LEVEL_ORDER[step]
                    bank, free = level_bank(step)
                    h = step[-1]
                    if n == 0:
                        pe.wait_ge(rgrms_ready, 1)
                    if free:
                        pe.wait_ge(merged, free)
                    if kind == "base":
                        pe.wait_ge(prep_done, h + 1)
                        out_ = ps[:, bank:bank + 2, :].rearrange("p a b -> p (a b)")
                        for c in range(NCHUNK):
                            ins = mm(out_[:, c * P:(c + 1) * P], kbuf[:, h, c * P:(c + 1) * P], qbuf[:, h, c * P:(c + 1) * P], start=True, stop=True)
                    else:
                        m = step[1]
                        pe.wait_ge(updated, n - 3)
                        qo = qbuf[:, h, :].rearrange("p (c j two m) -> p c j two m", c=NCHUNK, two=2, m=m)
                        for c in range(NCHUNK):
                            ins = mm(ps[:, bank, c * 64:(c + 1) * 64].rearrange("p (j m) -> p j m", m=m),
                                     kbuf[:, h, c * P:(c + 1) * P], qo[:, c, :, 1, :], start=True, stop=True)
                    ins.then_inc(step_mm, 1)

            def k_transposes(h):
                if h == 0:
                    pe.wait_ge(updated, len(LEVEL_ORDER))
                    pe.wait_ge(evac_done, len(GROUPS))
                    pe.wait_ge(row_ready, 16)
                    pe.wait_ge(merged, len(LEVEL_ORDER))
                else:
                    pe.wait_ge(kt_ready, h)
                o_ = ps[:, 0:2, :].rearrange("p a b -> p (a b)")
                for c in range(NCHUNK):
                    ins = nc.tensor.transpose(o_[:, c * P:(c + 1) * P], kbuf[:, h, c * P:(c + 1) * P], ident)
                ins.then_inc(kt_mm, 1)

            def state_sums(h):
                pe.wait_ge(kt_ready, h + 1)
                if h:
                    pe.wait_ge(st_ready, h)
                o_ = ps[:, 2:4, :].rearrange("p a b -> p (a b)")
                for c in range(NCHUNK - 1):
                    ins = mm(o_[:, c * P:(c + 1) * P], k_nat[:, h % 2, c * P:(c + 1) * P], vbuf[:, c, h * P:(h + 1) * P], start=True, stop=True)
                ins.then_inc(ds_mm, 1)

            def outputs(h):
                pe.wait_ge(st_ready, h + 1)
                if h:
                    pe.wait_ge(oa_ready, h)
                o_ = ps[:, 4:6, :].rearrange("p a b -> p (a b)")
                for c in range(NCHUNK):
                    dst = o_[:, c * P:(c + 1) * P]
                    ins = mm(dst, vbuf[:, c, h * P:(h + 1) * P], pbuf[:, h, c * P:(c + 1) * P], start=True, stop=c == 0)
                    if c:
                        ins = mm(dst, states[:, h % 2, c * P:(c + 1) * P], qbuf[:, h, c * P:(c + 1) * P], start=False, stop=True)
                ins.then_inc(o_mm, 1)

            def output_sums(h):
                pe.wait_ge(osq_ready, h + 1)
                for half in range(2):
                    ins = mm(ps[:, 6 + half, :], ones, osq[:, h % 2, half * HALF:(half + 1) * HALF], start=True, stop=True)
                ins.then_inc(os_mm, 1)

            k_transposes(0)
            state_sums(0)
            for h in range(HEADS):
                if h + 1 < HEADS:
                    k_transposes(h + 1)
                    state_sums(h + 1)
                outputs(h)
                output_sums(h)

            def mix(i):
                if i >= 2:
                    pe.wait_ge(x1_ready, i - 1)
                for half in range(2):
                    for k in range(KD):
                        if i == 0 and k >= 4:
                            pe.wait_ge(oa_ready, k - 3)
                        src = rgbuf[:, k, :] if k < 4 else gzbuf[:, k - 4, :]
                        ins = mm(ps[:, 2 * (i % 2) + half, :], src[:, i * P:(i + 1) * P], ring[half][:, (k + 4) % 8, :],
                                 start=k == 0, stop=k == KD - 1)
                ins.then_inc(mix_mm, 1)

            def logits(i):
                pe.wait_ge(h2_ready, i + 1)
                if i:
                    pe.wait_ge(h2t_ready, i)
                else:
                    pe.wait_ge(oa_ready, HEADS)
                o_ = ps[:, 4:6, :].rearrange("p a b -> p (a b)")
                for k in range(KD):
                    ins = nc.tensor.transpose(o_[:, k * P:(k + 1) * P], h2[:, i % 2, k * P:(k + 1) * P], ident)
                ins.then_inc(h2t_mm, 1)
                pe.wait_ge(h2t_ready, i + 1)
                for k in range(KD):
                    ins = mm(ps[:, 6, 36 * i:36 * i + 36], h2T[:, i % 2, k * P:(k + 1) * P], wrt[:, k, :], start=k == 0, stop=k == KD - 1)
                ins.then_inc(logit_mm, 1)

            for n in range(2):
                pe.wait_ge(ld_ring[n], 16 * 4)
            pe.wait_ge(ob_ready, CT)
            pe.wait_ge(ld_wrt, 16)
            mix(0)
            mix(1)
            for i in range(NT):
                logits(i)
                if i + 2 < NT:
                    mix(i + 2)
            pe.wait_ge(mm_ready, 1)
            flat = lambda a: a.rearrange("p t e -> p (t e)")
            mm(ps[:, 0, 0:NT * NE], C("upper"), flat(m_all), start=True, stop=False)
            mm(ps[:, 0, 0:NT * NE], ones, flat(m_pre[:, 0:NT, :]), start=False, stop=True)
            mm(ps[:, 1, 0:NE], ones, m_pre[:, NT, :], start=True, stop=True).then_inc(rank_mm, 1)
            for n in range(16):
                pe.wait_ge(ab_ready, n + 1)
                mm(ps[:, 2, 0:N_BLOCKS], a_oh[:, n % 2, :], b_oh[:, n % 2, :], start=n == 0, stop=n == 15).then_inc(tab_mm, 1)

            def x_transposes(b, q, loaded, wait_prev=True):
                pe.wait_ge(ld_g[q], loaded)
                if wait_prev:
                    pe.wait_ge(xt_ready, b)
                o_ = ps[:, 6:8, :].rearrange("p a b -> p (a b)")
                for k in range(KD):
                    ins = nc.tensor.transpose(o_[:, k * P:(k + 1) * P], x_ring[:, q, k * P:(k + 1) * P], ident)
                ins.then_inc(xg_tr, 1)

            def hidden(bank, w, q, s):
                for k in range(KD):
                    ins = mm(ps[:, bank, :], xT_e[:, q, k * P:(k + 1) * P], w[:, k, :], start=k == 0, stop=k == KD - 1)
                ins.then_inc(s, 1)

            def g_transposes(b):
                pe.wait_ge(g_ready, b + 1)
                for k in range(KF):
                    ins = nc.tensor.transpose(ps[:, 2, k * P:(k + 1) * P], gbuf[:, k * P:(k + 1) * P], ident)
                ins.then_inc(g_tr, 1)

            def down(w, s):
                for half in range(2):
                    for k in range(KF):
                        ins = mm(ps[:, 3 + half, :], gT[:, k * P:(k + 1) * P], w[:, k, half * HALF:(half + 1) * HALF], start=k == 0, stop=k == KF - 1)
                ins.then_inc(s, 1)

            pe.wait_ge(route_ready, 1)
            x_transposes(0, 0, 16, wait_prev=False)
            pe.wait_ge(xt_ready, 1)
            pe.wait_ge(ld_m[0], 16)
            hidden(0, m_slots[0], 0, h1_mm)
            pe.wait_ge(ld_m[1], 16)
            hidden(1, m_slots[1], 0, h3_mm)
            x_transposes(1, 1, 16)

            def block_step(b, q, n1, n3, n2, n_g, last=False):
                s1, s3, s2 = (2, 3, 4) if q == 1 else (5, 0, 1)
                pe.wait_ge(xt_ready, b + 1)
                pe.wait_ge(sil_ready, b)
                pe.wait_ge(ld_m[s1], n1)
                hidden(0, m_slots[s1], q, h1_mm)
                g_transposes(b - 1)
                pe.wait_ge(g_ready, b)
                pe.wait_ge(ld_m[s3], n3)
                hidden(1, m_slots[s3], q, h3_mm)
                if not last:
                    x_transposes(b + 1, 1 - q, n_g)
                pe.wait_ge(gt_ready, b)
                pe.wait_ge(ld_m[s2], n2)

            block_step(1, 1, 16, 16, 16, 32)
            down(m_slots2[4], y_mm)
            block_step(2, 0, 16, 32, 32, 32)
            pe.wait_ge(y_act, 1)
            pe.wait_ge(y_dve, 1)
            down(m_slots2[1], y_mm)
            with pe.Fori(0, (NE - 4) // 2) as i:
                for odd in range(2):
                    b = 2 * i + (3 + odd)
                    q = 1 - odd
                    if odd == 0:
                        n1 = n3 = n2 = 16 * i + 32
                        n_g = 16 * i + 48
                    else:
                        n1, n3, n2, n_g = 16 * i + 32, 16 * i + 48, 16 * i + 48, 16 * i + 48
                    block_step(b, q, n1, n3, n2, n_g)
                    pe.wait_ge(y_act, b - 1)
                    pe.wait_ge(y_dve, b - 1)
                    down(m_slots2[4 if odd == 0 else 1], y_mm)
            b = NE - 1
            block_step(b, 1, 256, 256, 256, 0, last=True)
            pe.wait_ge(y_act, b - 1)
            pe.wait_ge(y_dve, b - 1)
            down(m_slots2[4], y_mm)
            g_transposes(b)
            pe.wait_ge(gt_ready, b + 1)
            pe.wait_ge(ld_m[5], 256)
            pe.wait_ge(y_act, b)
            pe.wait_ge(y_dve, b)
            down(m_slots2[5], y_mm)
            n_over = pe.value_load(over[0:1, 15:16], min_val=0, max_val=N_OVER)
            pe.wait_ge(y_act, NE)
            pe.wait_ge(y_dve, NE)
            with pe.Fori(0, N_OVER) as o:
                with pe.If(o < n_over):
                    pe.wait_ge(ov_x, 16 * (o + 1))
                    o_ = ps[:, 6:8, :].rearrange("p a b -> p (a b)")
                    for k in range(KD):
                        ins = nc.tensor.transpose(o_[:, k * P:(k + 1) * P], x_ring[:, 0, k * P:(k + 1) * P], ident)
                    ins.then_inc(ov_xtr, 1)
                    pe.wait_ge(ov_xt, o + 1)
                    pe.wait_ge(ld_ov, 48 * (o + 1))
                    for bank in range(2):
                        for k in range(KD):
                            ins = mm(ps[:, bank, :], xT_e[:, 0, k * P:(k + 1) * P], m_slots[bank][:, k, :], start=k == 0, stop=k == KD - 1)
                    ins.then_inc(ov_h, 1)
                    pe.wait_ge(ov_g, o + 1)
                    for k in range(KF):
                        ins = nc.tensor.transpose(ps[:, 2, k * P:(k + 1) * P], gbuf[:, k * P:(k + 1) * P], ident)
                    ins.then_inc(ov_gtr, 1)
                    pe.wait_ge(ov_gt, o + 1)
                    down(m_slots2[2], ov_y)
                    stand(pe, ov_sent, 16 * (o + 1))


def kernel(**inputs):
    import concourse.bacc as _bacc
    from concourse.bass_utils import run_bass_kernel_spmd as _run

    a = {k: np.asarray(v) for k, v in inputs.items()}
    col = lambda v: np.ascontiguousarray(v.reshape(-1, P).T)
    cols = {
        "c": col(a["c"][0]), "g_pre": col(a["g_pre_mix"][0]), "b_ada": col(a["b_ada"][0, :2 * D]),
        "gam0": col(a["hgrn_gamma"][0]), "gam1": col(a["hgrn_gamma"][1]), "hg": col(a["hgrn_norm_g"][0]),
        "cw0": col(a["conv_w"][0, 0]), "cw1": col(a["conv_w"][0, 1]), "cw2": col(a["conv_w"][0, 2]), "cw3": col(a["conv_w"][0, 3]),
        "cb": col(a["conv_b"][0]), "br": col(a["rg_b_r"][0]), "bi": col(a["rg_b_i"][0]), "lam": col(a["rg_lambda"][0]),
        "rgg": col(a["rg_norm_g"][0]),
        "rbias": np.broadcast_to(np.concatenate([a["b_router_group"][0], a["b_router_expert"][0]]), (P, 36)),
    }
    params = np.concatenate([cols[n] for n in PARAM], axis=1)
    i128 = np.arange(P)
    const = {
        "ident": np.eye(P), "ones": np.ones((P, P)), "upper": (i128[:, None] < i128[None, :]),
        "iota128": np.broadcast_to(i128, (P, P)), "iota47": np.broadcast_to(np.arange(N_BLOCKS), (P, N_BLOCKS)),
        "iota32": np.broadcast_to(np.arange(NE), (P, NE)), "iota15": np.broadcast_to(np.arange(N_OVER), (P, N_OVER)),
        "tok": i128[:, None] + P * np.arange(NT)[None, :], "rev4": np.broadcast_to(np.arange(4, 0, -1), (P, 4)),
        "rev8": np.broadcast_to(np.arange(8, 0, -1), (P, 8)),
    }
    consts = np.concatenate([np.asarray(const[n], np.float32) for n in CONST], axis=1)
    s, t = i128[:, None], i128[None, :]
    mask = [(s // 2 == t // 2) & (s <= t)]
    for m in LEVELS:
        u = np.arange(64)[None, :]
        mask.append((s // (2 * m) == u // m) & ((s // m) % 2 == 0))
    masks = np.concatenate(mask, axis=1).astype(np.int32)
    g = {0: a["g_post_mix"][0], 2: a["g_pre_ffn"][0], 3: a["g_post_ffn"][0]}
    gain = np.concatenate([g.get(i, np.ones(D, np.float32)) for i in range(4)]).reshape(8, HALF)
    addend = np.zeros((8, HALF), np.float32)
    addend[4:6] = 1.0
    mod_rows = np.stack([a["b_ada"][0, 2 * D:].reshape(8, HALF), addend, gain], axis=1)
    w_route = np.concatenate([a["w_router_group"][0], a["w_router_expert"][0]], axis=1).reshape(KD, P, 36).transpose(1, 0, 2)
    arrays = {
        "x": a["x"][0], "x_t": a["x"][0].T, "params": params, "consts": consts, "masks": masks, "w_ada": a["w_ada"][0],
        "mod_rows": mod_rows, "w_in": a["w_in"][0], "w_r": a["rg_w_r"][0], "w_i": a["rg_w_i"][0], "w_out": a["w_out"][0],
        "w_route": w_route, "w1": a["w1"][0], "w3": a["w3"][0], "w2": a["w2"][0],
    }
    arrays = {f"in_{k}": np.ascontiguousarray(v) for k, v in arrays.items()}
    nc = _bacc.Bacc("TRN2", target_bir_lowering=False, num_devices=1)
    args = [nc.dram_tensor(k, v.shape, mybir.dt.from_np(v.dtype), kind="ExternalInput").ap() for k, v in arrays.items()]
    out = nc.dram_tensor("out_0", (T, D), F32, kind="ExternalOutput").ap()
    build(nc, *args, out)
    r = _run(nc, [arrays], core_ids=[0])
    return r.results[0]["out_0"].reshape(1, T, D)
```

```python
import numpy as np
import concourse.bass as bass
from concourse import mybir

F32 = mybir.dt.float32
F32R = mybir.dt.float32r
I32 = mybir.dt.int32
ALU = mybir.AluOpType
ACT = mybir.ActivationFunctionType
AX = mybir.AxisListType

P = 128
D = 1024
T = 1024
KD = D // P
NT = T // P
HALF = 512
CH = 512
HEADS = 4
CT = CH // P
NG, EPG = 4, 8
NE = NG * EPG
FE = D // 2
KF = FE // P
NCHUNK = T // P
LEVELS = (2, 4, 8, 16, 32, 64)
N_OVER = (2 * T - NE) // P
N_BLOCKS = NE + N_OVER
EPS = 1e-6
UNUSED = 4096

PARAM = {}
_at = 0
for _name, _n in (("c", 8), ("g_pre", 8), ("b_ada", 16), ("gam0", 4), ("gam1", 4), ("hg", 4), ("cw0", 4), ("cw1", 4),
                  ("cw2", 4), ("cw3", 4), ("cb", 4), ("br", 4), ("bi", 4), ("lam", 4), ("rgg", 4), ("rbias", 36)):
    PARAM[_name] = (_at, _n)
    _at += _n
N_PARAM = _at
CONST = {}
_at = 0
for _name, _n in (("ident", P), ("ones", P), ("upper", P), ("iota128", P), ("iota47", N_BLOCKS), ("iota32", NE),
                  ("iota15", N_OVER), ("tok", 2 * NT), ("rev4", 4), ("rev8", 8)):
    CONST[_name] = (_at, _n)
    _at += _n
N_CONST = _at
MASK_BASE = P


def mixer_steps():
    steps = []
    ada = iter(range(16))

    def fill(name, ct, half):
        steps.append(("proj", name, ct, half))

    for ct in range(CT):
        fill("xr", ct, 0)
        fill("xr", ct, 1)
        if ct:
            steps.append(("gate", ct - 1))
            steps.append(("scan", ct - 1))
        steps.append(("conv", ct))
    fill("yr", 0, 0)
    fill("yr", 0, 1)
    steps.append(("gate", CT - 1))
    steps.append(("scan", CT - 1))
    steps.append(("gelu_mul", 0))
    pending = []

    def ada_step():
        u = next(ada, None)
        if pending:
            steps.append(("row", pending.pop(0)))
        if u is not None:
            steps.append(("ada", u))
            pending.append(u)

    for ct in range(1, CT):
        fill("yr", ct, 0)
        ada_step()
        fill("yr", ct, 1)
        steps.append(("gelu_mul", ct))
    for h in range(HEADS):
        fill("q", h, 0)
        ada_step()
        fill("q", h, 1)
        if h == 0:
            steps.append(("rg_norm",))
    for h in range(HEADS):
        fill("f", h, 0)
        ada_step()
        fill("f", h, 1)
        steps.append(("prep", h))
    level_steps = [("base", h) for h in range(HEADS)] + [("level", m, h) for m in LEVELS for h in range(HEADS)]
    fills = [("iv", i, 0) for i in range(NT)] + [("gz", h, half) for h in range(HEADS) for half in range(2)]
    n = 0
    for i, f in enumerate(fills):
        fill(*f)
        if i % 2 == 0 or pending:
            ada_step()
        for _ in range(2 if i % 4 != 3 else 1):
            if n < len(level_steps):
                steps.append(level_steps[n])
                n += 1
    while pending:
        ada_step()
    steps += level_steps[n:]
    return steps


STEPS = mixer_steps()
GROUPS = {s[1:]: n for n, s in enumerate([s for s in STEPS if s[0] == "proj"])}
LEVEL_ORDER = {s: n for n, s in enumerate([s for s in STEPS if s[0] in ("base", "level")])}
PIECES = ["xr", "yr", "q", "f", "iv", "gz"]
PIECE_COL = {"q": 0, "f": 512, "iv": 1024, "gz": 1536, "xr": 2048, "yr": 2560}


def build(nc, x, x_t, params, consts, masks, w_ada, mod_rows, w_in, w_r, w_i, w_out, w_route, w1, w3, w2, out):
    KB = 256
    ps = nc.alloc_psum_tensor("banks", [P, 8, HALF], F32)
    h2_rows = nc.dram_tensor("h2_rows", [T, D], F32).ap()
    y_rows = nc.dram_tensor("y_rows", [2 * T, D], F32).ap()
    mod_raw = nc.dram_tensor("mod_raw", [8, HALF], F32).ap()
    mod_done = nc.dram_tensor("mod_done", [8, HALF], F32).ap()

    arena = nc.alloc_sbuf_tensor("arena", [P, 207 * KB], F32)
    base = nc.sbuf_base - 207 * 1024

    def halves(name, kb, a, b):
        return nc.alloc_sbuf_tensor_at(name, [P, a, b], F32R, offset=base + int(kb * 1024))[:, :, :]

    drawn = {}

    def region(kb, cols, dtype=None):
        if (kb, cols) not in drawn:
            drawn[kb, cols] = nc.alloc_sbuf_tensor_at(f"buf_{len(drawn)}", [P, cols], F32, offset=base + int(kb * 1024))[:, :]
        a = drawn[kb, cols]
        return a if dtype is None else a.bitcast(dtype)

    def region3(kb, a, b):
        return region(kb, a * b).rearrange("p (a b) -> p a b", a=a)

    ring = [region3(kb, KD, HALF) for kb in (0, 16)]
    hT = region3(32, KD, T)
    fbuf = region3(64, HEADS, T)
    qbuf = region3(80, HEADS, T)
    kbuf = region3(96, HEADS, T)
    pbuf = region3(112, HEADS, T)
    vbuf = region3(128, NCHUNK, CH)
    gzbuf = region3(144, HEADS, T)
    rgbuf = region3(160, CT, T)
    t2buf = region3(176, HEADS, HALF)
    early = [region3(kb, KD, HALF) for kb in (64, 80, 128, 144)]
    sq = region3(96, 2, T)
    rbc = region(104, T)
    acc_early = region3(108, 2, HALF)
    gy = region3(128, CT, T)
    xc, rgate, igate, th = (region(112 + 4 * n, T) for n in range(4))
    early_row = th
    k_nat, states = region3(32, 2, T), region3(40, 2, T)
    diag = region3(176, 2, T)
    wo_hi, wo_lo = halves("wo_hi", 48, 2 * KD, HALF), halves("wo_lo", 0, 2 * KD, HALF)
    s_hi, s_lo = halves("s_hi", 40, 2, D), halves("s_lo", 88, 2, D)
    modbc = region(128, 4 * T).rearrange("p (a b) -> p a b", a=4)
    x1 = region(96, NT * T).rearrange("p (a b) -> p a b", a=NT)
    xtile = region3(176, 2, T)
    h2 = region3(32, 2, T)
    h2T = region3(80, 2, T)
    x_ring = region3(176, 2, D)
    w_hi, w_lo = halves("w_hi", 144, 4, D), halves("w_lo", 160, 4, D)
    x_hi, x_lo = halves("x_hi", 128, 2, D), halves("x_lo", 136, 2, D)
    y_pair = region(0, 2 * NT * D).rearrange("p (i j d) -> p i j d", i=NT, j=2)
    y_sum, o_tile = region3(160, 2, D), region3(168, 2, D)
    m_slots = [region3(kb, KD, HALF) for kb in (32, 48, 0, 16, 64, 80)]
    m_slots2 = [region3(kb, KF, D) for kb in (32, 48, 0, 16, 64, 80)]

    at = [0]
    smalls = region(184, 23 * KB)

    def small(cols, dtype=None):
        a = smalls[:, at[0]:at[0] + cols]
        at[0] += cols
        return a if dtype is None else a.bitcast(dtype)

    con = small(N_CONST)
    par = small(N_PARAM)
    msk_at = at[0]
    msk = small(MASK_BASE + 64 * len(LEVELS), I32)
    wrt = small(KD * 36).rearrange("p (a b) -> p a b", a=KD)
    bd_at = at[0]
    bd = small(2 * CT * P).rearrange("p (g c j) -> p g c j", g=2, c=CT)
    A1, SH1 = small(8), small(8)
    lb, omlb, cl = small(4), small(4), small(4)
    eps = small(1)
    cs = small(8)
    hrt = small(HEADS * 8).rearrange("p (a b) -> p a b", a=HEADS)
    tiny = small(4 * 12).rearrange("p (a b) -> p a b", a=12)
    ptot = small(HEADS * 8).rearrange("p (a b) -> p a b", a=HEADS)
    ssq = small(3 * 8).rearrange("p (a b) -> p a b", a=3)
    rst = small(3 * 8).rearrange("p (a b) -> p a b", a=3)
    acc = small(2 * 256).rearrange("p (a b) -> p a b", a=2)
    ada_at = at[0]
    ada_half = small(KD * 256).rearrange("p (a b) -> p a b", a=KD)
    osq = ada_half.rearrange("p a b -> p (a b)").rearrange("p (a b) -> p a b", a=2)
    rowt = small(2 * 256).rearrange("p (a b) -> p a b", a=2)
    assert at[0] <= 23 * KB, at[0] / KB
    scratch = region(128, 4 * T)
    m_all = scratch[:, 3 * T:3 * T + NT * NE].rearrange("p (a b) -> p a b", a=NT)
    m_pre = scratch[:, 3 * T + NT * NE:3 * T + (2 * NT + 1) * NE].rearrange("p (a b) -> p a b", a=NT + 1)
    modfix = acc.rearrange("p a b -> p (a b)").rearrange("p (a b) -> p a b", a=4)
    junk = smalls[:, bd_at:bd_at + T]
    rat = [ada_at]

    def keep(cols, dtype=None):
        a = smalls[:, rat[0]:rat[0] + cols]
        rat[0] += cols
        assert rat[0] <= at[0]
        return a if dtype is None else a.bitcast(dtype)

    wtok = keep(16).rearrange("p (j t) -> p j t", j=2)
    tbl = keep(N_BLOCKS, I32)
    ttab = keep(N_BLOCKS, I32)
    gate2 = keep(D)
    over = keep(16, I32)
    xidx, sidx = keep(2, I32), keep(2, I32)
    a_oh = smalls[:, bd_at:bd_at + 8 * P].rearrange("p (a n b) -> p a n b", a=2, n=4)
    b_oh = smalls[:, msk_at:msk_at + 8 * N_BLOCKS].rearrange("p (a n b) -> p a n b", a=2, n=4)
    keep(-rat[0] % 8)
    g_hi, g_lo = (halves(n, 184 + o / KB, 1, FE)[:, 0, :] for n, o in (("g_hi", rat[0]), ("g_lo", rat[0] + FE)))
    keep(2 * FE)
    y_sb = smalls[:, bd_at:bd_at + D]
    sil = smalls[:, msk_at:msk_at + FE]

    def C(name, rows=P):
        o, n = CONST[name]
        return con[0:rows, o:o + n]

    def PR(name, i=None):
        o, n = PARAM[name]
        return par[:, o:o + n] if i is None else par[:, o + i:o + i + 1]

    ident, ones = C("ident"), C("ones")

    def sem(name):
        return nc.alloc_semaphore(name)

    ld_par, ld_con, ld_msk, ld_wrt, ld_bd, ld_fix, ld_mod = (sem(n) for n in
        ("ld_par", "ld_con", "ld_msk", "ld_wrt", "ld_bd", "ld_fix", "ld_mod"))
    ld_x = [sem(f"ld_x{i}") for i in range(2)]
    ld_early = [sem(f"ld_early{i}") for i in range(4)]
    ld_ring = [sem(f"ld_ring{i}") for i in range(2)]
    ld_ada = sem("ld_ada")
    ld_xt = [sem(f"ld_xtile{i}") for i in range(2)]
    ld_m = [sem(f"ld_expert{i}") for i in range(6)]
    ld_g = [sem(f"ld_gather{i}") for i in range(2)]
    (bd_zero, cs_ready, sq_ready, sq_summed, rms_ready, xs_ready, acc_ready, modc_ready, a1_ready, h_ready,
     proj_done, evac_done, conv_done, gate_mm, gates_ready, sqrt_in, sqrt_out, scan_done, gmul_done, rgsq_ready,
     rgsq_summed, rgrms_ready, ob_ready, row_mm, row_ready, row_sent, p_zero, prep_done, step_mm, merged, updated,
     kt_mm, kt_ready, ds_mm, st_ready, o_mm, osq_ready, os_mm, hsd_ready, osb_ready, gzo_ready, diag_ready, bc_mm, wohi_ready, wolo_ready, shi_ready, slo_ready, erow_mm, erow_ready, oa_ready, fix_ready, fix_sent,
     mix_mm, ss_ready, sd_ready, r1_ready, x1_ready, r2_ready, h2_ready, h2_sent, h2t_mm, h2t_ready, logit_mm,
     lg_ready, ex_ready, mm_ready, rank_mm, ab_ready, tab_mm, route_ready, dve_chain, act_chain, pool_chain,
     lbin_ready, lbexp_ready) = (sem(n) for n in
        ("bd_zero cs_ready sq_ready sq_summed rms_ready xs_ready acc_ready modc_ready a1_ready h_ready "
         "proj_done evac_done conv_done gate_mm gates_ready sqrt_in sqrt_out scan_done gmul_done rgsq_ready "
         "rgsq_summed rgrms_ready ob_ready row_mm row_ready row_sent p_zero prep_done step_mm merged updated "
         "kt_mm kt_ready ds_mm st_ready o_mm osq_ready os_mm hsd_ready osb_ready gzo_ready diag_ready bc_mm wohi_ready wolo_ready shi_ready slo_ready erow_mm erow_ready oa_ready fix_ready fix_sent "
         "mix_mm ss_ready sd_ready r1_ready x1_ready r2_ready h2_ready h2_sent h2t_mm h2t_ready logit_mm "
         "lg_ready ex_ready mm_ready rank_mm ab_ready tab_mm route_ready dve_chain act_chain pool_chain "
         "lbin_ready lbexp_ready").split())
    (xg_tr, xt_ready, sil_ready, g_ready, g_tr, ghi_ready, glo_ready, y_act, y_dve, hi_ready, lo_ready, w_used, xlo_ready, x_clear) = (sem(n) for n in
        "xg_tr xt_ready sil_ready g_ready g_tr ghi_ready glo_ready y_act y_dve hi_ready lo_ready w_used xlo_ready x_clear".split())
    y_sent = [sem(f"y_sent{i}") for i in range(2)]
    xidx_ready, sidx_ready = sem("xidx_ready"), sem("sidx_ready")
    (ld_ov, ov_x, ov_xtr, ov_hi, ov_lo, ov_used, ov_xhi, ov_xlo, ov_sil, ov_g, ov_gtr, ov_ghi, ov_glo,
     ov_ysb, ov_sent) = (sem(n) for n in
        "ld_ov ov_x ov_xtr ov_hi ov_lo ov_used ov_xhi ov_xlo ov_sil ov_g ov_gtr ov_ghi ov_glo ov_ysb ov_sent".split())
    ld_y = [sem(f"ld_y{i}") for i in range(NT)]
    fin_a, fin_b, fin_s, fin_sd, fin_r, fin_g, fin_o = (sem(n) for n in "fin_a fin_b fin_s fin_sd fin_r fin_g fin_o".split())
    o_sent = [sem(f"o_sent{i}") for i in range(2)]
    ada_v = w_ada.rearrange("(k p) c -> p k c", p=P)
    win_v = w_in.rearrange("(k p) c -> p k c", p=P)
    wout_v = w_out.rearrange("(k p) c -> p k c", p=P)
    xt_v = x_t.rearrange("(k p) t -> p k t", p=P)
    w1_v = w1.rearrange("e (k p) c -> e p k c", p=P)
    w3_v = w3.rearrange("e (k p) c -> e p k c", p=P)
    w2_v = w2.rearrange("e (k p) c -> e p k c", p=P)

    def chain_of(eng, s):
        count = [0]

        def link(ins):
            count[0] += 1
            ins.then_inc(s, 1)
            eng.wait_ge(s, count[0])
        return link

    passed = sem("passed")

    def stand(eng, s, value):
        eng.wait_ge(s, value)
        eng.sem_inc(passed, 1)

    def quarter(piece, r):
        return piece.rearrange("p a b -> p (a b)")[:, r * D:(r + 1) * D]

    def pairs(buf, m):
        return buf.rearrange("p (b two m) -> p b two m", two=2, m=m)

    def block_products(h, m):
        if m == 1:
            return fbuf[:, h, :]
        if m == 2:
            return t2buf[:, h, :]
        if m == P:
            return ptot[:, h, :]
        o = 512 - 1024 // m * 2
        return fbuf[:, h, o:o + T // m]

    def level_bank(s):
        n = LEVEL_ORDER[s]
        return 4 + 2 * (n % 2), max(n - 1, 0)

    block_cm = nc.Block()
    with block_cm as block:

        @block.sync
        def _(sp):
            sp.dma_start(par, params).then_inc(ld_par, 16)
            for i in range(2):
                sp.dma_start(hT[:, 4 * i:4 * i + 4, :], xt_v[:, 4 * i:4 * i + 4, :]).then_inc(ld_x[i], 16)
            sp.dma_start(con, consts).then_inc(ld_con, 16)
            for n in range(4):
                sp.dma_start(early[n], ada_v[:, :, n * HALF:(n + 1) * HALF]).then_inc(ld_early[n], 16)
            for n in range(2):
                c = PIECE_COL[PIECES[n]]
                sp.dma_start(ring[n], win_v[:, :, c:c + HALF]).then_inc(ld_ring[n], 16)
            sp.wait_ge(bd_zero, 1)
            for g, w in enumerate((w_r, w_i)):
                wv = w.rearrange("(c two) i j -> two i c j", two=2)
                for two in range(2):
                    sp.dma_start(bd[64 * two:64 * two + 64, g, :, 64 * two:64 * two + 64], wv[two]).then_inc(ld_bd, 16)
            sp.dma_start(msk, masks).then_inc(ld_msk, 16)
            sp.dma_start(wrt, w_route).then_inc(ld_wrt, 16)
            for n in range(2, 8):
                last = {0: ("xr", 3, 1), 1: ("yr", 3, 1), 2: ("q", 3, 1), 3: ("f", 3, 1), 4: ("iv", 7, 0), 5: ("gz", 3, 1)}[n - 2]
                sp.wait_ge(proj_done, GROUPS[last] + 1)
                if n < 6:
                    c = PIECE_COL[PIECES[n]]
                    src = win_v[:, :, c:c + HALF]
                else:
                    src = wout_v[:, :, (n - 6) * HALF:(n - 5) * HALF]
                sp.dma_start(ring[n % 2], src).then_inc(ld_ring[n % 2], 16)
            sp.wait_ge(row_sent, 16 * 16)
            sp.wait_ge(updated, len(LEVEL_ORDER))
            sp.dma_start(modfix[0:32, 0, :], mod_raw.rearrange("a (b c) -> (a b) c", c=P)).then_inc(ld_fix, 16)
            sp.dma_start(modfix[0:32, 1:4, :], mod_rows).then_inc(ld_fix, 16)
            sp.wait_ge(fix_ready, 1)
            sp.dma_start(mod_done.rearrange("a (b c) -> (a b) c", c=P), modfix[0:32, 0, :]).then_inc(fix_sent, 16)
            sp.wait_ge(fix_sent, 16)
            sp.wait_ge(o_mm, HEADS)
            sp.wait_ge(os_mm, HEADS)
            sp.dma_start(modbc, mod_done.rearrange("a b -> (a b)").partition_broadcast(P)
                         .rearrange("p (a b) -> p a b", a=4)).then_inc(ld_mod, 16)
            sp.dma_start(gate2, mod_done[6:8, :].rearrange("a b -> (a b)").partition_broadcast(P)).then_inc(ld_mod, 16)
            sp.wait_ge(bc_mm, HEADS)
            for i in range(NT):
                if i >= 2:
                    sp.wait_ge(x1_ready, i - 1)
                sp.dma_start(xtile[:, i % 2, :], x[i * P:(i + 1) * P, :]).then_inc(ld_xt[i % 2], 16)
            sp.wait_ge(mix_mm, NT)
            sp.dma_start(m_slots[1], w3_v[0]).then_inc(ld_m[1], 16)
            sp.dma_start(m_slots[2], w1_v[1]).then_inc(ld_m[2], 16)
            sp.wait_ge(h2_sent, 16 * NT)
            sp.wait_ge(h2t_mm, NT)
            sp.dma_start(m_slots[0], w1_v[0]).then_inc(ld_m[0], 16)
            sp.dma_start(m_slots2[4], w2_v[0]).then_inc(ld_m[4], 16)
            sp.dma_start(m_slots[3], w3_v[1]).then_inc(ld_m[3], 16)
            sp.wait_ge(logit_mm, NT)
            sp.dma_start(m_slots[5], w1_v[2]).then_inc(ld_m[5], 16)
            sp.wait_ge(lo_ready, 4)
            sp.dma_start(m_slots[0], w3_v[2]).then_inc(ld_m[0], 16)
            sp.wait_ge(lo_ready, 8)
            sp.dma_start(m_slots2[1], w2_v[1]).then_inc(ld_m[1], 16)
            with sp.Fori(0, (NE - 4) // 2) as i:
                for odd in range(2):
                    b = 2 * i + (3 + odd)
                    s1, s3, s2 = (2, 3, 4) if odd == 0 else (5, 0, 1)
                    q = 24 * i + 12 * (1 + odd)
                    sp.wait_ge(lo_ready, q)
                    sp.dma_start(m_slots[s1], w1_v[b]).then_inc(ld_m[s1], 16)
                    sp.wait_ge(lo_ready, q + 4)
                    sp.dma_start(m_slots[s3], w3_v[b]).then_inc(ld_m[s3], 16)
                    sp.wait_ge(lo_ready, q + 8)
                    sp.dma_start(m_slots2[s2], w2_v[b - 1]).then_inc(ld_m[s2], 16)
            b = NE - 1
            q = 12 * (b - 2)
            sp.wait_ge(lo_ready, q)
            sp.dma_start(m_slots[2], w1_v[b]).then_inc(ld_m[2], 16)
            sp.wait_ge(lo_ready, q + 4)
            sp.dma_start(m_slots[3], w3_v[b]).then_inc(ld_m[3], 16)
            sp.wait_ge(lo_ready, q + 8)
            sp.dma_start(m_slots2[4], w2_v[b - 1]).then_inc(ld_m[4], 16)
            sp.wait_ge(lo_ready, q + 12)
            sp.dma_start(m_slots2[5], w2_v[b]).then_inc(ld_m[5], 16)
            n_over = sp.value_load(over[0:1, 15:16], min_val=0, max_val=N_OVER)
            sp.wait_ge(lo_ready, 12 * NE)
            with sp.If(n_over > 0):
                with sp.Fori(0, N_OVER) as o:
                    with sp.If(o < n_over):
                        e = sp.value_load(over[0:1, bass.ds(o, 1)], min_val=0, max_val=NE - 1)
                        sp.dma_start(m_slots[0], w1_v[bass.ds(e, 1)].rearrange("a p k c -> (a p) k c")).then_inc(ld_ov, 16)
                        sp.dma_start(m_slots[1], w3_v[bass.ds(e, 1)].rearrange("a p k c -> (a p) k c")).then_inc(ld_ov, 16)
                        sp.dma_start(m_slots2[2], w2_v[bass.ds(e, 1)].rearrange("a p k c -> (a p) k c")).then_inc(ld_ov, 16)
                        stand(sp, ov_sent, 16 * (o + 1))
            for q in range(2):
                sp.wait_ge(y_sent[q], 8 * NE)
            for i in range(NT):
                sp.dma_start(y_pair[:, i, :, :], y_rows.rearrange("(j t) d -> t j d", j=2)[i * P:(i + 1) * P]).then_inc(ld_y[i], 16)
            for i in range(NT):
                sp.wait_ge(fin_o, i + 1)
                sp.dma_start(out[i * P:(i + 1) * P, :], o_tile[:, i % 2, :]).then_inc(o_sent[i % 2], 16)
            for i in range(2):
                sp.wait_ge(o_sent[i], 16 * NT // 2)

        @block.gpsimd
        def _(pool):
            link = chain_of(pool, pool_chain)
            link(pool.memset(eps, EPS))
            pool.memset(bd.rearrange("p g c j -> p (g c j)"), 0.0).then_inc(bd_zero, 1)
            for u in range(16):
                if u:
                    pool.wait_ge(acc_ready, 2 + u)
                c = 4 * HALF + u * 256
                pool.dma_start(ada_half, ada_v[:, :, c:c + 256]).then_inc(ld_ada, 16)
                if u == 3:
                    pool.wait_ge(ob_ready, CT)
                    pool.memset(pbuf.rearrange("p a b -> p (a b)"), 0.0).then_inc(p_zero, 1)
            for i in range(NT):
                pool.wait_ge(h2_ready, i + 1)
                pool.dma_start(h2_rows[i * P:(i + 1) * P, :], h2[:, i % 2, :]).then_inc(h2_sent, 16)
                pool.wait_ge(h2_sent, 16 * (i + 1))
            pool.wait_ge(x1_ready, NT)
            pool.memset(x_ring.rearrange("p a b -> p (a b)"), 0.0).then_inc(x_clear, 1)
            pool.wait_ge(x_clear, 1)
            pool.wait_ge(route_ready, 1)

            def gather(idx, dst, s):
                pool.indirect_dma_start(dst, None, h2_rows, bass.IndirectOffsetOnAxis(ap=idx, axis=0),
                                        bounds_check=T - 1, oob_is_err=False).then_inc(s, 16)

            def scatter(idx, s):
                pool.indirect_dma_start(y_rows, bass.IndirectOffsetOnAxis(ap=idx, axis=0), y_sb, None,
                                        bounds_check=2 * T - 1, oob_is_err=False).then_inc(s, 16)

            def gather_block(b, q, ring_used=True):
                if ring_used:
                    pool.wait_ge(xg_tr, b - 1)
                pool.tensor_copy(xidx[:, q:q + 1], ttab[:, bass.ds(b, 1)]).then_inc(xidx_ready, 1)
                stand(pool, xidx_ready, b + 1)
                gather(xidx[:, q:q + 1], x_ring[:, q, :], ld_g[q])

            def scatter_block(b, q):
                pool.wait_ge(y_act, b + 1)
                pool.wait_ge(y_dve, b + 1)
                pool.tensor_copy(sidx[:, q:q + 1], tbl[:, bass.ds(b, 1)]).then_inc(sidx_ready, 1)
                stand(pool, sidx_ready, b + 1)
                scatter(sidx[:, q:q + 1], y_sent[q])

            gather_block(0, 0, ring_used=False)
            gather_block(1, 1, ring_used=False)
            gather_block(2, 0)
            with pool.Fori(0, (NE - 4) // 2) as i:
                for odd in range(2):
                    gather_block(2 * i + (3 + odd), 1 - odd)
                    scatter_block(2 * i + odd, odd)
            gather_block(NE - 1, 1)
            for b in range(NE - 4, NE):
                scatter_block(b, b % 2)
            for q in range(2):
                pool.wait_ge(y_sent[q], 8 * NE)
            n_over = pool.value_load(over[0:1, 15:16], min_val=0, max_val=N_OVER)
            with pool.If(n_over > 0):
                with pool.Fori(0, N_OVER) as o:
                    with pool.If(o < n_over):
                        pool.tensor_copy(sidx[:, 0:1], tbl[:, bass.ds(o + NE, 1)])
                        pool.tensor_copy(xidx[:, 0:1], ttab[:, bass.ds(o + NE, 1)]).then_inc(xidx_ready, 1)
                        stand(pool, xidx_ready, o + (NE + 1))
                        gather(xidx[:, 0:1], x_ring[:, 0, :], ov_x)
                        stand(pool, ov_ysb, o + 1)
                        scatter(sidx[:, 0:1], ov_sent)
                        stand(pool, ov_sent, 16 * (o + 1))

        @block.scalar
        def _(act):
            link = chain_of(act, act_chain)
            act.wait_ge(ld_par, 16)
            act.activation(cs, PR("c"), ACT.Silu).then_inc(cs_ready, 1)
            for k in range(KD):
                act.wait_ge(ld_x[k // 4], 16)
                if k >= 2:
                    act.wait_ge(sq_summed, k - 1)
                act.activation(sq[:, k % 2, :], hT[:, k, :], ACT.Square).then_inc(sq_ready, 1)
            act.wait_ge(lbin_ready, 1)
            act.activation(tiny[:, 0:3, :], tiny[:, 0:3, :], ACT.Exp).then_inc(lbexp_ready, 1)
            act.wait_ge(pool_chain, 1)
            act.wait_ge(sq_summed, KD)
            act.activation(rbc, ps[:, 0:2, :].rearrange("p a b -> p (a b)"), ACT.Sqrt, bias=eps, scale=1.0 / D).then_inc(rms_ready, 1)
            for n in range(2):
                act.wait_ge(erow_mm, n + 1)
                act.activation(early_row[0:1, n * HALF:(n + 1) * HALF], ps[0:1, 3 + n, :], ACT.Copy).then_inc(erow_ready, 1)
            act.wait_ge(a1_ready, 1)
            for k in range(KD):
                act.wait_ge(xs_ready, k + 1)
                act.activation(hT[:, k, :], hT[:, k, :], ACT.Identity, bias=SH1[:, k:k + 1], scale=A1[:, k:k + 1]).then_inc(h_ready, 1)
            act.wait_ge(ld_bd, 64)
            n_row = 0
            for step in STEPS:
                kind = step[0]
                if kind == "proj":
                    _, name, a, half = step
                    g = GROUPS[step[1:]]
                    src = ps[:, g % 3, :]
                    cols = slice(half * HALF, (half + 1) * HALF)
                    act.wait_ge(proj_done, g + 1)
                    if name == "xr":
                        ins = act.activation(rgbuf[:, a, cols], src, ACT.Copy)
                    elif name == "yr":
                        act.wait_ge(a1_ready, 1)
                        ins = act.activation(gy[:, a, cols], src, ACT.Gelu_apprx_tanh)
                    elif name == "q":
                        ins = act.activation(qbuf[:, a, cols], src, ACT.Silu)
                    elif name == "f":
                        act.activation(fbuf[:, a, cols], src, ACT.Sigmoid)
                        ins = act.activation(kbuf[:, a, cols], src, ACT.Sigmoid, scale=-1.0)
                    elif name == "iv":
                        if a == 0:
                            act.wait_ge(ob_ready, CT)
                        ins = act.activation(vbuf[:, a, :], src, ACT.Copy)
                    else:
                        ins = act.activation(gzbuf[:, a, cols], src, ACT.Silu)
                    ins.then_inc(evac_done, 1)
                elif kind == "gate":
                    ct = step[1]
                    act.wait_ge(gate_mm, ct + 1)
                    if ct:
                        act.wait_ge(scan_done, ct)
                    act.activation(rgate, ps[:, 4:6, :].rearrange("p a b -> p (a b)"), ACT.Sigmoid, bias=PR("br", ct)).then_inc(gates_ready, 1)
                    act.activation(igate, ps[:, 6:8, :].rearrange("p a b -> p (a b)"), ACT.Sigmoid, bias=PR("bi", ct)).then_inc(gates_ready, 1)
                    act.wait_ge(gates_ready, 4 * ct + 1)
                    act.activation(th, rgate, ACT.Tanh, scale=cl[:, ct:ct + 1]).then_inc(gates_ready, 1)
                    act.wait_ge(gates_ready, 4 * ct + 3)
                    act.activation(rgate, rgate, ACT.Exp, scale=cl[:, ct:ct + 1]).then_inc(gates_ready, 1)
                elif kind == "scan":
                    ct = step[1]
                    act.wait_ge(sqrt_in, ct + 1)
                    act.activation(xc, xc, ACT.Sqrt, scale=-1.0).then_inc(sqrt_out, 1)
                elif kind == "rg_norm":
                    act.wait_ge(scan_done, CT)
                    for ct in range(CT):
                        act.wait_ge(gmul_done, ct + 1)
                        if ct >= 2:
                            act.wait_ge(rgsq_summed, ct - 1)
                        act.activation((xc, rgate)[ct % 2], rgbuf[:, ct, :], ACT.Square).then_inc(rgsq_ready, 1)
                    act.wait_ge(rgsq_summed, CT)
                    act.activation(igate, ps[:, 4:6, :].rearrange("p a b -> p (a b)"), ACT.Sqrt, bias=eps, scale=1.0 / CH).then_inc(rgrms_ready, 1)
                elif kind == "row":
                    u = step[1]
                    act.wait_ge(row_mm, u + 1)
                    if u >= 2:
                        act.wait_ge(row_sent, 16 * (u - 1))
                    act.activation(rowt[0:1, u % 2, :], ps[0:1, 3, (u % 2) * 256:(u % 2) * 256 + 256], ACT.Copy).then_inc(row_ready, 1)
                    act.wait_ge(row_ready, u + 1)
                    if u:
                        act.wait_ge(row_sent, 16 * u)
                    act.dma_start(mod_raw[u // 2:u // 2 + 1, (u % 2) * 256:(u % 2) * 256 + 256], rowt[0:1, u % 2, :]).then_inc(row_sent, 16)
            def k_out(h):
                act.wait_ge(kt_mm, h + 1)
                if h >= 2:
                    act.wait_ge(ds_mm, h - 1)
                act.activation(k_nat[:, h % 2, :], ps[:, 0:2, :].rearrange("p a b -> p (a b)"), ACT.Copy).then_inc(kt_ready, 1)

            def o_out(h):
                o_ = ps[:, 4:6, :].rearrange("p a b -> p (a b)")
                act.wait_ge(o_mm, h + 1)
                if h >= 2:
                    act.wait_ge(os_mm, h - 1)
                act.activation(osq[:, h % 2, :], o_, ACT.Square).then_inc(osq_ready, 1)
                act.activation(kbuf[:, h, :], o_, ACT.Copy, scale=PR("hg", h)).then_inc(osb_ready, 1)

            def head_root(h):
                act.wait_ge(os_mm, h + 1)
                act.activation(hrt[:, h, :], ps[:, 6, 0:NCHUNK], ACT.Sqrt, bias=eps, scale=1.0 / P).then_inc(hsd_ready, 1)

            def wo_high(n):
                act.activation(wo_hi[:, 2 * n:2 * n + 2, :], ring[n // 4][:, 2 * (n % 4):2 * (n % 4) + 2, :], ACT.Copy).then_inc(wohi_ready, 1)

            act.wait_ge(ld_ring[0], 16 * 4)
            act.wait_ge(proj_done, len(GROUPS))
            for n in range(4):
                wo_high(n)
            k_out(0)
            k_out(1)
            for h in range(HEADS):
                o_out(h)
                if h + 2 < HEADS:
                    k_out(h + 2)
                head_root(h)
                if h == 0:
                    act.wait_ge(ld_ring[1], 16 * 4)
                wo_high(4 + h)

            def s_high(i):
                for part, src in enumerate((rgbuf, gzbuf)):
                    if i == 0:
                        act.wait_ge((ob_ready, oa_ready)[part], 4)
                    act.activation(s_hi[:, i % 2, part * CH:(part + 1) * CH].rearrange("p (a b) -> p a b", a=CT),
                                   src[:, :, i * P:(i + 1) * P], ACT.Copy).then_inc(shi_ready, 1)

            s_high(0)
            s_high(1)
            def h2_out(i):
                act.wait_ge(h2t_mm, i + 1)
                if i >= 2:
                    act.wait_ge(logit_mm, i - 1)
                act.activation(h2T[:, i % 2, :], ps[:, 4:6, :].rearrange("p a b -> p (a b)"), ACT.Copy).then_inc(h2t_ready, 1)

            for i in range(NT):
                act.wait_ge(mix_mm, i + 1)
                if i + 2 < NT:
                    s_high(i + 2)
                link(act.activation(junk, ps[:, 2 * (i % 2):2 * (i % 2) + 2, :].rearrange("p a b -> p (a b)"), ACT.Square, accum_out=ssq[:, 0, i:i + 1]))
                act.activation(ssq[:, 0, i:i + 1], ssq[:, 0, i:i + 1], ACT.Sqrt, bias=eps, scale=1.0 / D).then_inc(ss_ready, 1)
                if i:
                    h2_out(i - 1)
                act.wait_ge(x1_ready, i + 1)
                link(act.activation(junk, x1[:, i, :], ACT.Square, accum_out=ssq[:, 1, i:i + 1]))
                act.activation(ssq[:, 1, i:i + 1], ssq[:, 1, i:i + 1], ACT.Sqrt, bias=eps, scale=1.0 / D).then_inc(sd_ready, 1)
            h2_out(NT - 1)
            act.wait_ge(lg_ready, 1)
            lg = scratch[:, 0:NT * 36]
            act.activation(lg, lg, ACT.Exp).then_inc(ex_ready, 1)

            def x_out(b, q):
                act.wait_ge(xg_tr, b + 1)
                act.activation(x_hi[:, q, :], ps[:, 6:8, :].rearrange("p a b -> p (a b)"), ACT.Copy).then_inc(xt_ready, 1)

            def w_high(n, piece, free=True):
                for r in range(4):
                    if free:
                        act.wait_ge(w_used, n + (r - 3))
                    act.activation(w_hi[:, r, :], quarter(piece, r), ACT.Copy).then_inc(hi_ready, 1)

            def silu_out(h1_done):
                act.wait_ge(w_used, h1_done)
                act.activation(sil, ps[:, 0, :], ACT.Silu).then_inc(sil_ready, 1)

            def g_out(b):
                act.wait_ge(g_tr, b + 1)
                act.activation(g_hi, ps[:, 2, :], ACT.Copy).then_inc(ghi_ready, 1)

            def y_out(y_done):
                act.wait_ge(w_used, y_done)
                act.activation(y_sb[:, 0:HALF], ps[:, 3, :], ACT.Copy).then_inc(y_act, 1)

            act.wait_ge(ld_m[0], 16)
            w_high(0, m_slots[0], free=False)
            x_out(0, 0)
            act.wait_ge(ld_m[1], 16)
            w_high(4, m_slots[1])
            silu_out(4)
            x_out(1, 1)
            act.wait_ge(ld_m[2], 16)
            w_high(8, m_slots[2])

            def block_step(b, n, q, n3, n2, n1, sent, last=False):
                s3, s2, s1 = (3, 4, 5) if q == 1 else (0, 1, 2)
                act.wait_ge(ld_m[s3], n3)
                w_high(n, m_slots[s3])
                if b is not first:
                    act.wait_ge(w_used, n - 4)
                g_out(b - 1)
                silu_out(n)
                act.wait_ge(ld_m[s2], n2)
                w_high(n + 4, m_slots2[s2])
                if not last:
                    act.wait_ge(w_used, n - (8 if b is not first else 4))
                    x_out(b + 1, 1 - q)
                act.wait_ge(ld_m[s1], n1)
                w_high(n + 8, m_slots[s1] if not last else m_slots2[s1])
                if b is not first:
                    act.wait_ge(y_sent[q], sent)
                y_out(n + 8)

            first = 1
            block_step(first, 12, 1, 16, 16, 16, 0)
            block_step(2, 24, 0, 32, 32, 32, 16)
            with act.Fori(0, (NE - 4) // 2) as i:
                block_step(2 * i + 3, 24 * i + 36, 1, 16 * i + 32, 16 * i + 32, 16 * i + 32, 16 * i + 16)
                block_step(2 * i + 4, 24 * i + 48, 0, 16 * i + 48, 16 * i + 48, 16 * i + 48, 16 * i + 32)
            b = NE - 1
            block_step(b, 12 * b, 1, 256, 256, 256, 16 * (b // 2), last=True)
            act.wait_ge(w_used, 12 * b + 8)
            g_out(b)
            act.wait_ge(y_sent[0], 8 * NE)
            y_out(12 * b + 12)
            n_over = act.value_load(over[0:1, 15:16], min_val=0, max_val=N_OVER)
            for q in range(2):
                act.wait_ge(y_sent[q], 8 * NE)
            with act.If(n_over > 0):
                with act.Fori(0, N_OVER) as o:
                    with act.If(o < n_over):
                        act.wait_ge(ov_xtr, o + 1)
                        act.activation(x_hi[:, 0, :], ps[:, 6:8, :].rearrange("p a b -> p (a b)"), ACT.Copy).then_inc(ov_xhi, 1)
                        act.wait_ge(ld_ov, 48 * (o + 1))
                        for n in range(12):
                            if n >= 4:
                                act.wait_ge(ov_used, 12 * o + (n - 3))
                            if n == 8:
                                act.wait_ge(ov_used, 12 * o + 4)
                                act.activation(sil, ps[:, 0, :], ACT.Silu).then_inc(ov_sil, 1)
                            act.activation(w_hi[:, n % 4, :], quarter((m_slots[0], m_slots[1], m_slots2[2])[n // 4], n % 4), ACT.Copy).then_inc(ov_hi, 1)
                        act.wait_ge(ov_gtr, o + 1)
                        act.activation(g_hi, ps[:, 2, :], ACT.Copy).then_inc(ov_ghi, 1)
                        act.wait_ge(ov_used, 12 * o + 12)
                        act.activation(y_sb, ps[:, 3:5, :].rearrange("p a b -> p (a b)"), ACT.Copy).then_inc(ov_ysb, 1)
                        stand(act, ov_sent, 16 * (o + 1))
            def first_row(i):
                act.wait_ge(ld_y[i], 16)
                if i >= 2:
                    act.wait_ge(fin_g, i - 1)
                act.activation(y_sum[:, i % 2, :], y_pair[:, i, 0, :], ACT.Copy, scale=wtok[:, 0, i:i + 1]).then_inc(fin_a, 1)

            first_row(0)
            for i in range(NT):
                if i + 1 < NT:
                    first_row(i + 1)
                act.wait_ge(fin_b, i + 1)
                link(act.activation(junk, y_sum[:, i % 2, :], ACT.Square, accum_out=ssq[:, 2, i:i + 1]))
                act.activation(ssq[:, 2, i:i + 1], ssq[:, 2, i:i + 1], ACT.Sqrt, bias=eps, scale=1.0 / D).then_inc(fin_s, 1)

        @block.vector
        def _(dve):
            link = chain_of(dve, dve_chain)
            dve.wait_ge(ld_par, 16)
            mx, e0, e1, ab, s0, s1, s2 = (tiny[:, n, :] for n in (3, 0, 1, 2, 4, 5, 6))
            link(dve.tensor_tensor(mx, PR("gam0"), PR("gam1"), ALU.max))
            dve.tensor_tensor(e0, PR("gam0"), mx, ALU.subtract)
            dve.tensor_tensor(e1, PR("gam1"), mx, ALU.subtract)
            link(dve.tensor_scalar(s0, PR("lam"), -1.0, None, ALU.mult))
            dve.tensor_tensor(ab, PR("lam"), s0, ALU.min).then_inc(lbin_ready, 1)
            dve.wait_ge(lbexp_ready, 1)
            link(dve.tensor_tensor(s0, e0, e1, ALU.add))
            link(dve.reciprocal(s1, s0))
            dve.tensor_tensor(lb, e0, s1, ALU.mult)
            dve.tensor_tensor(omlb, e1, s1, ALU.mult)
            link(dve.tensor_scalar(s0, ab, 2.0, None, ALU.add))
            link(dve.reciprocal(s0, s0))
            link(dve.tensor_tensor(s0, ab, s0, ALU.mult))
            link(dve.tensor_tensor(s1, s0, s0, ALU.mult))
            link(dve.memset(s2, 1.0 / 19.0))
            for n in range(17, 0, -2):
                link(dve.tensor_tensor(s2, s2, s1, ALU.mult))
                link(dve.tensor_scalar(s2, s2, 1.0 / n, None, ALU.add))
            link(dve.tensor_tensor(s2, s2, s0, ALU.mult))
            link(dve.tensor_scalar(s1, PR("lam"), 0.0, 8.0, ALU.min, ALU.mult))
            link(dve.scalar_tensor_tensor(cl, s2, -16.0, s1, ALU.mult, ALU.add))

            def ada_acc(dst, src, n):
                link(dve.tensor_scalar(dst, src[:, 0, :], cs[:, 0:1], None, ALU.mult))
                for k in range(1, KD):
                    ins = dve.scalar_tensor_tensor(dst, src[:, k, :], cs[:, k:k + 1], dst, ALU.mult, ALU.add)
                    if k < KD - 1:
                        link(ins)
                ins.then_inc(acc_ready, 1)

            dve.wait_ge(cs_ready, 1)
            for n in range(2):
                dve.wait_ge(ld_early[n], 16)
                ada_acc(acc_early[:, n, :], early[n], n)
            dve.wait_ge(rms_ready, 1)
            link(dve.reciprocal(rbc, rbc))
            for k in range(KD):
                dve.tensor_tensor(hT[:, k, :], hT[:, k, :], rbc, ALU.mult).then_inc(xs_ready, 1)
            dve.wait_ge(modc_ready, 4)
            o = PARAM["b_ada"][0]
            dve.tensor_tensor(SH1, ps[:, 2, 0:8], par[:, o:o + 8], ALU.add)
            link(dve.tensor_tensor(A1, ps[:, 2, 8:16], par[:, o + 8:o + 16], ALU.add))
            dve.scalar_tensor_tensor(A1, A1, 1.0, PR("g_pre"), ALU.add, ALU.mult).then_inc(a1_ready, 1)
            for step in STEPS:
                kind = step[0]
                if kind == "conv":
                    ct = step[1]
                    dve.wait_ge(evac_done, GROUPS[("xr", ct, 1)] + 1)
                    if ct:
                        dve.wait_ge(scan_done, ct)
                    link(dve.tensor_scalar(xc, rgbuf[:, ct, :], PR("cw3", ct), PR("cb", ct), ALU.mult, ALU.add))
                    for j in range(1, 4):
                        ins = dve.scalar_tensor_tensor(xc[:, j:T], rgbuf[:, ct, 0:T - j], PR(f"cw{3 - j}", ct), xc[:, j:T], ALU.mult, ALU.add)
                        if j < 3:
                            link(ins)
                    ins.then_inc(conv_done, 1)
                elif kind == "gate":
                    ct = step[1]
                    dve.wait_ge(gates_ready, 4 * ct + 4)
                    dve.wait_ge(gate_mm, ct + 1)
                    link(dve.tensor_tensor(igate, igate, xc, ALU.mult))
                    link(dve.tensor_tensor(xc, rgate, rgate, ALU.mult))
                    dve.scalar_tensor_tensor(xc, xc, 1.0, th, ALU.add, ALU.mult).then_inc(sqrt_in, 1)
                    dve.wait_ge(sqrt_out, ct + 1)
                    link(dve.tensor_tensor(igate, igate, xc, ALU.mult))
                    dve.tensor_tensor_scan(rgbuf[:, ct, :], rgate, igate, 0.0, ALU.mult, ALU.add).then_inc(scan_done, 1)
                elif kind == "gelu_mul":
                    ct = step[1]
                    dve.wait_ge(evac_done, GROUPS[("yr", ct, 1)] + 1)
                    dve.wait_ge(scan_done, ct + 1)
                    dve.tensor_tensor(rgbuf[:, ct, :], rgbuf[:, ct, :], gy[:, ct, :], ALU.mult).then_inc(gmul_done, 1)
                elif kind == "ada":
                    u = step[1]
                    dve.wait_ge(ld_ada, 16 * (u + 1))
                    if u >= 2:
                        dve.wait_ge(row_mm, u - 1)
                    ada_acc(acc[:, u % 2, :], ada_half, u)
                elif kind == "rg_norm":
                    dve.wait_ge(rgrms_ready, 1)
                    link(dve.reciprocal(igate, igate))
                    for ct in range(CT):
                        dve.scalar_tensor_tensor(rgbuf[:, ct, :], rgbuf[:, ct, :], PR("rgg", ct), igate, ALU.mult, ALU.mult).then_inc(ob_ready, 1)
                elif kind == "prep":
                    h = step[1]
                    dve.wait_ge(evac_done, GROUPS[("f", h, 1)] + 1)
                    fo = pairs(fbuf[:, h, :], 1)[:, :, 1, :]
                    qo, ko = pairs(qbuf[:, h, :], 1)[:, :, 1, :], pairs(kbuf[:, h, :], 1)[:, :, 1, :]
                    rec = t2buf[:, h, :].unsqueeze(2)
                    dve.tensor_scalar(kbuf[:, h, :], kbuf[:, h, :], omlb[:, h:h + 1], None, ALU.mult)
                    link(dve.tensor_scalar(fbuf[:, h, :], fbuf[:, h, :], omlb[:, h:h + 1], lb[:, h:h + 1], ALU.mult, ALU.add))
                    dve.tensor_tensor(qo, qo, fo, ALU.mult)
                    link(dve.reciprocal(rec, fo))
                    dve.tensor_tensor(ko, ko, rec, ALU.mult).then_inc(prep_done, 1)
                elif kind == "base":
                    h = step[1]
                    n = LEVEL_ORDER[step]
                    bank, _ = level_bank(step)
                    dve.wait_ge(step_mm, n + 1)
                    if h == 0:
                        dve.wait_ge(p_zero, 1)
                        dve.wait_ge(ld_msk, 16)
                    v3 = lambda a: a.rearrange("p (c t) -> p c t", t=P)
                    dve.copy_predicated(v3(pbuf[:, h, :]), msk[:, 0:P].unsqueeze(1).to_broadcast([P, NCHUNK, P]),
                                        v3(ps[:, bank:bank + 2, :].rearrange("p a b -> p (a b)"))).then_inc(merged, 1)
                    q2, k2, f2 = (b[:, h, :].rearrange("p (b two) -> p b two", two=2) for b in (qbuf, kbuf, fbuf))
                    dve.tensor_tensor(q2, q2, f2[:, :, 0:1].to_broadcast([P, T // 2, 2]), ALU.mult)
                    dve.tensor_tensor(k2, k2, f2[:, :, 1:2].to_broadcast([P, T // 2, 2]), ALU.mult)
                    dve.tensor_tensor(t2buf[:, h, :].unsqueeze(2), f2[:, :, 0:1], f2[:, :, 1:2], ALU.mult).then_inc(updated, 1)
                elif kind == "level":
                    _, m, h = step
                    n = LEVEL_ORDER[step]
                    bank, _ = level_bank(step)
                    dve.wait_ge(step_mm, n + 1)
                    j = P // (2 * m)
                    o = MASK_BASE + 64 * LEVELS.index(m)
                    dst = pbuf[:, h, :].rearrange("p (c j two m) -> p c j two m", c=NCHUNK, two=2, m=m)[:, :, :, 1, :]
                    sc = ps[:, bank:bank + 2, :].rearrange("p a b -> p (a b)").rearrange("p (c j two m) -> p c j two m", c=NCHUNK, two=2, m=m)
                    mk = msk[:, o:o + 64].rearrange("p (j m) -> p j m", m=m).unsqueeze(1).to_broadcast([P, NCHUNK, j, m])
                    dve.copy_predicated(dst, mk, sc[:, :, :, 1, :]).then_inc(merged, 1)
                    tm = block_products(h, m).rearrange("p (b two) -> p b two", two=2)
                    qo, ke = pairs(qbuf[:, h, :], m)[:, :, 1, :], pairs(kbuf[:, h, :], m)[:, :, 0, :]
                    nb = T // (2 * m)
                    dve.wait_ge(updated, n - 3)
                    dve.tensor_tensor(qo, qo, tm[:, :, 0:1].to_broadcast([P, nb, m]), ALU.mult)
                    dve.tensor_tensor(ke, ke, tm[:, :, 1:2].to_broadcast([P, nb, m]), ALU.mult)
                    dve.tensor_tensor(block_products(h, 2 * m).unsqueeze(2), tm[:, :, 0:1], tm[:, :, 1:2], ALU.mult).then_inc(updated, 1)
            def fix_rows():
                dve.wait_ge(ld_fix, 32)
                r, b_, a_, g_ = (modfix[0:32, n, :] for n in range(4))
                link(dve.tensor_tensor(r, r, b_, ALU.add))
                link(dve.tensor_tensor(r, r, a_, ALU.add))
                dve.tensor_tensor(r, r, g_, ALU.mult).then_inc(fix_ready, 1)

            fix_rows()

            def state_chain(h):
                dve.wait_ge(ds_mm, h + 1)
                if h >= 2:
                    dve.wait_ge(o_mm, h - 1)
                if h == 0:
                    dve.wait_ge(updated, len(LEVEL_ORDER))
                st = states[:, h % 2, :].rearrange("p (c v) -> p c v", v=P)
                ds = ps[:, 2:4, :].rearrange("p a b -> p (a b)").rearrange("p (c v) -> p c v", v=P)
                ins = dve.tensor_copy(st[:, 1, :], ds[:, 0, :])
                for c in range(1, NCHUNK - 1):
                    link(ins)
                    ins = dve.scalar_tensor_tensor(st[:, c + 1, :], st[:, c, :], ptot[:, h, c:c + 1], ds[:, c, :], ALU.mult, ALU.add)
                ins.then_inc(st_ready, 1)

            def head_gate(h):
                dve.wait_ge(osb_ready, h + 1)
                dve.tensor_tensor(gzbuf[:, h, :], gzbuf[:, h, :], kbuf[:, h, :], ALU.mult).then_inc(gzo_ready, 1)

            def head_diag(h):
                dve.wait_ge(hsd_ready, h + 1)
                link(dve.reciprocal(hrt[:, h, :], hrt[:, h, :]))
                dve.tensor_tensor(diag[:, h % 2, :].rearrange("p (c t) -> p c t", c=NCHUNK), ident.unsqueeze(1).to_broadcast([P, NCHUNK, P]),
                                  hrt[:, h, :].unsqueeze(2).to_broadcast([P, NCHUNK, P]), ALU.mult).then_inc(diag_ready, 1)

            def head_norm(h):
                dve.wait_ge(bc_mm, h + 1)
                dve.wait_ge(gzo_ready, h + 1)
                dve.tensor_tensor(gzbuf[:, h, :], gzbuf[:, h, :], ps[:, 6:8, :].rearrange("p a b -> p (a b)"), ALU.mult).then_inc(oa_ready, 1)

            state_chain(0)
            state_chain(1)
            for h in range(HEADS):
                head_gate(h)
                if h:
                    head_norm(h - 1)
                if h + 2 < HEADS:
                    state_chain(h + 2)
                head_diag(h)
                for n in range(2 * h, 2 * h + 2):
                    dve.wait_ge(wohi_ready, n + 1)
                    dve.tensor_tensor(wo_lo[:, 2 * n:2 * n + 2, :], ring[n // 4][:, 2 * (n % 4):2 * (n % 4) + 2, :],
                                      wo_hi[:, 2 * n:2 * n + 2, :].bitcast(F32), ALU.subtract).then_inc(wolo_ready, 1)

            def s_low(i):
                for part, src in enumerate((rgbuf, gzbuf)):
                    dve.wait_ge(shi_ready, 2 * i + part + 1)
                    if i == 0:
                        dve.wait_ge((ob_ready, oa_ready)[part], 4)
                    split = lambda a: a[:, i % 2, part * CH:(part + 1) * CH].rearrange("p (a b) -> p a b", a=CT)
                    dve.tensor_tensor(split(s_lo), src[:, :, i * P:(i + 1) * P], split(s_hi.bitcast(F32)), ALU.subtract).then_inc(slo_ready, 1)

            head_norm(HEADS - 1)
            s_low(0)
            s_low(1)
            dve.wait_ge(ld_mod, 32)
            gate1, shift2, scale2 = modbc[:, 0, :], modbc[:, 1, :], modbc[:, 2, :]
            for i in range(NT):
                if i + 2 < NT:
                    s_low(i + 2)
                dve.wait_ge(ss_ready, i + 1)
                link(dve.reciprocal(rst[:, 0, i:i + 1], ssq[:, 0, i:i + 1]))
                mix = ps[:, 2 * (i % 2):2 * (i % 2) + 2, :].rearrange("p a b -> p (a b)")
                link(dve.scalar_tensor_tensor(x1[:, i, :], mix, rst[:, 0, i:i + 1], gate1, ALU.mult, ALU.mult))
                dve.wait_ge(ld_xt[i % 2], 16 * (i // 2 + 1))
                dve.tensor_tensor(x1[:, i, :], x1[:, i, :], xtile[:, i % 2, :], ALU.add).then_inc(x1_ready, 1)
                dve.wait_ge(sd_ready, i + 1)
                link(dve.reciprocal(rst[:, 1, i:i + 1], ssq[:, 1, i:i + 1]))
                if i >= 2:
                    dve.wait_ge(h2_sent, 16 * (i - 1))
                    dve.wait_ge(h2t_mm, i - 1)
                link(dve.scalar_tensor_tensor(h2[:, i % 2, :], x1[:, i, :], rst[:, 1, i:i + 1], scale2, ALU.mult, ALU.mult))
                dve.tensor_tensor(h2[:, i % 2, :], h2[:, i % 2, :], shift2, ALU.add).then_inc(h2_ready, 1)

            as32 = lambda a: a.bitcast(F32)

            def w_low(n, piece):
                for r in range(4):
                    dve.wait_ge(hi_ready, n + (r + 1))
                    dve.tensor_tensor(w_lo[:, r, :], quarter(piece, r), as32(w_hi[:, r, :]), ALU.subtract).then_inc(lo_ready, 1)

            rt = [0]

            def tmp(*shape):
                n = int(np.prod(shape))
                a = scratch[:, rt[0]:rt[0] + n]
                rt[0] += n
                assert rt[0] <= 3 * T
                if len(shape) == 2:
                    a = a.rearrange("p (a b) -> p a b", a=shape[0])
                elif len(shape) == 3:
                    a = a.rearrange("p (a b c) -> p a b c", a=shape[0], b=shape[1])
                return a

            lg = tmp(NT, 36)
            dve.wait_ge(logit_mm, NT)
            o = PARAM["rbias"][0]
            link(dve.tensor_tensor(lg, ps[:, 6, 0:NT * 36].rearrange("p (t e) -> p t e", t=NT),
                                   par[:, o:o + 36].unsqueeze(1).to_broadcast([P, NT, 36]), ALU.add))
            lgg = lg[:, :, 0:NG]
            lge = lg[:, :, NG:].rearrange("p t (g e) -> p t g e", g=NG)
            gmax, emax = tmp(NT, 1), tmp(NT, NG, 1)
            dve.tensor_reduce(gmax, lgg, AX.X, ALU.max)
            link(dve.tensor_reduce(emax, lge, AX.X, ALU.max))
            dve.tensor_tensor(lgg, lgg, gmax.to_broadcast([P, NT, NG]), ALU.subtract)
            dve.tensor_tensor(lge, lge, emax.to_broadcast([P, NT, NG, EPG]), ALU.subtract).then_inc(lg_ready, 1)
            dve.wait_ge(ex_ready, 1)

            def top(vals, n, rev):
                m, w, wm, oh = tmp(NT, 1), tmp(NT, n), tmp(NT, 1), tmp(NT, n)
                link(dve.tensor_reduce(m, vals, AX.X, ALU.max))
                link(dve.tensor_tensor(w, vals, m.to_broadcast([P, NT, n]), ALU.is_equal))
                link(dve.tensor_tensor(w, w, C(rev).unsqueeze(1).to_broadcast([P, NT, n]), ALU.mult))
                link(dve.tensor_reduce(wm, w, AX.X, ALU.max))
                link(dve.tensor_tensor(oh, w, wm.to_broadcast([P, NT, n]), ALU.is_equal))
                return m, oh

            gsum = tmp(NT, 1)
            link(dve.tensor_reduce(gsum, lgg, AX.X, ALU.add))
            link(dve.reciprocal(gsum, gsum))
            gm, ohg = top(lgg, NG, "rev4")
            gate = tmp(NT, 1)
            link(dve.tensor_tensor(gate, gm, gsum, ALU.mult))
            picked = tmp(NT, EPG, NG)
            se = tmp(NT, EPG)
            link(dve.tensor_tensor(picked, lge.rearrange("p t g e -> p t e g"), ohg.unsqueeze(2).to_broadcast([P, NT, EPG, NG]), ALU.mult))
            link(dve.tensor_reduce(se.unsqueeze(3), picked, AX.X, ALU.add))
            esum = tmp(NT, 1)
            link(dve.tensor_reduce(esum, se, AX.X, ALU.add))
            link(dve.reciprocal(esum, esum))
            m1, oh1 = top(se, EPG, "rev8")
            se2 = tmp(NT, EPG)
            link(dve.scalar_tensor_tensor(se2, oh1, -2.0, se, ALU.mult, ALU.add))
            m2, oh2 = top(se2, EPG, "rev8")
            p1, p2, den = tmp(NT, 1), tmp(NT, 1), tmp(NT, 1)
            dve.tensor_tensor(p1, m1, esum, ALU.mult)
            link(dve.tensor_tensor(p2, m2, esum, ALU.mult))
            link(dve.tensor_tensor(den, p1, p2, ALU.add))
            link(dve.reciprocal(den, den))
            link(dve.tensor_tensor(den, den, gate, ALU.mult))
            dve.tensor_tensor(wtok[:, 0, :].unsqueeze(2), p1, den, ALU.mult)
            dve.tensor_tensor(wtok[:, 1, :].unsqueeze(2), p2, den, ALU.mult)
            m_j = [tmp(NT, NE) for _ in range(2)]
            for j, oh in enumerate((oh1, oh2)):
                link(dve.tensor_tensor(m_j[j].rearrange("p t (g e) -> p t g e", g=NG), ohg.unsqueeze(3).to_broadcast([P, NT, NG, EPG]),
                                       oh.unsqueeze(2).to_broadcast([P, NT, NG, EPG]), ALU.mult))
            dve.memset(m_pre[:, 0, :], 0.0)
            link(dve.tensor_tensor(m_all, m_j[0], m_j[1], ALU.add))
            for i in range(NT):
                ins = dve.tensor_tensor(m_pre[:, i + 1, :], m_pre[:, i, :], m_all[:, i, :], ALU.add)
                if i < NT - 1:
                    link(ins)
            ins.then_inc(mm_ready, 1)
            w_low(0, m_slots[0])
            dve.wait_ge(rank_mm, 1)
            rank, cnt = ps[:, 0, 0:NT * NE].rearrange("p (t e) -> p t e", t=NT), ps[:, 1, 0:NE]
            n_i, n_f, end, beg = tmp(NE).bitcast(I32), tmp(NE), tmp(NE), tmp(NE)
            link(dve.tensor_scalar(n_f, cnt, 1.0, -1.0, ALU.max, ALU.add))
            link(dve.tensor_copy(n_i, n_f))
            link(dve.tensor_scalar(n_i, n_i, 7, None, ALU.logical_shift_right))
            link(dve.tensor_copy(n_f, n_i))
            link(dve.tensor_tensor_scan(end, C("ones")[:, 0:NE], n_f, 0.0, ALU.mult, ALU.add))
            link(dve.tensor_tensor(beg, end, n_f, ALU.subtract))
            rj, ej, oj = tmp(2, NT, 1), tmp(2, NT, 1), tmp(2, NT, 1)
            prod = tmp(NT, NE)
            for j in range(2):
                for dst, src in ((rj, rank), (ej, C("iota32").unsqueeze(1).to_broadcast([P, NT, NE])),
                                 (oj, beg.unsqueeze(1).to_broadcast([P, NT, NE]))):
                    link(dve.tensor_tensor(prod, m_j[j], src, ALU.mult))
                    link(dve.tensor_reduce(dst[:, j], prod, AX.X, ALU.add))
            r_i, b_i, s_i = (tmp(16).bitcast(I32) for _ in range(3))
            b_f, s_f, is_o, blk = (tmp(16) for _ in range(4))
            rj, ej, oj = (a.rearrange("p j t o -> p (j t o)") for a in (rj, ej, oj))
            link(dve.tensor_copy(r_i, rj))
            dve.tensor_scalar(b_i, r_i, 7, None, ALU.logical_shift_right)
            link(dve.tensor_scalar(s_i, r_i, 127, None, ALU.bitwise_and))
            dve.tensor_copy(s_f, s_i)
            link(dve.tensor_copy(b_f, b_i))
            link(dve.tensor_scalar(is_o, b_f, 1.0, None, ALU.min))
            link(dve.tensor_tensor(blk, oj, b_f, ALU.add))
            link(dve.scalar_tensor_tensor(blk, blk, float(NE - 1), ej, ALU.add, ALU.subtract))
            link(dve.tensor_tensor(blk, blk, is_o, ALU.mult))
            link(dve.tensor_tensor(blk, blk, ej, ALU.add))
            for n in range(0, 16, 4):
                if n >= 8:
                    dve.wait_ge(tab_mm, n - 4)
                q = n // 4 % 2
                wide = lambda a, m: a.unsqueeze(1).to_broadcast([P, 4, m])
                each = lambda a, m: a.unsqueeze(2).to_broadcast([P, 4, m])
                o = CONST["tok"][0] + n
                dve.tensor_tensor(a_oh[:, q], wide(C("iota128"), P), each(s_f[:, n:n + 4], P), ALU.is_equal)
                link(dve.tensor_tensor(b_oh[:, q], wide(C("iota47"), N_BLOCKS), each(blk[:, n:n + 4], N_BLOCKS), ALU.is_equal))
                dve.tensor_tensor(b_oh[:, q], b_oh[:, q], each(con[:, o:o + 4], N_BLOCKS), ALU.mult).then_inc(ab_ready, 1)
            cmp = tmp(N_OVER, NE)
            ov = tmp(16)
            link(dve.tensor_tensor(cmp, end.unsqueeze(1).to_broadcast([P, N_OVER, NE]), C("iota15").unsqueeze(2).to_broadcast([P, N_OVER, NE]), ALU.is_le))
            link(dve.tensor_reduce(ov[:, 0:N_OVER].unsqueeze(2), cmp, AX.X, ALU.add))
            link(dve.tensor_scalar(ov[:, 0:N_OVER], ov[:, 0:N_OVER], float(NE - 1), None, ALU.min))
            link(dve.tensor_copy(ov[:, 15:16], end[:, NE - 1:NE]))
            link(dve.tensor_copy(over, ov))
            dve.wait_ge(tab_mm, 16)
            link(dve.tensor_scalar(tbl, ps[:, 2, 0:N_BLOCKS], float(UNUSED), None, ALU.add))
            spare = tmp(N_BLOCKS).bitcast(I32)
            dve.tensor_scalar(spare, tbl, UNUSED, None, ALU.bitwise_and)
            link(dve.tensor_scalar(ttab, tbl, T - 1, None, ALU.bitwise_and))
            dve.tensor_tensor(ttab, ttab, spare, ALU.add).then_inc(route_ready, 1)

            def x_low(b, q):
                dve.wait_ge(xt_ready, b + 1)
                dve.tensor_tensor(x_lo[:, q, :], ps[:, 6:8, :].rearrange("p a b -> p (a b)"), as32(x_hi[:, q, :]), ALU.subtract).then_inc(xlo_ready, 1)

            def g_low(b):
                dve.wait_ge(ghi_ready, b + 1)
                dve.tensor_tensor(g_lo, ps[:, 2, :], as32(g_hi), ALU.subtract).then_inc(glo_ready, 1)

            def g_out(b, h3_done):
                dve.wait_ge(sil_ready, b + 1)
                dve.wait_ge(w_used, h3_done)
                dve.tensor_tensor(sil, sil, ps[:, 1, :], ALU.mult).then_inc(g_ready, 1)

            def y_half(y_done):
                dve.wait_ge(w_used, y_done)
                dve.tensor_copy(y_sb[:, HALF:D], ps[:, 4, :]).then_inc(y_dve, 1)

            x_low(0, 0)
            w_low(4, m_slots[1])
            g_out(0, 8)
            x_low(1, 1)
            w_low(8, m_slots[2])

            def block_step(b, n, q, sent, last=False):
                s3, s2, s1 = (3, 4, 5) if q == 1 else (0, 1, 2)
                w_low(n, m_slots[s3])
                g_low(b - 1)
                w_low(n + 4, m_slots2[s2])
                g_out(b, n + 4)
                if not last:
                    x_low(b + 1, 1 - q)
                w_low(n + 8, m_slots[s1] if not last else m_slots2[s1])
                if b is not first:
                    dve.wait_ge(y_sent[q], sent)
                y_half(n + 8)

            first = 1
            block_step(first, 12, 1, 0)
            block_step(2, 24, 0, 16)
            with dve.Fori(0, (NE - 4) // 2) as i:
                block_step(2 * i + 3, 24 * i + 36, 1, 16 * i + 16)
                block_step(2 * i + 4, 24 * i + 48, 0, 16 * i + 32)
            b = NE - 1
            block_step(b, 12 * b, 1, 16 * (b // 2), last=True)
            g_low(b)
            dve.wait_ge(y_sent[0], 8 * NE)
            y_half(12 * b + 12)
            n_over = dve.value_load(over[0:1, 15:16], min_val=0, max_val=N_OVER)
            with dve.If(n_over > 0):
                with dve.Fori(0, N_OVER) as o:
                    with dve.If(o < n_over):
                        dve.wait_ge(ov_xhi, o + 1)
                        dve.tensor_tensor(x_lo[:, 0, :], ps[:, 6:8, :].rearrange("p a b -> p (a b)"), as32(x_hi[:, 0, :]), ALU.subtract).then_inc(ov_xlo, 1)
                        for n in range(12):
                            if n == 8:
                                dve.wait_ge(ov_sil, o + 1)
                                dve.wait_ge(ov_used, 12 * o + 8)
                                dve.tensor_tensor(sil, sil, ps[:, 1, :], ALU.mult).then_inc(ov_g, 1)
                            dve.wait_ge(ov_hi, 12 * o + (n + 1))
                            dve.tensor_tensor(w_lo[:, n % 4, :], quarter((m_slots[0], m_slots[1], m_slots2[2])[n // 4], n % 4), as32(w_hi[:, n % 4, :]),
                                              ALU.subtract).then_inc(ov_lo, 1)
                        dve.wait_ge(ov_ghi, o + 1)
                        dve.tensor_tensor(g_lo, ps[:, 2, :], as32(g_hi), ALU.subtract).then_inc(ov_glo, 1)
                        stand(dve, ov_sent, 16 * (o + 1))
            def second_row(i):
                dve.wait_ge(fin_a, i + 1)
                dve.wait_ge(ld_y[i], 16)
                y = y_sum[:, i % 2, :]
                dve.scalar_tensor_tensor(y, y_pair[:, i, 1, :], wtok[:, 1, i:i + 1], y, ALU.mult, ALU.add).then_inc(fin_b, 1)

            second_row(0)
            for i in range(NT):
                y = y_sum[:, i % 2, :]
                if i + 1 < NT:
                    second_row(i + 1)
                dve.wait_ge(fin_s, i + 1)
                link(dve.reciprocal(rst[:, 2, i:i + 1], ssq[:, 2, i:i + 1]))
                if i >= 2:
                    dve.wait_ge(o_sent[i % 2], 16 * (i // 2))
                dve.scalar_tensor_tensor(o_tile[:, i % 2, :], y, rst[:, 2, i:i + 1], gate2, ALU.mult, ALU.mult).then_inc(fin_g, 1)
                dve.wait_ge(fin_g, i + 1)
                dve.tensor_tensor(o_tile[:, i % 2, :], o_tile[:, i % 2, :], x1[:, i, :], ALU.add).then_inc(fin_o, 1)

        @block.tensor
        def _(pe):
            mm = nc.tensor.matmul
            pe.wait_ge(ld_con, 16)
            for k in range(KD):
                pe.wait_ge(sq_ready, k + 1)
                for half in range(2):
                    ins = mm(ps[:, half, :], ones, sq[:, k % 2, half * HALF:(half + 1) * HALF], start=k == 0, stop=k == KD - 1)
                ins.then_inc(sq_summed, 1)
            for n in range(2):
                pe.wait_ge(acc_ready, n + 1)
                for j in range(4):
                    ins = mm(ps[:, 2, 4 * n + j:4 * n + j + 1], acc_early[:, n, j * P:(j + 1) * P], ones[:, 0:1], start=True, stop=True)
                ins.then_inc(modc_ready, 1)
            pe.wait_ge(cs_ready, 1)
            for n in range(2):
                pe.wait_ge(ld_early[2 + n], 16)
                for k in range(KD):
                    ins = mm(ps[0:1, 3 + n, :], cs[:, k:k + 1], early[2 + n][:, k, :], start=k == 0, stop=k == KD - 1)
                ins.then_inc(erow_mm, 1)
            for n in range(2):
                pe.wait_ge(erow_ready, n + 1)
                for j in range(4):
                    o = (4 * n + j) * P
                    ins = mm(ps[:, 2, 8 + 4 * n + j:9 + 4 * n + j], early_row[0:1, o:o + P], ones[0:1, 0:1], start=True, stop=True)
                ins.then_inc(modc_ready, 1)
            seen = set()
            for step in STEPS:
                kind = step[0]
                if kind == "proj":
                    _, name, a, half = step
                    g = GROUPS[step[1:]]
                    if g < 3:
                        pe.wait_ge(rms_ready, 1)
                        pe.wait_ge(a1_ready, 1)
                    else:
                        pe.wait_ge(evac_done, g - 2)
                    if name not in seen:
                        seen.add(name)
                        n = PIECES.index(name)
                        pe.wait_ge(ld_ring[n % 2], 16 * (n // 2 + 1))
                    w = ring[PIECES.index(name) % 2]
                    for k in range(KD):
                        if g == 0:
                            pe.wait_ge(h_ready, k + 1)
                        if name == "iv":
                            lhs, rhs = hT[:, k, a * P:(a + 1) * P], w[:, k, :]
                        else:
                            lhs, rhs = w[:, k, a * P:(a + 1) * P], hT[:, k, half * HALF:(half + 1) * HALF]
                        ins = mm(ps[:, g % 3, :], lhs, rhs, start=k == 0, stop=k == KD - 1)
                    ins.then_inc(proj_done, 1)
                elif kind == "gate":
                    ct = step[1]
                    pe.wait_ge(conv_done, ct + 1)
                    pe.wait_ge(ld_bd, 64)
                    if ct:
                        pe.wait_ge(gates_ready, 4 * ct)
                    for g in range(2):
                        for half in range(2):
                            ins = mm(ps[:, 4 + 2 * g + half, :], bd[:, g, ct, :], xc[:, half * HALF:(half + 1) * HALF], start=True, stop=True)
                    ins.then_inc(gate_mm, 1)
                elif kind == "rg_norm":
                    pe.wait_ge(gates_ready, 4 * CT)
                    for ct in range(CT):
                        pe.wait_ge(rgsq_ready, ct + 1)
                        for half in range(2):
                            ins = mm(ps[:, 4 + half, :], ones, (xc, rgate)[ct % 2][:, half * HALF:(half + 1) * HALF], start=ct == 0, stop=ct == CT - 1)
                        ins.then_inc(rgsq_summed, 1)
                elif kind == "row":
                    u = step[1]
                    pe.wait_ge(acc_ready, 2 + u + 1)
                    if u:
                        pe.wait_ge(row_ready, u)
                    mm(ps[0:1, 3, (u % 2) * 256:(u % 2) * 256 + 256], ones[:, 0:1], acc[:, u % 2, :], start=True, stop=True).then_inc(row_mm, 1)
                elif kind in ("base", "level"):
                    n = LEVEL_ORDER[step]
                    bank, free = level_bank(step)
                    h = step[-1]
                    if n == 0:
                        pe.wait_ge(rgrms_ready, 1)
                    if free:
                        pe.wait_ge(merged, free)
                    if kind == "base":
                        pe.wait_ge(prep_done, h + 1)
                    else:
                        pe.wait_ge(updated, n - 3)
                    out_ = ps[:, bank:bank + 2, :].rearrange("p a b -> p (a b)")
                    for c in range(NCHUNK):
                        ins = mm(out_[:, c * P:(c + 1) * P], kbuf[:, h, c * P:(c + 1) * P], qbuf[:, h, c * P:(c + 1) * P], start=True, stop=True)
                    ins.then_inc(step_mm, 1)

            def k_transposes(h):
                if h == 0:
                    pe.wait_ge(updated, len(LEVEL_ORDER))
                    pe.wait_ge(evac_done, len(GROUPS))
                    pe.wait_ge(row_ready, 16)
                    pe.wait_ge(merged, len(LEVEL_ORDER))
                else:
                    pe.wait_ge(kt_ready, h)
                o_ = ps[:, 0:2, :].rearrange("p a b -> p (a b)")
                for c in range(NCHUNK):
                    ins = nc.tensor.transpose(o_[:, c * P:(c + 1) * P], kbuf[:, h, c * P:(c + 1) * P], ident)
                ins.then_inc(kt_mm, 1)

            def state_sums(h):
                pe.wait_ge(kt_ready, h + 1)
                if h:
                    pe.wait_ge(st_ready, h)
                o_ = ps[:, 2:4, :].rearrange("p a b -> p (a b)")
                for c in range(NCHUNK - 1):
                    ins = mm(o_[:, c * P:(c + 1) * P], k_nat[:, h % 2, c * P:(c + 1) * P], vbuf[:, c, h * P:(h + 1) * P], start=True, stop=True)
                ins.then_inc(ds_mm, 1)

            def outputs(h):
                pe.wait_ge(st_ready, h + 1)
                if h:
                    pe.wait_ge(osb_ready, h)
                o_ = ps[:, 4:6, :].rearrange("p a b -> p (a b)")
                for c in range(NCHUNK):
                    dst = o_[:, c * P:(c + 1) * P]
                    ins = mm(dst, vbuf[:, c, h * P:(h + 1) * P], pbuf[:, h, c * P:(c + 1) * P], start=True, stop=c == 0)
                    if c:
                        ins = mm(dst, states[:, h % 2, c * P:(c + 1) * P], qbuf[:, h, c * P:(c + 1) * P], start=False, stop=True)
                ins.then_inc(o_mm, 1)

            def output_sums(h):
                if h:
                    pe.wait_ge(oa_ready, h)
                pe.wait_ge(osq_ready, h + 1)
                for c in range(NCHUNK):
                    ins = mm(ps[:, 6, c:c + 1], osq[:, h % 2, c * P:(c + 1) * P], ones[:, 0:1], start=True, stop=True)
                ins.then_inc(os_mm, 1)

            def root_rows(h):
                pe.wait_ge(diag_ready, h + 1)
                if h:
                    pe.wait_ge(oa_ready, h)
                for half in range(2):
                    ins = mm(ps[:, 6 + half, :], ones, diag[:, h % 2, half * HALF:(half + 1) * HALF], start=True, stop=True)
                ins.then_inc(bc_mm, 1)

            for h in range(2):
                k_transposes(h)
                state_sums(h)
            for h in range(HEADS):
                outputs(h)
                if h:
                    root_rows(h - 1)
                if h + 2 < HEADS:
                    k_transposes(h + 2)
                output_sums(h)
                if h + 2 < HEADS:
                    state_sums(h + 2)
            root_rows(HEADS - 1)

            def products(out_, xh, xl, wh, wl, first_, last_):
                mm(out_, xh, wh, start=first_, stop=False)
                mm(out_, xh, wl, start=False, stop=False)
                return mm(out_, xl, wh, start=False, stop=last_)

            def mix(i):
                if i >= 2:
                    pe.wait_ge(x1_ready, i - 1)
                for half in range(2):
                    for k in range(KD):
                        if half == 0 and k % CT == 0:
                            pe.wait_ge(slo_ready, 2 * i + k // CT + 1)
                        ks, w = slice(k * P, (k + 1) * P), KD * half + (k + CT) % KD
                        ins = products(ps[:, 2 * (i % 2) + half, :], s_hi[:, i % 2, ks], s_lo[:, i % 2, ks], wo_hi[:, w, :], wo_lo[:, w, :],
                                       k == 0, k == KD - 1)
                ins.then_inc(mix_mm, 1)

            def logits(i):
                pe.wait_ge(h2_ready, i + 1)
                if i:
                    pe.wait_ge(h2t_ready, i)
                else:
                    pe.wait_ge(oa_ready, HEADS)
                o_ = ps[:, 4:6, :].rearrange("p a b -> p (a b)")
                for k in range(KD):
                    ins = nc.tensor.transpose(o_[:, k * P:(k + 1) * P], h2[:, i % 2, k * P:(k + 1) * P], ident)
                ins.then_inc(h2t_mm, 1)
                pe.wait_ge(h2t_ready, i + 1)
                for k in range(KD):
                    ins = mm(ps[:, 6, 36 * i:36 * i + 36], h2T[:, i % 2, k * P:(k + 1) * P], wrt[:, k, :], start=k == 0, stop=k == KD - 1)
                ins.then_inc(logit_mm, 1)

            pe.wait_ge(wolo_ready, 8)
            pe.wait_ge(ld_wrt, 16)
            mix(0)
            mix(1)
            for i in range(NT):
                logits(i)
                if i + 2 < NT:
                    mix(i + 2)
            pe.wait_ge(mm_ready, 1)
            flat = lambda a: a.rearrange("p t e -> p (t e)")
            mm(ps[:, 0, 0:NT * NE], C("upper"), flat(m_all), start=True, stop=False)
            mm(ps[:, 0, 0:NT * NE], ones, flat(m_pre[:, 0:NT, :]), start=False, stop=True)
            mm(ps[:, 1, 0:NE], ones, m_pre[:, NT, :], start=True, stop=True).then_inc(rank_mm, 1)
            for n in range(16):
                pe.wait_ge(ab_ready, n // 4 + 1)
                mm(ps[:, 2, 0:N_BLOCKS], a_oh[:, n // 4 % 2, n % 4, :], b_oh[:, n // 4 % 2, n % 4, :], start=n == 0, stop=n == 15).then_inc(tab_mm, 1)

            def x_transposes(b, q, loaded, wait_prev=True):
                pe.wait_ge(ld_g[q], loaded)
                if wait_prev:
                    pe.wait_ge(xlo_ready, b)
                o_ = ps[:, 6:8, :].rearrange("p a b -> p (a b)")
                for k in range(KD):
                    ins = nc.tensor.transpose(o_[:, k * P:(k + 1) * P], x_ring[:, q, k * P:(k + 1) * P], ident)
                ins.then_inc(xg_tr, 1)

            def hidden(bank, q, n, lo_s, used_s):
                for r in range(4):
                    pe.wait_ge(lo_s, n + (r + 1))
                    for kk in range(2):
                        k = 2 * r + kk
                        xs, ws = slice(k * P, (k + 1) * P), slice(kk * HALF, (kk + 1) * HALF)
                        ins = products(ps[:, bank, :], x_hi[:, q, xs], x_lo[:, q, xs], w_hi[:, r, ws], w_lo[:, r, ws], k == 0, k == KD - 1)
                    ins.then_inc(used_s, 1)

            def g_transposes(b):
                pe.wait_ge(g_ready, b + 1)
                for k in range(KF):
                    ins = nc.tensor.transpose(ps[:, 2, k * P:(k + 1) * P], sil[:, k * P:(k + 1) * P], ident)
                ins.then_inc(g_tr, 1)

            def down(n, lo_s, used_s):
                for r in range(KF):
                    pe.wait_ge(lo_s, n + (r + 1))
                    gs = slice(r * P, (r + 1) * P)
                    for half in range(2):
                        ws = slice(half * HALF, (half + 1) * HALF)
                        ins = products(ps[:, 3 + half, :], g_hi[:, gs], g_lo[:, gs], w_hi[:, r, ws], w_lo[:, r, ws], r == 0, r == KF - 1)
                    ins.then_inc(used_s, 1)

            pe.wait_ge(route_ready, 1)
            x_transposes(0, 0, 16, wait_prev=False)
            pe.wait_ge(xlo_ready, 1)
            hidden(0, 0, 0, lo_ready, w_used)
            hidden(1, 0, 4, lo_ready, w_used)
            x_transposes(1, 1, 16)

            def block_step(b, n, q, n_g, last=False):
                pe.wait_ge(xlo_ready, b + 1)
                pe.wait_ge(sil_ready, b)
                hidden(0, q, n - 4, lo_ready, w_used)
                g_transposes(b - 1)
                hidden(1, q, n, lo_ready, w_used)
                if not last:
                    x_transposes(b + 1, 1 - q, n_g)
                pe.wait_ge(glo_ready, b)
                if b is not first:
                    pe.wait_ge(y_act, b - 1)
                    pe.wait_ge(y_dve, b - 1)
                down(n + 4, lo_ready, w_used)

            first = 1
            block_step(first, 12, 1, 32)
            block_step(2, 24, 0, 32)
            with pe.Fori(0, (NE - 4) // 2) as i:
                block_step(2 * i + 3, 24 * i + 36, 1, 16 * i + 48)
                block_step(2 * i + 4, 24 * i + 48, 0, 16 * i + 48)
            b = NE - 1
            block_step(b, 12 * b, 1, 0, last=True)
            g_transposes(b)
            pe.wait_ge(glo_ready, b + 1)
            pe.wait_ge(y_act, b)
            pe.wait_ge(y_dve, b)
            down(12 * b + 8, lo_ready, w_used)
            n_over = pe.value_load(over[0:1, 15:16], min_val=0, max_val=N_OVER)
            pe.wait_ge(y_act, NE)
            pe.wait_ge(y_dve, NE)
            with pe.If(n_over > 0):
                with pe.Fori(0, N_OVER) as o:
                    with pe.If(o < n_over):
                        pe.wait_ge(ov_x, 16 * (o + 1))
                        o_ = ps[:, 6:8, :].rearrange("p a b -> p (a b)")
                        for k in range(KD):
                            ins = nc.tensor.transpose(o_[:, k * P:(k + 1) * P], x_ring[:, 0, k * P:(k + 1) * P], ident)
                        ins.then_inc(ov_xtr, 1)
                        pe.wait_ge(ov_xlo, o + 1)
                        hidden(0, 0, 12 * o, ov_lo, ov_used)
                        hidden(1, 0, 12 * o + 4, ov_lo, ov_used)
                        pe.wait_ge(ov_g, o + 1)
                        for k in range(KF):
                            ins = nc.tensor.transpose(ps[:, 2, k * P:(k + 1) * P], sil[:, k * P:(k + 1) * P], ident)
                        ins.then_inc(ov_gtr, 1)
                        pe.wait_ge(ov_glo, o + 1)
                        down(12 * o + 8, ov_lo, ov_used)
                        stand(pe, ov_sent, 16 * (o + 1))



def kernel(**inputs):
    import concourse.bacc as _bacc
    from concourse.bass_utils import run_bass_kernel_spmd as _run

    a = {k: np.asarray(v) for k, v in inputs.items()}
    col = lambda v: np.ascontiguousarray(v.reshape(-1, P).T)
    cols = {
        "c": col(a["c"][0]), "g_pre": col(a["g_pre_mix"][0]), "b_ada": col(a["b_ada"][0, :2 * D]),
        "gam0": col(a["hgrn_gamma"][0]), "gam1": col(a["hgrn_gamma"][1]), "hg": col(a["hgrn_norm_g"][0]),
        "cw0": col(a["conv_w"][0, 0]), "cw1": col(a["conv_w"][0, 1]), "cw2": col(a["conv_w"][0, 2]), "cw3": col(a["conv_w"][0, 3]),
        "cb": col(a["conv_b"][0]), "br": col(a["rg_b_r"][0]), "bi": col(a["rg_b_i"][0]), "lam": col(a["rg_lambda"][0]),
        "rgg": col(a["rg_norm_g"][0]),
        "rbias": np.broadcast_to(np.concatenate([a["b_router_group"][0], a["b_router_expert"][0]]), (P, 36)),
    }
    params = np.concatenate([cols[n] for n in PARAM], axis=1)
    i128 = np.arange(P)
    const = {
        "ident": np.eye(P), "ones": np.ones((P, P)), "upper": (i128[:, None] < i128[None, :]),
        "iota128": np.broadcast_to(i128, (P, P)), "iota47": np.broadcast_to(np.arange(N_BLOCKS), (P, N_BLOCKS)),
        "iota32": np.broadcast_to(np.arange(NE), (P, NE)), "iota15": np.broadcast_to(np.arange(N_OVER), (P, N_OVER)),
        "tok": i128[:, None] + P * np.arange(2 * NT)[None, :] - UNUSED, "rev4": np.broadcast_to(np.arange(4, 0, -1), (P, 4)),
        "rev8": np.broadcast_to(np.arange(8, 0, -1), (P, 8)),
    }
    consts = np.concatenate([np.asarray(const[n], np.float32) for n in CONST], axis=1)
    s, t = i128[:, None], i128[None, :]
    mask = [(s // 2 == t // 2) & (s <= t)]
    for m in LEVELS:
        u = np.arange(64)[None, :]
        mask.append((s // (2 * m) == u // m) & ((s // m) % 2 == 0))
    masks = np.concatenate(mask, axis=1).astype(np.int32)
    g = {0: a["g_post_mix"][0], 2: a["g_pre_ffn"][0], 3: a["g_post_ffn"][0]}
    gain = np.concatenate([g.get(i, np.ones(D, np.float32)) for i in range(4)]).reshape(32, P)
    addend = np.zeros((32, P), np.float32)
    addend[16:24] = 1.0
    mod_rows = np.stack([a["b_ada"][0, 2 * D:].reshape(32, P), addend, gain], axis=1)
    w_route = np.concatenate([a["w_router_group"][0], a["w_router_expert"][0]], axis=1).reshape(KD, P, 36).transpose(1, 0, 2)
    arrays = {
        "x": a["x"][0], "x_t": a["x"][0].T, "params": params, "consts": consts, "masks": masks, "w_ada": a["w_ada"][0],
        "mod_rows": mod_rows, "w_in": a["w_in"][0], "w_r": a["rg_w_r"][0], "w_i": a["rg_w_i"][0], "w_out": a["w_out"][0],
        "w_route": w_route, "w1": a["w1"][0], "w3": a["w3"][0], "w2": a["w2"][0],
    }
    arrays = {f"in_{k}": np.ascontiguousarray(v) for k, v in arrays.items()}
    nc = _bacc.Bacc("TRN2", target_bir_lowering=False, num_devices=1)
    args = [nc.dram_tensor(k, v.shape, mybir.dt.from_np(v.dtype), kind="ExternalInput").ap() for k, v in arrays.items()]
    out = nc.dram_tensor("out_0", (T, D), F32, kind="ExternalOutput").ap()
    build(nc, *args, out)
    r = _run(nc, [arrays], core_ids=[0])
    return r.results[0]["out_0"].reshape(1, T, D)
```

```python
import numpy as np
import concourse.bass as bass
from concourse import mybir

F32 = mybir.dt.float32
F32R = mybir.dt.float32r
I32 = mybir.dt.int32
ALU = mybir.AluOpType
ACT = mybir.ActivationFunctionType
AX = mybir.AxisListType

P = 128
D = 1024
T = 1024
KD = D // P
NT = T // P
HALF = 512
CH = 512
HEADS = 4
CT = CH // P
NG, EPG = 4, 8
NE = NG * EPG
FE = D // 2
KF = FE // P
NCHUNK = T // P
LEVELS = (2, 4, 8, 16, 32, 64)
N_OVER = (2 * T - NE) // P
N_BLOCKS = NE + N_OVER
EPS = 1e-6
UNUSED = 4096

PARAM = {}
_at = 0
for _name, _n in (("c", 8), ("g_pre", 8), ("b_ada", 16), ("gam0", 4), ("gam1", 4), ("hg", 4), ("cw0", 4), ("cw1", 4),
                  ("cw2", 4), ("cw3", 4), ("cb", 4), ("br", 4), ("bi", 4), ("lam", 4), ("rgg", 4), ("rbias", 36)):
    PARAM[_name] = (_at, _n)
    _at += _n
N_PARAM = _at
CONST = {}
_at = 0
for _name, _n in (("ident", P), ("ones", P), ("upper", P), ("iota128", P), ("iota47", N_BLOCKS), ("iota32", NE),
                  ("iota15", N_OVER), ("tok", 2 * NT), ("rev4", 4), ("rev8", 8)):
    CONST[_name] = (_at, _n)
    _at += _n
N_CONST = _at
MASK_BASE = P


def mixer_steps():
    steps = []
    ada = iter(range(16))
    pending = []

    def fill(name, a, half=0):
        steps.append(("proj", name, a, half))

    def ada_step():
        u = next(ada, None)
        if len(pending) == 2 or (pending and u is None):
            steps.append(("row", pending.pop(0)))
        if u is not None:
            steps.append(("ada", u))
            pending.append(u)

    def split(name, r):
        steps.append(("split", name, r))

    groups = [(name, ct, half) for name in ("xr", "yr", "q") for ct in range(CT) for half in range(2)]
    after = {1: ["conv0"], 3: ["gate0", "conv1"], 8: ["gate1", "conv2"], 12: ["gate2", "mul0"], 13: ["mul1"], 14: ["mul2"],
             16: ["conv3"], 17: ["gate3", "mul3"], 19: ["norm"]}
    for n, group in enumerate(groups):
        fill(*group)
        if n in (6, 8, 10, 12, 17, 19, 22):
            ada_step()
        for item in after.get(n, []):
            if item[:4] == "conv":
                steps.append(("conv", int(item[4])))
            elif item[:4] == "gate":
                steps += [("gate", int(item[4])), ("scan", int(item[4]))]
            elif item[:3] == "mul":
                steps.append(("gelu_mul", int(item[3])))
            else:
                steps.append(("rg_norm",))
        if 4 <= n < 8:
            split("yr", n - 4)
        if n == 15:
            for r in range(4):
                split("q", r)
        if n >= 20:
            split("iv", n - 20)
    for a in range(NT):
        fill("iv", a)
        if a in (0, 3, 6):
            ada_step()
    for r in range(4):
        split("gz", r)
    for h in range(HEADS):
        fill("gz", h, 0)
        ada_step()
        fill("gz", h, 1)
    steps.append(("restore",))
    pair = lambda hs, ms: [("level", m, h) if m > 1 else ("base", h) for m in ms for h in hs]
    early = pair((0, 1), (1, 2, 4, 8, 16))
    for h in range(HEADS):
        fill("f", h, 0)
        if h >= 2:
            steps += early[:2]
            early = early[2:]
        else:
            ada_step()
        fill("f", h, 1)
        if h >= 2:
            steps += early[:3]
            early = early[3:]
        steps.append(("prep", h))
    while pending:
        ada_step()
    rest = pair((2, 3), (1,) + LEVELS)
    first_pair = early + pair((0, 1), (32, 64))
    for i in range(max(len(rest), len(first_pair))):
        steps += first_pair[i:i + 1] + rest[i:i + 1]
        if i == len(first_pair) + 2:
            steps.append(("head", 0))
        if i == len(first_pair) + 5:
            steps.append(("head", 1))
    return steps


STEPS = mixer_steps()
GROUPS = {s[1:]: n for n, s in enumerate([s for s in STEPS if s[0] == "proj"])}
HEADS_EARLY = 2
LEVEL_ORDER = {s: n for n, s in enumerate([s for s in STEPS if s[0] in ("base", "level")])}
SPLIT = ["xr", "yr", "q", "iv", "gz"]
PIECES = SPLIT + ["f"]
PIECE_COL = {"q": 0, "f": 512, "iv": 1024, "gz": 1536, "xr": 2048, "yr": 2560}


def build(nc, x, x_t, params, consts, masks, w_ada, mod_rows, w_in, w_r, w_i, w_out, w_route, w1, w3, w2, out):
    KB = 256
    ps = nc.alloc_psum_tensor("banks", [P, 8, HALF], F32)
    h2_rows = nc.dram_tensor("h2_rows", [T, D], F32).ap()
    y_rows = nc.dram_tensor("y_rows", [2 * T, D], F32).ap()
    mod_raw = nc.dram_tensor("mod_raw", [8, HALF], F32).ap()
    mod_done = nc.dram_tensor("mod_done", [8, HALF], F32).ap()

    arena = nc.alloc_sbuf_tensor("arena", [P, 207 * KB], F32)
    base = nc.sbuf_base - 207 * 1024

    def halves(name, kb, a, b):
        return nc.alloc_sbuf_tensor_at(name, [P, a, b], F32R, offset=base + int(kb * 1024))[:, :, :]

    drawn = {}

    def region(kb, cols, dtype=None):
        if (kb, cols) not in drawn:
            drawn[kb, cols] = nc.alloc_sbuf_tensor_at(f"buf_{len(drawn)}", [P, cols], F32, offset=base + int(kb * 1024))[:, :]
        a = drawn[kb, cols]
        return a if dtype is None else a.bitcast(dtype)

    def region3(kb, a, b):
        return region(kb, a * b).rearrange("p (a b) -> p a b", a=a)

    ring = [region3(kb, KD, HALF) for kb in (0, 16)]
    hT = region3(32, KD, T)
    h_hi = halves("h_hi", 32, KD, T)
    h_lo_a, h_lo_b = halves("h_lo_a", 64, 4, T), halves("h_lo_b", 96, 4, T)
    win_hi = {n: halves(f"w_{n}_hi", kb, KD, HALF) for n, kb in (("xr", 80), ("yr", 144), ("iv", 112))}
    win_hi["q"], win_hi["gz"] = win_hi["yr"], win_hi["iv"]
    ring_lo = halves("ring_lo", 0, 2 * KD, HALF)
    fbuf = region3(64, HEADS, T)
    qbuf = region3(80, HEADS, T)
    kbuf = region3(96, HEADS, T)
    pbuf = region3(112, HEADS, T)
    vbuf = region3(128, NCHUNK, CH)
    gzbuf = region3(144, HEADS, T)
    rgbuf = region3(160, CT, T)
    t2buf = region3(176, HEADS, HALF)
    early = [region3(kb, KD, HALF) for kb in (64, 80, 128, 144)]
    sq = region3(96, 2, T)
    rbc = region(104, T)
    acc_early = region3(108, 2, HALF)
    gy = region3(128, CT, T)
    xc, rgate, igate, th = (region(112 + 4 * n, T) for n in range(4))
    early_row = th
    k_nat, states = region3(32, 2, T), region3(40, 2, T)
    diag = region3(176, 2, T)
    wo_hi, wo_lo = halves("wo_hi", 48, 2 * KD, HALF), ring_lo
    s_hi, s_lo = halves("s_hi", 40, 2, D), halves("s_lo", 88, 2, D)
    modbc = region(128, 4 * T).rearrange("p (a b) -> p a b", a=4)
    x1 = region(96, NT * T).rearrange("p (a b) -> p a b", a=NT)
    xtile = region3(176, 2, T)
    h2 = region3(32, 2, T)
    h2T = region3(80, 2, T)
    x_ring = region3(176, 2, D)
    w_hi, w_lo = halves("w_hi", 144, 4, D), halves("w_lo", 160, 4, D)
    x_hi, x_lo = halves("x_hi", 128, 2, D), halves("x_lo", 136, 2, D)
    y_pair = region(0, 2 * NT * D).rearrange("p (i j d) -> p i j d", i=NT, j=2)
    y_sum, o_tile = region3(160, 2, D), region3(168, 2, D)
    m_slots = [region3(kb, KD, HALF) for kb in (32, 48, 0, 16, 64, 80)]
    m_slots2 = [region3(kb, KF, D) for kb in (32, 48, 0, 16, 64, 80)]

    at = [0]
    smalls = region(184, 23 * KB)

    def small(cols, dtype=None):
        a = smalls[:, at[0]:at[0] + cols]
        at[0] += cols
        return a if dtype is None else a.bitcast(dtype)

    con = small(N_CONST)
    par = small(N_PARAM)
    msk_at = at[0]
    msk = small(MASK_BASE + 64 * len(LEVELS), I32)
    wrt = small(KD * 36).rearrange("p (a b) -> p a b", a=KD)
    bd_at = at[0]
    bd = small(2 * CT * P).rearrange("p (g c j) -> p g c j", g=2, c=CT)
    A1, SH1 = small(8), small(8)
    lb, omlb, cl = small(4), small(4), small(4)
    eps = small(1)
    cs = small(8)
    hrt = small(HEADS * 8).rearrange("p (a b) -> p a b", a=HEADS)
    tiny = small(4 * 12).rearrange("p (a b) -> p a b", a=12)
    ptot = small(HEADS * 8).rearrange("p (a b) -> p a b", a=HEADS)
    ssq = small(3 * 8).rearrange("p (a b) -> p a b", a=3)
    rst = small(3 * 8).rearrange("p (a b) -> p a b", a=3)
    acc = small(2 * 256).rearrange("p (a b) -> p a b", a=2)
    ada_at = at[0]
    ada_half = small(KD * 256).rearrange("p (a b) -> p a b", a=KD)
    osq = ada_half.rearrange("p a b -> p (a b)").rearrange("p (a b) -> p a b", a=2)
    rowt = small(2 * 256).rearrange("p (a b) -> p a b", a=2)
    assert at[0] <= 23 * KB, at[0] / KB
    scratch = region(128, 4 * T)
    m_all = scratch[:, 3 * T:3 * T + NT * NE].rearrange("p (a b) -> p a b", a=NT)
    m_pre = scratch[:, 3 * T + NT * NE:3 * T + (2 * NT + 1) * NE].rearrange("p (a b) -> p a b", a=NT + 1)
    modfix = acc.rearrange("p a b -> p (a b)").rearrange("p (a b) -> p a b", a=4)
    junk = smalls[:, bd_at:bd_at + T]
    rat = [ada_at]

    def keep(cols, dtype=None):
        a = smalls[:, rat[0]:rat[0] + cols]
        rat[0] += cols
        assert rat[0] <= at[0]
        return a if dtype is None else a.bitcast(dtype)

    wtok = keep(16).rearrange("p (j t) -> p j t", j=2)
    tbl = keep(N_BLOCKS, I32)
    ttab = keep(N_BLOCKS, I32)
    gate2 = keep(D)
    over = keep(16, I32)
    xidx, sidx = keep(2, I32), keep(2, I32)
    a_oh = smalls[:, bd_at:bd_at + 8 * P].rearrange("p (a n b) -> p a n b", a=2, n=4)
    b_oh = smalls[:, msk_at:msk_at + 8 * N_BLOCKS].rearrange("p (a n b) -> p a n b", a=2, n=4)
    keep(-rat[0] % 8)
    g_hi, g_lo = (halves(n, 184 + o / KB, 1, FE)[:, 0, :] for n, o in (("g_hi", rat[0]), ("g_lo", rat[0] + FE)))
    keep(2 * FE)
    y_sb = smalls[:, bd_at:bd_at + D]
    sil = smalls[:, msk_at:msk_at + FE]

    def C(name, rows=P):
        o, n = CONST[name]
        return con[0:rows, o:o + n]

    def PR(name, i=None):
        o, n = PARAM[name]
        return par[:, o:o + n] if i is None else par[:, o + i:o + i + 1]

    ident, ones = C("ident"), C("ones")

    def sem(name):
        return nc.alloc_semaphore(name)

    ld_par, ld_con, ld_msk, ld_wrt, ld_bd, ld_fix, ld_mod = (sem(n) for n in
        ("ld_par", "ld_con", "ld_msk", "ld_wrt", "ld_bd", "ld_fix", "ld_mod"))
    ld_x = [sem(f"ld_x{i}") for i in range(2)]
    ld_early = [sem(f"ld_early{i}") for i in range(4)]
    ld_ring = [sem(f"ld_ring{i}") for i in range(2)]
    ld_ada = sem("ld_ada")
    ld_xt = [sem(f"ld_xtile{i}") for i in range(2)]
    ld_m = [sem(f"ld_expert{i}") for i in range(6)]
    ld_g = [sem(f"ld_gather{i}") for i in range(2)]
    (bd_zero, cs_ready, sq_ready, sq_summed, rms_ready, xs_ready, acc_ready, modc_ready, a1_ready, h_ready,
     proj_done, evac_done, conv_done, gate_mm, gates_ready, sqrt_in, sqrt_out, scan_done, gmul_done, rgsq_ready,
     rgsq_summed, rgrms_ready, ob_ready, row_mm, row_ready, row_sent, p_zero, prep_done, step_mm, merged, updated,
     kt_mm, kt_ready, ds_mm, st_ready, o_mm, osq_ready, os_mm, hsd_ready, osb_ready, gzo_ready, diag_ready, bc_mm, k_updated, fk_ready, hhi_ready, hlo_ready, whi_ready, wlo_ready, restored, wohi_ready, wolo_ready, shi_ready, slo_ready, erow_mm, erow_ready, oa_ready, fix_ready, fix_sent,
     mix_mm, ss_ready, sd_ready, x1_ready, h2_ready, h2_sent, h2t_mm, h2t_ready, logit_mm,
     lg_ready, ex_ready, mm_ready, rank_mm, ab_ready, tab_mm, route_ready, dve_chain, act_chain, pool_chain,
     lbin_ready, lbexp_ready) = (sem(n) for n in
        ("bd_zero cs_ready sq_ready sq_summed rms_ready xs_ready acc_ready modc_ready a1_ready h_ready "
         "proj_done evac_done conv_done gate_mm gates_ready sqrt_in sqrt_out scan_done gmul_done rgsq_ready "
         "rgsq_summed rgrms_ready ob_ready row_mm row_ready row_sent p_zero prep_done step_mm merged updated "
         "kt_mm kt_ready ds_mm st_ready o_mm osq_ready os_mm hsd_ready osb_ready gzo_ready diag_ready bc_mm k_updated fk_ready hhi_ready hlo_ready whi_ready wlo_ready restored wohi_ready wolo_ready shi_ready slo_ready erow_mm erow_ready oa_ready fix_ready fix_sent "
         "mix_mm ss_ready sd_ready x1_ready h2_ready h2_sent h2t_mm h2t_ready logit_mm "
         "lg_ready ex_ready mm_ready rank_mm ab_ready tab_mm route_ready dve_chain act_chain pool_chain "
         "lbin_ready lbexp_ready").split())
    (xg_tr, xt_ready, sil_ready, g_ready, g_tr, ghi_ready, glo_ready, y_act, y_dve, hi_ready, lo_ready, w_used, xlo_ready, x_clear) = (sem(n) for n in
        "xg_tr xt_ready sil_ready g_ready g_tr ghi_ready glo_ready y_act y_dve hi_ready lo_ready w_used xlo_ready x_clear".split())
    y_sent = [sem(f"y_sent{i}") for i in range(2)]
    xidx_ready, sidx_ready = sem("xidx_ready"), sem("sidx_ready")
    (ld_ov, ov_x, ov_xtr, ov_hi, ov_lo, ov_used, ov_xhi, ov_xlo, ov_sil, ov_g, ov_gtr, ov_ghi, ov_glo,
     ov_ysb, ov_sent) = (sem(n) for n in
        "ld_ov ov_x ov_xtr ov_hi ov_lo ov_used ov_xhi ov_xlo ov_sil ov_g ov_gtr ov_ghi ov_glo ov_ysb ov_sent".split())
    ld_y = [sem(f"ld_y{i}") for i in range(NT)]
    fin_a, fin_b, fin_s, fin_g, fin_o = (sem(n) for n in "fin_a fin_b fin_s fin_g fin_o".split())
    o_sent = [sem(f"o_sent{i}") for i in range(2)]
    ada_v = w_ada.rearrange("(k p) c -> p k c", p=P)
    win_v = w_in.rearrange("(k p) c -> p k c", p=P)
    wout_v = w_out.rearrange("(k p) c -> p k c", p=P)
    xt_v = x_t.rearrange("(k p) t -> p k t", p=P)
    w1_v = w1.rearrange("e (k p) c -> e p k c", p=P)
    w3_v = w3.rearrange("e (k p) c -> e p k c", p=P)
    w2_v = w2.rearrange("e (k p) c -> e p k c", p=P)

    def chain_of(eng, s):
        count = [0]

        def link(ins):
            count[0] += 1
            ins.then_inc(s, 1)
            eng.wait_ge(s, count[0])
        return link

    passed = sem("passed")

    def stand(eng, s, value):
        eng.wait_ge(s, value)
        eng.sem_inc(passed, 1)

    def quarter(piece, r):
        return piece.rearrange("p a b -> p (a b)")[:, r * D:(r + 1) * D]

    def pairs(buf, m):
        return buf.rearrange("p (b two m) -> p b two m", two=2, m=m)

    def block_products(h, m):
        if m == 1:
            return fbuf[:, h, :]
        if m == 2:
            return t2buf[:, h, :]
        if m == P:
            return ptot[:, h, :]
        o = 512 - 1024 // m * 2
        return fbuf[:, h, o:o + T // m]

    def h_lo(k):
        return (h_lo_a, h_lo_b)[k // 4][:, k % 4, :]

    def h_full(k):
        return (fbuf, kbuf)[k // 4][:, k % 4, :]

    def before(s):
        _, m, h = s
        return LEVEL_ORDER[("level", m // 2, h) if m > 2 else ("base", h)] + 1

    def sums_bank(h):
        return 6 if h < 2 else h

    def level_bank(s):
        n = LEVEL_ORDER[s]
        return 4 + 2 * (n % 2), max(n - 1, 0)

    block_cm = nc.Block()
    with block_cm as block:

        @block.sync
        def _(sp):
            sp.dma_start(par, params).then_inc(ld_par, 16)
            for i in range(2):
                sp.dma_start(hT[:, 4 * i:4 * i + 4, :], xt_v[:, 4 * i:4 * i + 4, :]).then_inc(ld_x[i], 16)
            sp.dma_start(con, consts).then_inc(ld_con, 16)
            for n in range(4):
                sp.dma_start(early[n], ada_v[:, :, n * HALF:(n + 1) * HALF]).then_inc(ld_early[n], 16)
            for n in range(2):
                c = PIECE_COL[PIECES[n]]
                sp.dma_start(ring[n], win_v[:, :, c:c + HALF]).then_inc(ld_ring[n], 16)
            sp.wait_ge(bd_zero, 1)
            for g, w in enumerate((w_r, w_i)):
                wv = w.rearrange("(c two) i j -> two i c j", two=2)
                for two in range(2):
                    sp.dma_start(bd[64 * two:64 * two + 64, g, :, 64 * two:64 * two + 64], wv[two]).then_inc(ld_bd, 16)
            sp.dma_start(msk, masks).then_inc(ld_msk, 16)
            sp.dma_start(wrt, w_route).then_inc(ld_wrt, 16)
            for n in range(2, 8):
                last = (PIECES[n - 2], 7, 0) if PIECES[n - 2] == "iv" else (PIECES[n - 2], 3, 1)
                sp.wait_ge(proj_done, GROUPS[last] + 1)
                if n < 6:
                    c = PIECE_COL[PIECES[n]]
                    src = win_v[:, :, c:c + HALF]
                else:
                    src = wout_v[:, :, (n - 6) * HALF:(n - 5) * HALF]
                sp.dma_start(ring[n % 2], src).then_inc(ld_ring[n % 2], 16)
            sp.wait_ge(row_sent, 16 * 16)
            sp.dma_start(modfix[0:32, 0, :], mod_raw.rearrange("a (b c) -> (a b) c", c=P)).then_inc(ld_fix, 16)
            sp.dma_start(modfix[0:32, 1:4, :], mod_rows).then_inc(ld_fix, 16)
            sp.wait_ge(fix_ready, 1)
            sp.dma_start(mod_done.rearrange("a (b c) -> (a b) c", c=P), modfix[0:32, 0, :]).then_inc(fix_sent, 16)
            sp.wait_ge(fix_sent, 16)
            sp.wait_ge(o_mm, HEADS)
            sp.wait_ge(os_mm, HEADS)
            sp.dma_start(modbc, mod_done.rearrange("a b -> (a b)").partition_broadcast(P)
                         .rearrange("p (a b) -> p a b", a=4)).then_inc(ld_mod, 16)
            sp.dma_start(gate2, mod_done[6:8, :].rearrange("a b -> (a b)").partition_broadcast(P)).then_inc(ld_mod, 16)
            sp.wait_ge(bc_mm, HEADS)
            for i in range(NT):
                if i >= 2:
                    sp.wait_ge(x1_ready, i - 1)
                sp.dma_start(xtile[:, i % 2, :], x[i * P:(i + 1) * P, :]).then_inc(ld_xt[i % 2], 16)
            sp.wait_ge(mix_mm, NT)
            sp.dma_start(m_slots[1], w3_v[0]).then_inc(ld_m[1], 16)
            sp.dma_start(m_slots[2], w1_v[1]).then_inc(ld_m[2], 16)
            sp.wait_ge(h2_sent, 16 * NT)
            sp.wait_ge(h2t_mm, NT)
            sp.dma_start(m_slots[0], w1_v[0]).then_inc(ld_m[0], 16)
            sp.dma_start(m_slots2[4], w2_v[0]).then_inc(ld_m[4], 16)
            sp.dma_start(m_slots[3], w3_v[1]).then_inc(ld_m[3], 16)
            sp.wait_ge(logit_mm, NT)
            sp.dma_start(m_slots[5], w1_v[2]).then_inc(ld_m[5], 16)
            sp.wait_ge(lo_ready, 4)
            sp.dma_start(m_slots[0], w3_v[2]).then_inc(ld_m[0], 16)
            sp.wait_ge(lo_ready, 8)
            sp.dma_start(m_slots2[1], w2_v[1]).then_inc(ld_m[1], 16)
            with sp.Fori(0, (NE - 4) // 2) as i:
                for odd in range(2):
                    b = 2 * i + (3 + odd)
                    s1, s3, s2 = (2, 3, 4) if odd == 0 else (5, 0, 1)
                    q = 24 * i + 12 * (1 + odd)
                    sp.wait_ge(lo_ready, q)
                    sp.dma_start(m_slots[s1], w1_v[b]).then_inc(ld_m[s1], 16)
                    sp.wait_ge(lo_ready, q + 4)
                    sp.dma_start(m_slots[s3], w3_v[b]).then_inc(ld_m[s3], 16)
                    sp.wait_ge(lo_ready, q + 8)
                    sp.dma_start(m_slots2[s2], w2_v[b - 1]).then_inc(ld_m[s2], 16)
            b = NE - 1
            q = 12 * (b - 2)
            sp.wait_ge(lo_ready, q)
            sp.dma_start(m_slots[2], w1_v[b]).then_inc(ld_m[2], 16)
            sp.wait_ge(lo_ready, q + 4)
            sp.dma_start(m_slots[3], w3_v[b]).then_inc(ld_m[3], 16)
            sp.wait_ge(lo_ready, q + 8)
            sp.dma_start(m_slots2[4], w2_v[b - 1]).then_inc(ld_m[4], 16)
            sp.wait_ge(lo_ready, q + 12)
            sp.dma_start(m_slots2[5], w2_v[b]).then_inc(ld_m[5], 16)
            n_over = sp.value_load(over[0:1, 15:16], min_val=0, max_val=N_OVER)
            sp.wait_ge(lo_ready, 12 * NE)
            with sp.If(n_over > 0):
                with sp.Fori(0, N_OVER) as o:
                    with sp.If(o < n_over):
                        e = sp.value_load(over[0:1, bass.ds(o, 1)], min_val=0, max_val=NE - 1)
                        sp.dma_start(m_slots[0], w1_v[bass.ds(e, 1)].rearrange("a p k c -> (a p) k c")).then_inc(ld_ov, 16)
                        sp.dma_start(m_slots[1], w3_v[bass.ds(e, 1)].rearrange("a p k c -> (a p) k c")).then_inc(ld_ov, 16)
                        sp.dma_start(m_slots2[2], w2_v[bass.ds(e, 1)].rearrange("a p k c -> (a p) k c")).then_inc(ld_ov, 16)
                        stand(sp, ov_sent, 16 * (o + 1))
            for q in range(2):
                sp.wait_ge(y_sent[q], 8 * NE)
            for i in range(NT):
                sp.dma_start(y_pair[:, i, :, :], y_rows.rearrange("(j t) d -> t j d", j=2)[i * P:(i + 1) * P]).then_inc(ld_y[i], 16)
            for i in range(NT):
                sp.wait_ge(fin_o, i + 1)
                sp.dma_start(out[i * P:(i + 1) * P, :], o_tile[:, i % 2, :]).then_inc(o_sent[i % 2], 16)
            for i in range(2):
                sp.wait_ge(o_sent[i], 16 * NT // 2)

        @block.gpsimd
        def _(pool):
            link = chain_of(pool, pool_chain)
            link(pool.memset(eps, EPS))
            pool.memset(bd.rearrange("p g c j -> p (g c j)"), 0.0).then_inc(bd_zero, 1)
            for u in range(16):
                if u:
                    pool.wait_ge(acc_ready, 2 + u)
                c = 4 * HALF + u * 256
                pool.dma_start(ada_half, ada_v[:, :, c:c + 256]).then_inc(ld_ada, 16)
            pool.wait_ge(proj_done, GROUPS[(SPLIT[-1], HEADS - 1, 1)] + 1)
            pool.memset(pbuf.rearrange("p a b -> p (a b)"), 0.0).then_inc(p_zero, 1)
            for n, step in enumerate(LEVEL_ORDER):
                h = step[-1]
                if step[0] == "base":
                    pool.wait_ge(prep_done, h + 1)
                    pool.wait_ge(step_mm, n + 1)
                    k2, f2 = (b[:, h, :].rearrange("p (b two) -> p b two", two=2) for b in (kbuf, fbuf))
                    pool.tensor_tensor(k2, k2, f2[:, :, 1:2].to_broadcast([P, T // 2, 2]), ALU.mult).then_inc(k_updated, 1)
                else:
                    m = step[1]
                    pool.wait_ge(updated, before(step))
                    pool.wait_ge(k_updated, before(step))
                    pool.wait_ge(step_mm, n + 1)
                    tm = block_products(h, m).rearrange("p (b two) -> p b two", two=2)
                    ke = pairs(kbuf[:, h, :], m)[:, :, 0, :]
                    pool.tensor_tensor(ke, ke, tm[:, :, 1:2].to_broadcast([P, T // (2 * m), m]), ALU.mult).then_inc(k_updated, 1)
            for i in range(NT):
                pool.wait_ge(h2_ready, i + 1)
                pool.dma_start(h2_rows[i * P:(i + 1) * P, :], h2[:, i % 2, :]).then_inc(h2_sent, 16)
                pool.wait_ge(h2_sent, 16 * (i + 1))
            pool.wait_ge(x1_ready, NT)
            pool.memset(x_ring.rearrange("p a b -> p (a b)"), 0.0).then_inc(x_clear, 1)
            pool.wait_ge(x_clear, 1)
            pool.wait_ge(route_ready, 1)

            def gather(idx, dst, s):
                pool.indirect_dma_start(dst, None, h2_rows, bass.IndirectOffsetOnAxis(ap=idx, axis=0),
                                        bounds_check=T - 1, oob_is_err=False).then_inc(s, 16)

            def scatter(idx, s):
                pool.indirect_dma_start(y_rows, bass.IndirectOffsetOnAxis(ap=idx, axis=0), y_sb, None,
                                        bounds_check=2 * T - 1, oob_is_err=False).then_inc(s, 16)

            def gather_block(b, q, ring_used=True):
                if ring_used:
                    pool.wait_ge(xg_tr, b - 1)
                pool.tensor_copy(xidx[:, q:q + 1], ttab[:, bass.ds(b, 1)]).then_inc(xidx_ready, 1)
                stand(pool, xidx_ready, b + 1)
                gather(xidx[:, q:q + 1], x_ring[:, q, :], ld_g[q])

            def scatter_block(b, q):
                pool.wait_ge(y_act, b + 1)
                pool.wait_ge(y_dve, b + 1)
                pool.tensor_copy(sidx[:, q:q + 1], tbl[:, bass.ds(b, 1)]).then_inc(sidx_ready, 1)
                stand(pool, sidx_ready, b + 1)
                scatter(sidx[:, q:q + 1], y_sent[q])

            gather_block(0, 0, ring_used=False)
            gather_block(1, 1, ring_used=False)
            gather_block(2, 0)
            with pool.Fori(0, (NE - 4) // 2) as i:
                for odd in range(2):
                    gather_block(2 * i + (3 + odd), 1 - odd)
                    scatter_block(2 * i + odd, odd)
            gather_block(NE - 1, 1)
            for b in range(NE - 4, NE):
                scatter_block(b, b % 2)
            for q in range(2):
                pool.wait_ge(y_sent[q], 8 * NE)
            n_over = pool.value_load(over[0:1, 15:16], min_val=0, max_val=N_OVER)
            with pool.If(n_over > 0):
                with pool.Fori(0, N_OVER) as o:
                    with pool.If(o < n_over):
                        pool.tensor_copy(sidx[:, 0:1], tbl[:, bass.ds(o + NE, 1)])
                        pool.tensor_copy(xidx[:, 0:1], ttab[:, bass.ds(o + NE, 1)]).then_inc(xidx_ready, 1)
                        stand(pool, xidx_ready, o + (NE + 1))
                        gather(xidx[:, 0:1], x_ring[:, 0, :], ov_x)
                        stand(pool, ov_ysb, o + 1)
                        scatter(sidx[:, 0:1], ov_sent)
                        stand(pool, ov_sent, 16 * (o + 1))

        @block.scalar
        def _(act):
            link = chain_of(act, act_chain)
            act.wait_ge(ld_par, 16)
            act.activation(cs, PR("c"), ACT.Silu).then_inc(cs_ready, 1)
            act.wait_ge(lbin_ready, 1)
            act.activation(tiny[:, 0:3, :], tiny[:, 0:3, :], ACT.Exp).then_inc(lbexp_ready, 1)
            for k in range(KD):
                act.wait_ge(ld_x[k // 4], 16)
                if k >= 2:
                    act.wait_ge(sq_summed, k - 1)
                act.activation(sq[:, k % 2, :], hT[:, k, :], ACT.Square).then_inc(sq_ready, 1)
            act.wait_ge(pool_chain, 1)
            act.wait_ge(sq_summed, KD)
            act.activation(rbc, ps[:, 0:2, :].rearrange("p a b -> p (a b)"), ACT.Sqrt, bias=eps, scale=1.0 / D).then_inc(rms_ready, 1)
            def split_high(name, r):
                n = SPLIT.index(name)
                if r == 0:
                    act.wait_ge(ld_ring[n % 2], 16 * (n // 2 + 1))
                    if name == "xr":
                        act.wait_ge(acc_ready, 2)
                    elif name == "q":
                        act.wait_ge(proj_done, GROUPS[("yr", CT - 1, 1)] + 1)
                    elif name == "iv":
                        act.wait_ge(ob_ready, CT)
                    elif name == "gz":
                        act.wait_ge(proj_done, GROUPS[("iv", NT - 1, 0)] + 1)
                act.activation(win_hi[name][:, 2 * r:2 * r + 2, :], ring[n % 2][:, 2 * r:2 * r + 2, :], ACT.Copy).then_inc(whi_ready, 1)

            for n in range(2):
                act.wait_ge(erow_mm, n + 1)
                act.activation(early_row[0:1, n * HALF:(n + 1) * HALF], ps[0:1, 3 + n, :], ACT.Copy).then_inc(erow_ready, 1)
                if n == 0:
                    for r in range(4):
                        split_high("xr", r)
            act.wait_ge(a1_ready, 1)
            for k in range(KD):
                act.wait_ge(xs_ready, KD)
                act.activation(h_full(k), hT[:, k, :], ACT.Identity, bias=SH1[:, k:k + 1], scale=A1[:, k:k + 1]).then_inc(h_ready, 1)
                act.wait_ge(h_ready, k + 1)
                act.activation(h_hi[:, k, :], h_full(k), ACT.Copy).then_inc(hhi_ready, 1)
            def k_out(h):
                act.wait_ge(kt_mm, h + 1)
                if h >= 2:
                    act.wait_ge(ds_mm, h - 1)
                act.activation(k_nat[:, h % 2, :], ps[:, 0:2, :].rearrange("p a b -> p (a b)"), ACT.Copy).then_inc(kt_ready, 1)

            def wo_high(n):
                act.activation(wo_hi[:, 2 * n:2 * n + 2, :], ring[n // 4][:, 2 * (n % 4):2 * (n % 4) + 2, :], ACT.Copy).then_inc(wohi_ready, 1)

            def wo_first():
                act.wait_ge(ld_ring[0], 16 * 4)
                act.wait_ge(proj_done, len(GROUPS))
                for n in range(4):
                    wo_high(n)

            act.wait_ge(ld_bd, 64)
            for step in STEPS:
                kind = step[0]
                if kind == "proj":
                    _, name, a, half = step
                    g = GROUPS[step[1:]]
                    src = ps[:, g % 3, :]
                    cols = slice(half * HALF, (half + 1) * HALF)
                    act.wait_ge(proj_done, g + 1)
                    if name == "xr":
                        ins = act.activation(rgbuf[:, a, cols], src, ACT.Copy)
                    elif name == "yr":
                        act.wait_ge(a1_ready, 1)
                        ins = act.activation(gy[:, a, cols], src, ACT.Gelu_apprx_tanh)
                    elif name == "q":
                        ins = act.activation(qbuf[:, a, cols], src, ACT.Silu)
                    elif name == "f":
                        act.activation(fbuf[:, a, cols], src, ACT.Sigmoid)
                        ins = act.activation(kbuf[:, a, cols], src, ACT.Sigmoid, scale=-1.0)
                    elif name == "iv":
                        if a == 0:
                            act.wait_ge(gmul_done, CT)
                        ins = act.activation(vbuf[:, a, :], src, ACT.Copy)
                    else:
                        ins = act.activation(gzbuf[:, a, cols], src, ACT.Silu)
                    ins.then_inc(evac_done, 1)
                elif kind == "split":
                    split_high(*step[1:])
                elif kind == "prep":
                    h = step[1]
                    act.wait_ge(evac_done, GROUPS[("f", h, 1)] + 1)
                    act.activation(kbuf[:, h, :], kbuf[:, h, :], ACT.Copy, scale=omlb[:, h:h + 1]).then_inc(fk_ready, 1)
                    act.activation(fbuf[:, h, :], fbuf[:, h, :], ACT.Identity, bias=lb[:, h:h + 1], scale=omlb[:, h:h + 1]).then_inc(fk_ready, 1)
                elif kind == "head":
                    if step[1] == 0:
                        wo_first()
                    k_out(step[1])
                elif kind == "gate":
                    ct = step[1]
                    act.wait_ge(gate_mm, ct + 1)
                    if ct:
                        act.wait_ge(scan_done, ct)
                    act.activation(rgate, ps[:, 4:6, :].rearrange("p a b -> p (a b)"), ACT.Sigmoid, bias=PR("br", ct)).then_inc(gates_ready, 1)
                    act.activation(igate, ps[:, 6:8, :].rearrange("p a b -> p (a b)"), ACT.Sigmoid, bias=PR("bi", ct)).then_inc(gates_ready, 1)
                    act.wait_ge(gates_ready, 4 * ct + 1)
                    act.activation(th, rgate, ACT.Tanh, scale=cl[:, ct:ct + 1]).then_inc(gates_ready, 1)
                    act.wait_ge(gates_ready, 4 * ct + 3)
                    act.activation(rgate, rgate, ACT.Exp, scale=cl[:, ct:ct + 1]).then_inc(gates_ready, 1)
                elif kind == "scan":
                    ct = step[1]
                    act.wait_ge(sqrt_in, ct + 1)
                    act.activation(xc, xc, ACT.Sqrt, scale=-1.0).then_inc(sqrt_out, 1)
                elif kind == "rg_norm":
                    act.wait_ge(scan_done, CT)
                    for ct in range(CT):
                        act.wait_ge(gmul_done, ct + 1)
                        if ct >= 2:
                            act.wait_ge(rgsq_summed, ct - 1)
                        act.activation((xc, rgate)[ct % 2], rgbuf[:, ct, :], ACT.Square).then_inc(rgsq_ready, 1)
                    act.wait_ge(rgsq_summed, CT)
                    act.activation(igate, ps[:, 4:6, :].rearrange("p a b -> p (a b)"), ACT.Sqrt, bias=eps, scale=1.0 / CH).then_inc(rgrms_ready, 1)
                elif kind == "row":
                    u = step[1]
                    act.wait_ge(row_mm, u + 1)
                    if u >= 2:
                        act.wait_ge(row_sent, 16 * (u - 1))
                    act.activation(rowt[0:1, u % 2, :], ps[0:1, 3, (u % 2) * 256:(u % 2) * 256 + 256], ACT.Copy).then_inc(row_ready, 1)
                    act.wait_ge(row_ready, u + 1)
                    if u:
                        act.wait_ge(row_sent, 16 * u)
                    act.dma_start(mod_raw[u // 2:u // 2 + 1, (u % 2) * 256:(u % 2) * 256 + 256], rowt[0:1, u % 2, :]).then_inc(row_sent, 16)
            def o_out(h):
                o_ = ps[:, 4:6, :].rearrange("p a b -> p (a b)")
                act.wait_ge(o_mm, h + 1)
                if h >= 2:
                    act.wait_ge(os_mm, h - 1)
                act.activation(osq[:, h % 2, :], o_, ACT.Square).then_inc(osq_ready, 1)
                act.activation(kbuf[:, h, :], o_, ACT.Copy, scale=PR("hg", h)).then_inc(osb_ready, 1)

            def head_root(h):
                act.wait_ge(os_mm, h + 1)
                act.activation(hrt[:, h, :], ps[:, sums_bank(h), 0:NCHUNK], ACT.Sqrt, bias=eps, scale=1.0 / P).then_inc(hsd_ready, 1)

            for h in range(HEADS):
                o_out(h)
                if h + 2 < HEADS:
                    k_out(h + 2)
                if h == 0:
                    act.wait_ge(ld_ring[1], 16 * 4)
                if h < 2:
                    wo_high(4 + 2 * h)
                head_root(h)
                if h < 2:
                    wo_high(5 + 2 * h)

            def s_high(i):
                for part, src in enumerate((rgbuf, gzbuf)):
                    if i == 0:
                        act.wait_ge((ob_ready, oa_ready)[part], 4)
                    act.activation(s_hi[:, i % 2, part * CH:(part + 1) * CH].rearrange("p (a b) -> p a b", a=CT),
                                   src[:, :, i * P:(i + 1) * P], ACT.Copy).then_inc(shi_ready, 1)

            s_high(0)
            s_high(1)
            def h2_out(i):
                act.wait_ge(h2t_mm, i + 1)
                if i >= 2:
                    act.wait_ge(logit_mm, i - 1)
                act.activation(h2T[:, i % 2, :], ps[:, 4:6, :].rearrange("p a b -> p (a b)"), ACT.Copy).then_inc(h2t_ready, 1)

            for i in range(NT):
                act.wait_ge(mix_mm, i + 1)
                if i + 2 < NT:
                    s_high(i + 2)
                link(act.activation(junk, ps[:, 2 * (i % 2):2 * (i % 2) + 2, :].rearrange("p a b -> p (a b)"), ACT.Square, accum_out=ssq[:, 0, i:i + 1]))
                act.activation(ssq[:, 0, i:i + 1], ssq[:, 0, i:i + 1], ACT.Sqrt, bias=eps, scale=1.0 / D).then_inc(ss_ready, 1)
                if i:
                    h2_out(i - 1)
                act.wait_ge(x1_ready, i + 1)
                link(act.activation(junk, x1[:, i, :], ACT.Square, accum_out=ssq[:, 1, i:i + 1]))
                act.activation(ssq[:, 1, i:i + 1], ssq[:, 1, i:i + 1], ACT.Sqrt, bias=eps, scale=1.0 / D).then_inc(sd_ready, 1)
            h2_out(NT - 1)
            act.wait_ge(lg_ready, 1)
            lg = scratch[:, 0:NT * 36]
            act.activation(lg, lg, ACT.Exp).then_inc(ex_ready, 1)

            def x_out(b, q):
                act.wait_ge(xg_tr, b + 1)
                act.activation(x_hi[:, q, :], ps[:, 6:8, :].rearrange("p a b -> p (a b)"), ACT.Copy).then_inc(xt_ready, 1)

            def w_high(n, piece, free=True):
                for r in range(4):
                    if free:
                        act.wait_ge(w_used, n + (r - 3))
                    act.activation(w_hi[:, r, :], quarter(piece, r), ACT.Copy).then_inc(hi_ready, 1)

            def silu_out(h1_done):
                act.wait_ge(w_used, h1_done)
                act.activation(sil, ps[:, 0, :], ACT.Silu).then_inc(sil_ready, 1)

            def g_out(b):
                act.wait_ge(g_tr, b + 1)
                act.activation(g_hi, ps[:, 2, :], ACT.Copy).then_inc(ghi_ready, 1)

            def y_out(y_done):
                act.wait_ge(w_used, y_done)
                act.activation(y_sb[:, 0:HALF], ps[:, 3, :], ACT.Copy).then_inc(y_act, 1)

            act.wait_ge(ld_m[0], 16)
            w_high(0, m_slots[0], free=False)
            x_out(0, 0)
            act.wait_ge(ld_m[1], 16)
            w_high(4, m_slots[1])
            silu_out(4)
            x_out(1, 1)
            act.wait_ge(ld_m[2], 16)
            w_high(8, m_slots[2])

            def block_step(b, n, q, n3, n2, n1, sent, last=False):
                s3, s2, s1 = (3, 4, 5) if q == 1 else (0, 1, 2)
                act.wait_ge(ld_m[s3], n3)
                w_high(n, m_slots[s3])
                if b is not first:
                    act.wait_ge(w_used, n - 4)
                g_out(b - 1)
                silu_out(n)
                act.wait_ge(ld_m[s2], n2)
                w_high(n + 4, m_slots2[s2])
                if not last:
                    act.wait_ge(w_used, n - (8 if b is not first else 4))
                    x_out(b + 1, 1 - q)
                act.wait_ge(ld_m[s1], n1)
                w_high(n + 8, m_slots[s1] if not last else m_slots2[s1])
                if b is not first:
                    act.wait_ge(y_sent[q], sent)
                y_out(n + 8)

            first = 1
            block_step(first, 12, 1, 16, 16, 16, 0)
            block_step(2, 24, 0, 32, 32, 32, 16)
            with act.Fori(0, (NE - 4) // 2) as i:
                block_step(2 * i + 3, 24 * i + 36, 1, 16 * i + 32, 16 * i + 32, 16 * i + 32, 16 * i + 16)
                block_step(2 * i + 4, 24 * i + 48, 0, 16 * i + 48, 16 * i + 48, 16 * i + 48, 16 * i + 32)
            b = NE - 1
            block_step(b, 12 * b, 1, 256, 256, 256, 16 * (b // 2), last=True)
            act.wait_ge(w_used, 12 * b + 8)
            g_out(b)
            act.wait_ge(y_sent[0], 8 * NE)
            y_out(12 * b + 12)
            n_over = act.value_load(over[0:1, 15:16], min_val=0, max_val=N_OVER)
            for q in range(2):
                act.wait_ge(y_sent[q], 8 * NE)
            with act.If(n_over > 0):
                with act.Fori(0, N_OVER) as o:
                    with act.If(o < n_over):
                        act.wait_ge(ov_xtr, o + 1)
                        act.activation(x_hi[:, 0, :], ps[:, 6:8, :].rearrange("p a b -> p (a b)"), ACT.Copy).then_inc(ov_xhi, 1)
                        act.wait_ge(ld_ov, 48 * (o + 1))
                        for n in range(12):
                            if n >= 4:
                                act.wait_ge(ov_used, 12 * o + (n - 3))
                            if n == 8:
                                act.wait_ge(ov_used, 12 * o + 4)
                                act.activation(sil, ps[:, 0, :], ACT.Silu).then_inc(ov_sil, 1)
                            act.activation(w_hi[:, n % 4, :], quarter((m_slots[0], m_slots[1], m_slots2[2])[n // 4], n % 4), ACT.Copy).then_inc(ov_hi, 1)
                        act.wait_ge(ov_gtr, o + 1)
                        act.activation(g_hi, ps[:, 2, :], ACT.Copy).then_inc(ov_ghi, 1)
                        act.wait_ge(ov_used, 12 * o + 12)
                        act.activation(y_sb, ps[:, 3:5, :].rearrange("p a b -> p (a b)"), ACT.Copy).then_inc(ov_ysb, 1)
                        stand(act, ov_sent, 16 * (o + 1))
            def first_row(i):
                act.wait_ge(ld_y[i], 16)
                if i >= 2:
                    act.wait_ge(fin_g, i - 1)
                act.activation(y_sum[:, i % 2, :], y_pair[:, i, 0, :], ACT.Copy, scale=wtok[:, 0, i:i + 1]).then_inc(fin_a, 1)

            first_row(0)
            for i in range(NT):
                if i + 1 < NT:
                    first_row(i + 1)
                act.wait_ge(fin_b, i + 1)
                link(act.activation(junk, y_sum[:, i % 2, :], ACT.Square, accum_out=ssq[:, 2, i:i + 1]))
                act.activation(ssq[:, 2, i:i + 1], ssq[:, 2, i:i + 1], ACT.Sqrt, bias=eps, scale=1.0 / D).then_inc(fin_s, 1)

        @block.vector
        def _(dve):
            link = chain_of(dve, dve_chain)
            dve.wait_ge(ld_par, 16)
            mx, e0, e1, ab, s0, s1, s2 = (tiny[:, n, :] for n in (3, 0, 1, 2, 4, 5, 6))
            link(dve.tensor_tensor(mx, PR("gam0"), PR("gam1"), ALU.max))
            dve.tensor_tensor(e0, PR("gam0"), mx, ALU.subtract)
            dve.tensor_tensor(e1, PR("gam1"), mx, ALU.subtract)
            link(dve.tensor_scalar(s0, PR("lam"), -1.0, None, ALU.mult))
            dve.tensor_tensor(ab, PR("lam"), s0, ALU.min).then_inc(lbin_ready, 1)
            dve.wait_ge(lbexp_ready, 1)
            link(dve.tensor_tensor(s0, e0, e1, ALU.add))
            link(dve.reciprocal(s1, s0))
            dve.tensor_tensor(lb, e0, s1, ALU.mult)
            dve.tensor_tensor(omlb, e1, s1, ALU.mult)
            link(dve.tensor_scalar(s0, ab, 2.0, None, ALU.add))
            link(dve.reciprocal(s0, s0))
            link(dve.tensor_tensor(s0, ab, s0, ALU.mult))
            link(dve.tensor_tensor(s1, s0, s0, ALU.mult))
            link(dve.memset(s2, 1.0 / 19.0))
            for n in range(17, 0, -2):
                link(dve.tensor_tensor(s2, s2, s1, ALU.mult))
                link(dve.tensor_scalar(s2, s2, 1.0 / n, None, ALU.add))
            link(dve.tensor_tensor(s2, s2, s0, ALU.mult))
            link(dve.tensor_scalar(s1, PR("lam"), 0.0, 8.0, ALU.min, ALU.mult))
            link(dve.scalar_tensor_tensor(cl, s2, -16.0, s1, ALU.mult, ALU.add))

            def ada_acc(dst, src, n):
                link(dve.tensor_scalar(dst, src[:, 0, :], cs[:, 0:1], None, ALU.mult))
                for k in range(1, KD):
                    ins = dve.scalar_tensor_tensor(dst, src[:, k, :], cs[:, k:k + 1], dst, ALU.mult, ALU.add)
                    if k < KD - 1:
                        link(ins)
                ins.then_inc(acc_ready, 1)

            dve.wait_ge(cs_ready, 1)
            for n in range(2):
                dve.wait_ge(ld_early[n], 16)
                ada_acc(acc_early[:, n, :], early[n], n)
            dve.wait_ge(rms_ready, 1)
            link(dve.reciprocal(rbc, rbc))
            for k in range(KD):
                dve.tensor_tensor(hT[:, k, :], hT[:, k, :], rbc, ALU.mult).then_inc(xs_ready, 1)
            dve.wait_ge(modc_ready, 4)
            o = PARAM["b_ada"][0]
            dve.tensor_tensor(SH1, ps[:, 2, 0:8], par[:, o:o + 8], ALU.add)
            link(dve.tensor_tensor(A1, ps[:, 2, 8:16], par[:, o + 8:o + 16], ALU.add))
            dve.scalar_tensor_tensor(A1, A1, 1.0, PR("g_pre"), ALU.add, ALU.mult).then_inc(a1_ready, 1)

            def state_chain(h):
                dve.wait_ge(ds_mm, h + 1)
                if h >= 2:
                    dve.wait_ge(o_mm, h - 1)
                dve.wait_ge(updated, LEVEL_ORDER[("level", LEVELS[-1], h)] + 1)
                st = states[:, h % 2, :].rearrange("p (c v) -> p c v", v=P)
                ds = ps[:, 2:4, :].rearrange("p a b -> p (a b)").rearrange("p (c v) -> p c v", v=P)
                ins = dve.tensor_copy(st[:, 1, :], ds[:, 0, :])
                for c in range(1, NCHUNK - 1):
                    link(ins)
                    ins = dve.scalar_tensor_tensor(st[:, c + 1, :], st[:, c, :], ptot[:, h, c:c + 1], ds[:, c, :], ALU.mult, ALU.add)
                ins.then_inc(st_ready, 1)

            def split_low(name, r):
                n = SPLIT.index(name)
                dve.wait_ge(whi_ready, 4 * n + r + 1)
                dve.tensor_tensor(ring_lo[:, KD * (n % 2) + 2 * r:KD * (n % 2) + 2 * r + 2, :], ring[n % 2][:, 2 * r:2 * r + 2, :],
                                  win_hi[name][:, 2 * r:2 * r + 2, :].bitcast(F32), ALU.subtract).then_inc(wlo_ready, 1)

            for k in range(KD):
                if k % 2 == 0:
                    split_low("xr", k // 2)
                dve.wait_ge(hhi_ready, k + 1)
                dve.tensor_tensor(h_lo(k), h_full(k), h_hi[:, k, :].bitcast(F32), ALU.subtract).then_inc(hlo_ready, 1)
            for step in STEPS:
                kind = step[0]
                if kind == "split":
                    split_low(*step[1:])
                elif kind == "restore":
                    dve.wait_ge(proj_done, GROUPS[(SPLIT[-1], HEADS - 1, 1)] + 1)
                    for k in range(KD):
                        dve.tensor_tensor(hT[:, k, :], h_hi[:, k, :].bitcast(F32), h_lo(k).bitcast(F32), ALU.add).then_inc(restored, 1)
                elif kind == "head":
                    state_chain(step[1])
                elif kind == "conv":
                    ct = step[1]
                    dve.wait_ge(evac_done, GROUPS[("xr", ct, 1)] + 1)
                    if ct:
                        dve.wait_ge(scan_done, ct)
                    link(dve.tensor_scalar(xc, rgbuf[:, ct, :], PR("cw3", ct), PR("cb", ct), ALU.mult, ALU.add))
                    for j in range(1, 4):
                        ins = dve.scalar_tensor_tensor(xc[:, j:T], rgbuf[:, ct, 0:T - j], PR(f"cw{3 - j}", ct), xc[:, j:T], ALU.mult, ALU.add)
                        if j < 3:
                            link(ins)
                    ins.then_inc(conv_done, 1)
                elif kind == "gate":
                    ct = step[1]
                    dve.wait_ge(gates_ready, 4 * ct + 4)
                    dve.wait_ge(gate_mm, ct + 1)
                    link(dve.tensor_tensor(igate, igate, xc, ALU.mult))
                    link(dve.tensor_tensor(xc, rgate, rgate, ALU.mult))
                    dve.scalar_tensor_tensor(xc, xc, 1.0, th, ALU.add, ALU.mult).then_inc(sqrt_in, 1)
                    dve.wait_ge(sqrt_out, ct + 1)
                    link(dve.tensor_tensor(igate, igate, xc, ALU.mult))
                    dve.tensor_tensor_scan(rgbuf[:, ct, :], rgate, igate, 0.0, ALU.mult, ALU.add).then_inc(scan_done, 1)
                elif kind == "gelu_mul":
                    ct = step[1]
                    dve.wait_ge(evac_done, GROUPS[("yr", ct, 1)] + 1)
                    dve.wait_ge(scan_done, ct + 1)
                    dve.tensor_tensor(rgbuf[:, ct, :], rgbuf[:, ct, :], gy[:, ct, :], ALU.mult).then_inc(gmul_done, 1)
                elif kind == "ada":
                    u = step[1]
                    dve.wait_ge(ld_ada, 16 * (u + 1))
                    if u >= 2:
                        dve.wait_ge(row_mm, u - 1)
                    ada_acc(acc[:, u % 2, :], ada_half, u)
                elif kind == "rg_norm":
                    dve.wait_ge(rgrms_ready, 1)
                    link(dve.reciprocal(igate, igate))
                    for ct in range(CT):
                        dve.scalar_tensor_tensor(rgbuf[:, ct, :], rgbuf[:, ct, :], PR("rgg", ct), igate, ALU.mult, ALU.mult).then_inc(ob_ready, 1)
                elif kind == "prep":
                    h = step[1]
                    dve.wait_ge(fk_ready, 2 * h + 2)
                    fo = pairs(fbuf[:, h, :], 1)[:, :, 1, :]
                    qo, ko = pairs(qbuf[:, h, :], 1)[:, :, 1, :], pairs(kbuf[:, h, :], 1)[:, :, 1, :]
                    rec = t2buf[:, h, :].unsqueeze(2)
                    dve.tensor_tensor(qo, qo, fo, ALU.mult)
                    link(dve.reciprocal(rec, fo))
                    dve.tensor_tensor(ko, ko, rec, ALU.mult).then_inc(prep_done, 1)
                elif kind == "base":
                    h = step[1]
                    n = LEVEL_ORDER[step]
                    bank, _ = level_bank(step)
                    dve.wait_ge(step_mm, n + 1)
                    if h == 0:
                        dve.wait_ge(p_zero, 1)
                        dve.wait_ge(ld_msk, 16)
                    v3 = lambda a: a.rearrange("p (c t) -> p c t", t=P)
                    dve.copy_predicated(v3(pbuf[:, h, :]), msk[:, 0:P].unsqueeze(1).to_broadcast([P, NCHUNK, P]),
                                        v3(ps[:, bank:bank + 2, :].rearrange("p a b -> p (a b)"))).then_inc(merged, 1)
                    q2, f2 = (b[:, h, :].rearrange("p (b two) -> p b two", two=2) for b in (qbuf, fbuf))
                    dve.tensor_tensor(q2, q2, f2[:, :, 0:1].to_broadcast([P, T // 2, 2]), ALU.mult)
                    dve.tensor_tensor(t2buf[:, h, :].unsqueeze(2), f2[:, :, 0:1], f2[:, :, 1:2], ALU.mult).then_inc(updated, 1)
                elif kind == "level":
                    _, m, h = step
                    n = LEVEL_ORDER[step]
                    bank, _ = level_bank(step)
                    dve.wait_ge(step_mm, n + 1)
                    j = P // (2 * m)
                    o = MASK_BASE + 64 * LEVELS.index(m)
                    dst = pbuf[:, h, :].rearrange("p (c j two m) -> p c j two m", c=NCHUNK, two=2, m=m)[:, :, :, 1, :]
                    sc = ps[:, bank:bank + 2, :].rearrange("p a b -> p (a b)").rearrange("p (c j two m) -> p c j two m", c=NCHUNK, two=2, m=m)
                    mk = msk[:, o:o + 64].rearrange("p (j m) -> p j m", m=m).unsqueeze(1).to_broadcast([P, NCHUNK, j, m])
                    dve.copy_predicated(dst, mk, sc[:, :, :, 1, :]).then_inc(merged, 1)
                    tm = block_products(h, m).rearrange("p (b two) -> p b two", two=2)
                    qo = pairs(qbuf[:, h, :], m)[:, :, 1, :]
                    nb = T // (2 * m)
                    dve.wait_ge(updated, before(step))
                    if m == 2:
                        dve.wait_ge(k_updated, before(step))
                    dve.tensor_tensor(qo, qo, tm[:, :, 0:1].to_broadcast([P, nb, m]), ALU.mult)
                    dve.tensor_tensor(block_products(h, 2 * m).unsqueeze(2), tm[:, :, 0:1], tm[:, :, 1:2], ALU.mult).then_inc(updated, 1)
            def fix_rows():
                dve.wait_ge(ld_fix, 32)
                r, b_, a_, g_ = (modfix[0:32, n, :] for n in range(4))
                link(dve.tensor_tensor(r, r, b_, ALU.add))
                link(dve.tensor_tensor(r, r, a_, ALU.add))
                dve.tensor_tensor(r, r, g_, ALU.mult).then_inc(fix_ready, 1)

            fix_rows()

            def head_gate(h):
                dve.wait_ge(osb_ready, h + 1)
                dve.tensor_tensor(gzbuf[:, h, :], gzbuf[:, h, :], kbuf[:, h, :], ALU.mult).then_inc(gzo_ready, 1)

            def head_diag(h):
                dve.wait_ge(hsd_ready, h + 1)
                link(dve.reciprocal(hrt[:, h, :], hrt[:, h, :]))
                dve.tensor_tensor(diag[:, h % 2, :].rearrange("p (c t) -> p c t", c=NCHUNK), ident.unsqueeze(1).to_broadcast([P, NCHUNK, P]),
                                  hrt[:, h, :].unsqueeze(2).to_broadcast([P, NCHUNK, P]), ALU.mult).then_inc(diag_ready, 1)

            def head_norm(h):
                dve.wait_ge(bc_mm, h + 1)
                dve.wait_ge(gzo_ready, h + 1)
                dve.tensor_tensor(gzbuf[:, h, :], gzbuf[:, h, :], ps[:, 6:8, :].rearrange("p a b -> p (a b)"), ALU.mult).then_inc(oa_ready, 1)

            for h in range(HEADS):
                head_gate(h)
                if h:
                    head_norm(h - 1)
                if h + 2 < HEADS:
                    state_chain(h + 2)
                head_diag(h)
                for n in range(3 * h, min(3 * h + 3, KD)):
                    dve.wait_ge(wohi_ready, n + 1)
                    dve.tensor_tensor(wo_lo[:, 2 * n:2 * n + 2, :], ring[n // 4][:, 2 * (n % 4):2 * (n % 4) + 2, :],
                                      wo_hi[:, 2 * n:2 * n + 2, :].bitcast(F32), ALU.subtract).then_inc(wolo_ready, 1)

            def s_low(i, parts=(0, 1)):
                for part in parts:
                    src = (rgbuf, gzbuf)[part]
                    dve.wait_ge(shi_ready, 2 * i + part + 1)
                    if i == 0:
                        dve.wait_ge((ob_ready, oa_ready)[part], 4)
                    split = lambda a: a[:, i % 2, part * CH:(part + 1) * CH].rearrange("p (a b) -> p a b", a=CT)
                    dve.tensor_tensor(split(s_lo), src[:, :, i * P:(i + 1) * P], split(s_hi.bitcast(F32)), ALU.subtract).then_inc(slo_ready, 1)

            s_low(0, (0,))
            head_norm(HEADS - 1)
            s_low(0, (1,))
            s_low(1)
            dve.wait_ge(ld_mod, 32)
            gate1, shift2, scale2 = modbc[:, 0, :], modbc[:, 1, :], modbc[:, 2, :]
            for i in range(NT):
                if i + 2 < NT:
                    s_low(i + 2)
                dve.wait_ge(ss_ready, i + 1)
                link(dve.reciprocal(rst[:, 0, i:i + 1], ssq[:, 0, i:i + 1]))
                mix = ps[:, 2 * (i % 2):2 * (i % 2) + 2, :].rearrange("p a b -> p (a b)")
                link(dve.scalar_tensor_tensor(x1[:, i, :], mix, rst[:, 0, i:i + 1], gate1, ALU.mult, ALU.mult))
                dve.wait_ge(ld_xt[i % 2], 16 * (i // 2 + 1))
                dve.tensor_tensor(x1[:, i, :], x1[:, i, :], xtile[:, i % 2, :], ALU.add).then_inc(x1_ready, 1)
                dve.wait_ge(sd_ready, i + 1)
                link(dve.reciprocal(rst[:, 1, i:i + 1], ssq[:, 1, i:i + 1]))
                if i >= 2:
                    dve.wait_ge(h2_sent, 16 * (i - 1))
                    dve.wait_ge(h2t_mm, i - 1)
                link(dve.scalar_tensor_tensor(h2[:, i % 2, :], x1[:, i, :], rst[:, 1, i:i + 1], scale2, ALU.mult, ALU.mult))
                dve.tensor_tensor(h2[:, i % 2, :], h2[:, i % 2, :], shift2, ALU.add).then_inc(h2_ready, 1)

            as32 = lambda a: a.bitcast(F32)

            def w_low(n, piece, quarters=range(4)):
                for r in quarters:
                    dve.wait_ge(hi_ready, n + (r + 1))
                    dve.tensor_tensor(w_lo[:, r, :], quarter(piece, r), as32(w_hi[:, r, :]), ALU.subtract).then_inc(lo_ready, 1)

            rt = [0]

            def tmp(*shape):
                n = int(np.prod(shape))
                a = scratch[:, rt[0]:rt[0] + n]
                rt[0] += n
                assert rt[0] <= 3 * T
                if len(shape) == 2:
                    a = a.rearrange("p (a b) -> p a b", a=shape[0])
                elif len(shape) == 3:
                    a = a.rearrange("p (a b c) -> p a b c", a=shape[0], b=shape[1])
                return a

            lg = tmp(NT, 36)
            dve.wait_ge(logit_mm, NT)
            o = PARAM["rbias"][0]
            link(dve.tensor_tensor(lg, ps[:, 6, 0:NT * 36].rearrange("p (t e) -> p t e", t=NT),
                                   par[:, o:o + 36].unsqueeze(1).to_broadcast([P, NT, 36]), ALU.add))
            lgg = lg[:, :, 0:NG]
            lge = lg[:, :, NG:].rearrange("p t (g e) -> p t g e", g=NG)
            gmax, emax = tmp(NT, 1), tmp(NT, NG, 1)
            dve.tensor_reduce(gmax, lgg, AX.X, ALU.max)
            link(dve.tensor_reduce(emax, lge, AX.X, ALU.max))
            dve.tensor_tensor(lgg, lgg, gmax.to_broadcast([P, NT, NG]), ALU.subtract)
            dve.tensor_tensor(lge, lge, emax.to_broadcast([P, NT, NG, EPG]), ALU.subtract).then_inc(lg_ready, 1)
            dve.wait_ge(ex_ready, 1)

            def top(vals, n, rev):
                m, w, wm, oh = tmp(NT, 1), tmp(NT, n), tmp(NT, 1), tmp(NT, n)
                link(dve.tensor_reduce(m, vals, AX.X, ALU.max))
                link(dve.tensor_tensor(w, vals, m.to_broadcast([P, NT, n]), ALU.is_equal))
                link(dve.tensor_tensor(w, w, C(rev).unsqueeze(1).to_broadcast([P, NT, n]), ALU.mult))
                link(dve.tensor_reduce(wm, w, AX.X, ALU.max))
                link(dve.tensor_tensor(oh, w, wm.to_broadcast([P, NT, n]), ALU.is_equal))
                return m, oh

            gsum = tmp(NT, 1)
            link(dve.tensor_reduce(gsum, lgg, AX.X, ALU.add))
            link(dve.reciprocal(gsum, gsum))
            gm, ohg = top(lgg, NG, "rev4")
            gate = tmp(NT, 1)
            link(dve.tensor_tensor(gate, gm, gsum, ALU.mult))
            picked = tmp(NT, EPG, NG)
            se = tmp(NT, EPG)
            link(dve.tensor_tensor(picked, lge.rearrange("p t g e -> p t e g"), ohg.unsqueeze(2).to_broadcast([P, NT, EPG, NG]), ALU.mult))
            link(dve.tensor_reduce(se.unsqueeze(3), picked, AX.X, ALU.add))
            esum = tmp(NT, 1)
            link(dve.tensor_reduce(esum, se, AX.X, ALU.add))
            link(dve.reciprocal(esum, esum))
            m1, oh1 = top(se, EPG, "rev8")
            se2 = tmp(NT, EPG)
            link(dve.scalar_tensor_tensor(se2, oh1, -2.0, se, ALU.mult, ALU.add))
            m2, oh2 = top(se2, EPG, "rev8")
            p1, p2, den = tmp(NT, 1), tmp(NT, 1), tmp(NT, 1)
            dve.tensor_tensor(p1, m1, esum, ALU.mult)
            link(dve.tensor_tensor(p2, m2, esum, ALU.mult))
            link(dve.tensor_tensor(den, p1, p2, ALU.add))
            link(dve.reciprocal(den, den))
            link(dve.tensor_tensor(den, den, gate, ALU.mult))
            dve.tensor_tensor(wtok[:, 0, :].unsqueeze(2), p1, den, ALU.mult)
            dve.tensor_tensor(wtok[:, 1, :].unsqueeze(2), p2, den, ALU.mult)
            m_j = [tmp(NT, NE) for _ in range(2)]
            for j, oh in enumerate((oh1, oh2)):
                link(dve.tensor_tensor(m_j[j].rearrange("p t (g e) -> p t g e", g=NG), ohg.unsqueeze(3).to_broadcast([P, NT, NG, EPG]),
                                       oh.unsqueeze(2).to_broadcast([P, NT, NG, EPG]), ALU.mult))
            dve.memset(m_pre[:, 0, :], 0.0)
            link(dve.tensor_tensor(m_all, m_j[0], m_j[1], ALU.add))
            for i in range(NT):
                ins = dve.tensor_tensor(m_pre[:, i + 1, :], m_pre[:, i, :], m_all[:, i, :], ALU.add)
                if i < NT - 1:
                    link(ins)
            ins.then_inc(mm_ready, 1)
            w_low(0, m_slots[0], (0, 1))
            dve.wait_ge(rank_mm, 1)
            rank, cnt = ps[:, 0, 0:NT * NE].rearrange("p (t e) -> p t e", t=NT), ps[:, 1, 0:NE]
            n_i, n_f, end, beg = tmp(NE).bitcast(I32), tmp(NE), tmp(NE), tmp(NE)
            link(dve.tensor_scalar(n_f, cnt, 1.0, -1.0, ALU.max, ALU.add))
            link(dve.tensor_copy(n_i, n_f))
            link(dve.tensor_scalar(n_i, n_i, 7, None, ALU.logical_shift_right))
            link(dve.tensor_copy(n_f, n_i))
            link(dve.tensor_tensor_scan(end, C("ones")[:, 0:NE], n_f, 0.0, ALU.mult, ALU.add))
            link(dve.tensor_tensor(beg, end, n_f, ALU.subtract))
            codes, code, own, prod = tmp(NT, NE), tmp(2, NT, 1), tmp(NE), tmp(NT, NE)
            assert T <= 1 << 10 and N_OVER < 16 and NE <= 32
            link(dve.scalar_tensor_tensor(own, beg, 32.0, C("iota32"), ALU.mult, ALU.add))
            link(dve.scalar_tensor_tensor(codes, rank, 512.0, own.unsqueeze(1).to_broadcast([P, NT, NE]), ALU.mult, ALU.add))
            for j in range(2):
                link(dve.tensor_tensor(prod, m_j[j], codes, ALU.mult))
                link(dve.tensor_reduce(code[:, j], prod, AX.X, ALU.add))
            c_i, b_i, s_i, o_i, e_i = (tmp(16).bitcast(I32) for _ in range(5))
            b_f, s_f, is_o, blk, ej, oj = (tmp(16) for _ in range(6))
            link(dve.tensor_copy(c_i, code.rearrange("p j t o -> p (j t o)")))
            dve.tensor_scalar(b_i, c_i, 16, None, ALU.logical_shift_right)
            dve.tensor_scalar(s_i, c_i, 9, None, ALU.logical_shift_right)
            dve.tensor_scalar(o_i, c_i, 5, None, ALU.logical_shift_right)
            link(dve.tensor_scalar(e_i, c_i, NE - 1, None, ALU.bitwise_and))
            dve.tensor_scalar(s_i, s_i, P - 1, None, ALU.bitwise_and)
            link(dve.tensor_scalar(o_i, o_i, 15, None, ALU.bitwise_and))
            for dst, src in ((b_f, b_i), (s_f, s_i), (ej, e_i)):
                dve.tensor_copy(dst, src)
            link(dve.tensor_copy(oj, o_i))
            link(dve.tensor_scalar(is_o, b_f, 1.0, None, ALU.min))
            link(dve.tensor_tensor(blk, oj, b_f, ALU.add))
            link(dve.scalar_tensor_tensor(blk, blk, float(NE - 1), ej, ALU.add, ALU.subtract))
            link(dve.tensor_tensor(blk, blk, is_o, ALU.mult))
            link(dve.tensor_tensor(blk, blk, ej, ALU.add))
            for n in range(0, 16, 4):
                if n >= 8:
                    dve.wait_ge(tab_mm, n - 4)
                q = n // 4 % 2
                wide = lambda a, m: a.unsqueeze(1).to_broadcast([P, 4, m])
                each = lambda a, m: a.unsqueeze(2).to_broadcast([P, 4, m])
                o = CONST["tok"][0] + n
                dve.tensor_tensor(a_oh[:, q], wide(C("iota128"), P), each(s_f[:, n:n + 4], P), ALU.is_equal)
                link(dve.tensor_tensor(b_oh[:, q], wide(C("iota47"), N_BLOCKS), each(blk[:, n:n + 4], N_BLOCKS), ALU.is_equal))
                dve.tensor_tensor(b_oh[:, q], b_oh[:, q], each(con[:, o:o + 4], N_BLOCKS), ALU.mult).then_inc(ab_ready, 1)
            cmp = tmp(N_OVER, NE)
            ov = tmp(16)
            link(dve.tensor_tensor(cmp, end.unsqueeze(1).to_broadcast([P, N_OVER, NE]), C("iota15").unsqueeze(2).to_broadcast([P, N_OVER, NE]), ALU.is_le))
            link(dve.tensor_reduce(ov[:, 0:N_OVER].unsqueeze(2), cmp, AX.X, ALU.add))
            link(dve.tensor_scalar(ov[:, 0:N_OVER], ov[:, 0:N_OVER], float(NE - 1), None, ALU.min))
            link(dve.tensor_copy(ov[:, 15:16], end[:, NE - 1:NE]))
            link(dve.tensor_copy(over, ov))
            dve.wait_ge(tab_mm, 16)
            link(dve.tensor_scalar(tbl, ps[:, 2, 0:N_BLOCKS], float(UNUSED), None, ALU.add))
            spare = tmp(N_BLOCKS).bitcast(I32)
            dve.tensor_scalar(spare, tbl, UNUSED, None, ALU.bitwise_and)
            link(dve.tensor_scalar(ttab, tbl, T - 1, None, ALU.bitwise_and))
            dve.tensor_tensor(ttab, ttab, spare, ALU.add).then_inc(route_ready, 1)

            def x_low(b, q):
                dve.wait_ge(xt_ready, b + 1)
                dve.tensor_tensor(x_lo[:, q, :], ps[:, 6:8, :].rearrange("p a b -> p (a b)"), as32(x_hi[:, q, :]), ALU.subtract).then_inc(xlo_ready, 1)

            def g_low(b):
                dve.wait_ge(ghi_ready, b + 1)
                dve.tensor_tensor(g_lo, ps[:, 2, :], as32(g_hi), ALU.subtract).then_inc(glo_ready, 1)

            def g_out(b, h3_done):
                dve.wait_ge(sil_ready, b + 1)
                dve.wait_ge(w_used, h3_done)
                dve.tensor_tensor(sil, sil, ps[:, 1, :], ALU.mult).then_inc(g_ready, 1)

            def y_half(y_done):
                dve.wait_ge(w_used, y_done)
                dve.tensor_copy(y_sb[:, HALF:D], ps[:, 4, :]).then_inc(y_dve, 1)

            w_low(0, m_slots[0], (2, 3))
            x_low(0, 0)
            w_low(4, m_slots[1])
            g_out(0, 8)
            x_low(1, 1)
            w_low(8, m_slots[2])

            def block_step(b, n, q, sent, last=False):
                s3, s2, s1 = (3, 4, 5) if q == 1 else (0, 1, 2)
                w_low(n, m_slots[s3])
                g_low(b - 1)
                w_low(n + 4, m_slots2[s2])
                g_out(b, n + 4)
                if not last:
                    x_low(b + 1, 1 - q)
                w_low(n + 8, m_slots[s1] if not last else m_slots2[s1])
                if b is not first:
                    dve.wait_ge(y_sent[q], sent)
                y_half(n + 8)

            first = 1
            block_step(first, 12, 1, 0)
            block_step(2, 24, 0, 16)
            with dve.Fori(0, (NE - 4) // 2) as i:
                block_step(2 * i + 3, 24 * i + 36, 1, 16 * i + 16)
                block_step(2 * i + 4, 24 * i + 48, 0, 16 * i + 32)
            b = NE - 1
            block_step(b, 12 * b, 1, 16 * (b // 2), last=True)
            g_low(b)
            dve.wait_ge(y_sent[0], 8 * NE)
            y_half(12 * b + 12)
            n_over = dve.value_load(over[0:1, 15:16], min_val=0, max_val=N_OVER)
            with dve.If(n_over > 0):
                with dve.Fori(0, N_OVER) as o:
                    with dve.If(o < n_over):
                        dve.wait_ge(ov_xhi, o + 1)
                        dve.tensor_tensor(x_lo[:, 0, :], ps[:, 6:8, :].rearrange("p a b -> p (a b)"), as32(x_hi[:, 0, :]), ALU.subtract).then_inc(ov_xlo, 1)
                        for n in range(12):
                            if n == 8:
                                dve.wait_ge(ov_sil, o + 1)
                                dve.wait_ge(ov_used, 12 * o + 8)
                                dve.tensor_tensor(sil, sil, ps[:, 1, :], ALU.mult).then_inc(ov_g, 1)
                            dve.wait_ge(ov_hi, 12 * o + (n + 1))
                            dve.tensor_tensor(w_lo[:, n % 4, :], quarter((m_slots[0], m_slots[1], m_slots2[2])[n // 4], n % 4), as32(w_hi[:, n % 4, :]),
                                              ALU.subtract).then_inc(ov_lo, 1)
                        dve.wait_ge(ov_ghi, o + 1)
                        dve.tensor_tensor(g_lo, ps[:, 2, :], as32(g_hi), ALU.subtract).then_inc(ov_glo, 1)
                        stand(dve, ov_sent, 16 * (o + 1))
            def second_row(i):
                dve.wait_ge(fin_a, i + 1)
                dve.wait_ge(ld_y[i], 16)
                y = y_sum[:, i % 2, :]
                dve.scalar_tensor_tensor(y, y_pair[:, i, 1, :], wtok[:, 1, i:i + 1], y, ALU.mult, ALU.add).then_inc(fin_b, 1)

            second_row(0)
            for i in range(NT):
                y = y_sum[:, i % 2, :]
                if i + 1 < NT:
                    second_row(i + 1)
                dve.wait_ge(fin_s, i + 1)
                link(dve.reciprocal(rst[:, 2, i:i + 1], ssq[:, 2, i:i + 1]))
                if i >= 2:
                    dve.wait_ge(o_sent[i % 2], 16 * (i // 2))
                dve.scalar_tensor_tensor(o_tile[:, i % 2, :], y, rst[:, 2, i:i + 1], gate2, ALU.mult, ALU.mult).then_inc(fin_g, 1)
                dve.wait_ge(fin_g, i + 1)
                dve.tensor_tensor(o_tile[:, i % 2, :], o_tile[:, i % 2, :], x1[:, i, :], ALU.add).then_inc(fin_o, 1)

        @block.tensor
        def _(pe):
            mm = nc.tensor.matmul
            pe.wait_ge(ld_con, 16)
            for k in range(KD):
                pe.wait_ge(sq_ready, k + 1)
                for half in range(2):
                    ins = mm(ps[:, half, :], ones, sq[:, k % 2, half * HALF:(half + 1) * HALF], start=k == 0, stop=k == KD - 1)
                ins.then_inc(sq_summed, 1)
            pe.wait_ge(cs_ready, 1)
            for n in range(2):
                pe.wait_ge(acc_ready, n + 1)
                for j in range(4):
                    ins = mm(ps[:, 2, 4 * n + j:4 * n + j + 1], acc_early[:, n, j * P:(j + 1) * P], ones[:, 0:1], start=True, stop=True)
                ins.then_inc(modc_ready, 1)
                pe.wait_ge(ld_early[2 + n], 16)
                for k in range(KD):
                    ins = mm(ps[0:1, 3 + n, :], cs[:, k:k + 1], early[2 + n][:, k, :], start=k == 0, stop=k == KD - 1)
                ins.then_inc(erow_mm, 1)
            for n in range(2):
                pe.wait_ge(erow_ready, n + 1)
                for j in range(4):
                    o = (4 * n + j) * P
                    ins = mm(ps[:, 2, 8 + 4 * n + j:9 + 4 * n + j], early_row[0:1, o:o + P], ones[0:1, 0:1], start=True, stop=True)
                ins.then_inc(modc_ready, 1)
            def products(out_, xh, xl, wh, wl, first_, last_):
                mm(out_, xh, wh, start=first_, stop=False)
                mm(out_, xh, wl, start=False, stop=False)
                return mm(out_, xl, wh, start=False, stop=last_)

            def k_transposes(h):
                pe.wait_ge(updated, LEVEL_ORDER[("level", LEVELS[-1], h)] + 1)
                pe.wait_ge(k_updated, LEVEL_ORDER[("level", LEVELS[-1], h)] + 1)
                if h == 0:
                    pe.wait_ge(evac_done, len(GROUPS))
                    pe.wait_ge(row_ready, 16)
                else:
                    pe.wait_ge(kt_ready, h)
                o_ = ps[:, 0:2, :].rearrange("p a b -> p (a b)")
                for c in range(NCHUNK):
                    ins = nc.tensor.transpose(o_[:, c * P:(c + 1) * P], kbuf[:, h, c * P:(c + 1) * P], ident)
                ins.then_inc(kt_mm, 1)

            def state_sums(h):
                pe.wait_ge(kt_ready, h + 1)
                if h:
                    pe.wait_ge(st_ready, h)
                o_ = ps[:, 2:4, :].rearrange("p a b -> p (a b)")
                for c in range(NCHUNK - 1):
                    ins = mm(o_[:, c * P:(c + 1) * P], k_nat[:, h % 2, c * P:(c + 1) * P], vbuf[:, c, h * P:(h + 1) * P], start=True, stop=True)
                ins.then_inc(ds_mm, 1)

            def project(name, a, half, k):
                n = PIECES.index(name)
                out_ = ps[:, GROUPS[(name, a, half)] % 3, :]
                t, c = slice(half * HALF, (half + 1) * HALF), slice(a * P, (a + 1) * P)
                if name == "f":
                    return mm(out_, ring[n % 2][:, k, c], hT[:, k, t], start=k == 0, stop=k == KD - 1)
                wh, wl = win_hi[name][:, k, :], ring_lo[:, KD * (n % 2) + k, :]
                if name == "iv":
                    return products(out_, h_hi[:, k, c], h_lo(k)[:, c], wh, wl, k == 0, k == KD - 1)
                return products(out_, wh[:, c], wl[:, c], h_hi[:, k, t], h_lo(k)[:, t], k == 0, k == KD - 1)

            TRIPLE = {name: [(name, 0, 0), (name, 0, 1), (name, 1, 0)] for name in ("xr", "f")}

            for step in STEPS:
                kind = step[0]
                if kind == "proj":
                    _, name, a, half = step
                    group = step[1:]
                    g = GROUPS[group]
                    n = PIECES.index(name)
                    triple = TRIPLE.get(name, [])
                    if group in triple[1:]:
                        continue
                    together = triple if group in triple else [group]
                    if g == 0:
                        pe.wait_ge(rms_ready, 1)
                        pe.wait_ge(a1_ready, 1)
                    else:
                        pe.wait_ge(evac_done, g + len(together) - 3)
                    if group == (name, 0, 0) and name == "f":
                        pe.wait_ge(ld_ring[n % 2], 16 * (n // 2 + 1))
                    for k in range(KD):
                        if group == (name, 0, 0):
                            if name == "f":
                                pe.wait_ge(restored, k + 1)
                            elif k % 2 == 0:
                                pe.wait_ge(wlo_ready, 4 * n + k // 2 + 1)
                            if name == "xr":
                                pe.wait_ge(hlo_ready, k + 1)
                        for one in together:
                            ins = project(*one, k)
                            if k == KD - 1:
                                ins.then_inc(proj_done, 1)
                elif kind == "head":
                    k_transposes(step[1])
                    state_sums(step[1])
                elif kind == "gate":
                    ct = step[1]
                    pe.wait_ge(conv_done, ct + 1)
                    pe.wait_ge(ld_bd, 64)
                    if ct:
                        pe.wait_ge(gates_ready, 4 * ct)
                    for g in range(2):
                        for half in range(2):
                            ins = mm(ps[:, 4 + 2 * g + half, :], bd[:, g, ct, :], xc[:, half * HALF:(half + 1) * HALF], start=True, stop=True)
                    ins.then_inc(gate_mm, 1)
                elif kind == "rg_norm":
                    pe.wait_ge(gates_ready, 4 * CT)
                    for ct in range(CT):
                        pe.wait_ge(rgsq_ready, ct + 1)
                        for half in range(2):
                            ins = mm(ps[:, 4 + half, :], ones, (xc, rgate)[ct % 2][:, half * HALF:(half + 1) * HALF], start=ct == 0, stop=ct == CT - 1)
                        ins.then_inc(rgsq_summed, 1)
                elif kind == "row":
                    u = step[1]
                    pe.wait_ge(acc_ready, 2 + u + 1)
                    if u:
                        pe.wait_ge(row_ready, u)
                    mm(ps[0:1, 3, (u % 2) * 256:(u % 2) * 256 + 256], ones[:, 0:1], acc[:, u % 2, :], start=True, stop=True).then_inc(row_mm, 1)
                elif kind in ("base", "level"):
                    n = LEVEL_ORDER[step]
                    bank, free = level_bank(step)
                    h = step[-1]
                    if n == 0:
                        pe.wait_ge(rgrms_ready, 1)
                    if free:
                        pe.wait_ge(merged, free)
                    if kind == "base":
                        pe.wait_ge(prep_done, h + 1)
                    else:
                        pe.wait_ge(updated, before(step))
                        pe.wait_ge(k_updated, before(step))
                    out_ = ps[:, bank:bank + 2, :].rearrange("p a b -> p (a b)")
                    for c in range(NCHUNK):
                        ins = mm(out_[:, c * P:(c + 1) * P], kbuf[:, h, c * P:(c + 1) * P], qbuf[:, h, c * P:(c + 1) * P], start=True, stop=True)
                    ins.then_inc(step_mm, 1)

            def outputs(h):
                pe.wait_ge(st_ready, h + 1)
                if h:
                    pe.wait_ge(osb_ready, h)
                o_ = ps[:, 4:6, :].rearrange("p a b -> p (a b)")
                for c in range(NCHUNK):
                    dst = o_[:, c * P:(c + 1) * P]
                    ins = mm(dst, vbuf[:, c, h * P:(h + 1) * P], pbuf[:, h, c * P:(c + 1) * P], start=True, stop=c == 0)
                    if c:
                        ins = mm(dst, states[:, h % 2, c * P:(c + 1) * P], qbuf[:, h, c * P:(c + 1) * P], start=False, stop=True)
                ins.then_inc(o_mm, 1)

            def output_sums(h):
                if h == 1:
                    pe.wait_ge(oa_ready, h)
                elif h >= 2:
                    pe.wait_ge(st_ready, HEADS)
                pe.wait_ge(osq_ready, h + 1)
                for c in range(NCHUNK):
                    ins = mm(ps[:, sums_bank(h), c:c + 1], osq[:, h % 2, c * P:(c + 1) * P], ones[:, 0:1], start=True, stop=True)
                ins.then_inc(os_mm, 1)

            def root_rows(h):
                pe.wait_ge(diag_ready, h + 1)
                if h:
                    pe.wait_ge(oa_ready, h)
                for half in range(2):
                    ins = mm(ps[:, 6 + half, :], ones, diag[:, h % 2, half * HALF:(half + 1) * HALF], start=True, stop=True)
                ins.then_inc(bc_mm, 1)

            pe.wait_ge(updated, len(LEVEL_ORDER))
            pe.wait_ge(merged, len(LEVEL_ORDER))
            for h in range(HEADS):
                outputs(h)
                if h:
                    root_rows(h - 1)
                if h + 2 < HEADS:
                    k_transposes(h + 2)
                output_sums(h)
                if h + 2 < HEADS:
                    state_sums(h + 2)
            def mix_part(i, half, part):
                for k in range(CT * part, CT * part + CT):
                    ks, w = slice(k * P, (k + 1) * P), KD * half + (k + CT) % KD
                    ins = products(ps[:, 2 * (i % 2) + half, :], s_hi[:, i % 2, ks], s_lo[:, i % 2, ks], wo_hi[:, w, :], wo_lo[:, w, :],
                                   k == 0, k == KD - 1)
                return ins

            def mix(i):
                if i >= 2:
                    pe.wait_ge(x1_ready, i - 1)
                pe.wait_ge(slo_ready, 2 * i + 2)
                for half in range(2):
                    mix_part(i, half, 0)
                    ins = mix_part(i, half, 1)
                ins.then_inc(mix_mm, 1)

            def h2_transposes(i):
                pe.wait_ge(h2_ready, i + 1)
                if i:
                    pe.wait_ge(h2t_ready, i)
                else:
                    pe.wait_ge(oa_ready, HEADS)
                o_ = ps[:, 4:6, :].rearrange("p a b -> p (a b)")
                for k in range(KD):
                    ins = nc.tensor.transpose(o_[:, k * P:(k + 1) * P], h2[:, i % 2, k * P:(k + 1) * P], ident)
                ins.then_inc(h2t_mm, 1)

            def logits(i):
                pe.wait_ge(h2t_ready, i + 1)
                for k in range(KD):
                    ins = mm(ps[:, 6, 36 * i:36 * i + 36], h2T[:, i % 2, k * P:(k + 1) * P], wrt[:, k, :], start=k == 0, stop=k == KD - 1)
                ins.then_inc(logit_mm, 1)

            pe.wait_ge(wolo_ready, 8)
            pe.wait_ge(ld_wrt, 16)
            pe.wait_ge(slo_ready, 1)
            mix_part(0, 0, 0)
            mix_part(0, 1, 0)
            root_rows(HEADS - 1)
            pe.wait_ge(slo_ready, 2)
            mix_part(0, 0, 1)
            mix_part(0, 1, 1).then_inc(mix_mm, 1)
            mix(1)
            for i in range(NT):
                h2_transposes(i)
                if i + 2 < NT:
                    mix(i + 2)
                logits(i)
            pe.wait_ge(mm_ready, 1)
            flat = lambda a: a.rearrange("p t e -> p (t e)")
            mm(ps[:, 0, 0:NT * NE], C("upper"), flat(m_all), start=True, stop=False)
            mm(ps[:, 0, 0:NT * NE], ones, flat(m_pre[:, 0:NT, :]), start=False, stop=True)
            mm(ps[:, 1, 0:NE], ones, m_pre[:, NT, :], start=True, stop=True).then_inc(rank_mm, 1)
            for n in range(16):
                pe.wait_ge(ab_ready, n // 4 + 1)
                mm(ps[:, 2, 0:N_BLOCKS], a_oh[:, n // 4 % 2, n % 4, :], b_oh[:, n // 4 % 2, n % 4, :], start=n == 0, stop=n == 15).then_inc(tab_mm, 1)

            def x_transposes(b, q, loaded, wait_prev=True):
                pe.wait_ge(ld_g[q], loaded)
                if wait_prev:
                    pe.wait_ge(xlo_ready, b)
                o_ = ps[:, 6:8, :].rearrange("p a b -> p (a b)")
                for k in range(KD):
                    ins = nc.tensor.transpose(o_[:, k * P:(k + 1) * P], x_ring[:, q, k * P:(k + 1) * P], ident)
                ins.then_inc(xg_tr, 1)

            def hidden(bank, q, n, lo_s, used_s):
                for r in range(4):
                    pe.wait_ge(lo_s, n + (r + 1))
                    for kk in range(2):
                        k = 2 * r + kk
                        xs, ws = slice(k * P, (k + 1) * P), slice(kk * HALF, (kk + 1) * HALF)
                        ins = products(ps[:, bank, :], x_hi[:, q, xs], x_lo[:, q, xs], w_hi[:, r, ws], w_lo[:, r, ws], k == 0, k == KD - 1)
                    ins.then_inc(used_s, 1)

            def g_transposes(b):
                pe.wait_ge(g_ready, b + 1)
                for k in range(KF):
                    ins = nc.tensor.transpose(ps[:, 2, k * P:(k + 1) * P], sil[:, k * P:(k + 1) * P], ident)
                ins.then_inc(g_tr, 1)

            def down(n, lo_s, used_s):
                for r in range(KF):
                    pe.wait_ge(lo_s, n + (r + 1))
                    gs = slice(r * P, (r + 1) * P)
                    for half in range(2):
                        ws = slice(half * HALF, (half + 1) * HALF)
                        ins = products(ps[:, 3 + half, :], g_hi[:, gs], g_lo[:, gs], w_hi[:, r, ws], w_lo[:, r, ws], r == 0, r == KF - 1)
                    ins.then_inc(used_s, 1)

            pe.wait_ge(route_ready, 1)
            x_transposes(0, 0, 16, wait_prev=False)
            pe.wait_ge(xlo_ready, 1)
            hidden(0, 0, 0, lo_ready, w_used)
            hidden(1, 0, 4, lo_ready, w_used)
            x_transposes(1, 1, 16)

            def block_step(b, n, q, n_g, last=False):
                pe.wait_ge(xlo_ready, b + 1)
                pe.wait_ge(sil_ready, b)
                hidden(0, q, n - 4, lo_ready, w_used)
                g_transposes(b - 1)
                hidden(1, q, n, lo_ready, w_used)
                if not last:
                    x_transposes(b + 1, 1 - q, n_g)
                pe.wait_ge(glo_ready, b)
                if b is not first:
                    pe.wait_ge(y_act, b - 1)
                    pe.wait_ge(y_dve, b - 1)
                down(n + 4, lo_ready, w_used)

            first = 1
            block_step(first, 12, 1, 32)
            block_step(2, 24, 0, 32)
            with pe.Fori(0, (NE - 4) // 2) as i:
                block_step(2 * i + 3, 24 * i + 36, 1, 16 * i + 48)
                block_step(2 * i + 4, 24 * i + 48, 0, 16 * i + 48)
            b = NE - 1
            block_step(b, 12 * b, 1, 0, last=True)
            g_transposes(b)
            pe.wait_ge(glo_ready, b + 1)
            pe.wait_ge(y_act, b)
            pe.wait_ge(y_dve, b)
            down(12 * b + 8, lo_ready, w_used)
            n_over = pe.value_load(over[0:1, 15:16], min_val=0, max_val=N_OVER)
            pe.wait_ge(y_act, NE)
            pe.wait_ge(y_dve, NE)
            with pe.If(n_over > 0):
                with pe.Fori(0, N_OVER) as o:
                    with pe.If(o < n_over):
                        pe.wait_ge(ov_x, 16 * (o + 1))
                        o_ = ps[:, 6:8, :].rearrange("p a b -> p (a b)")
                        for k in range(KD):
                            ins = nc.tensor.transpose(o_[:, k * P:(k + 1) * P], x_ring[:, 0, k * P:(k + 1) * P], ident)
                        ins.then_inc(ov_xtr, 1)
                        pe.wait_ge(ov_xlo, o + 1)
                        hidden(0, 0, 12 * o, ov_lo, ov_used)
                        hidden(1, 0, 12 * o + 4, ov_lo, ov_used)
                        pe.wait_ge(ov_g, o + 1)
                        for k in range(KF):
                            ins = nc.tensor.transpose(ps[:, 2, k * P:(k + 1) * P], sil[:, k * P:(k + 1) * P], ident)
                        ins.then_inc(ov_gtr, 1)
                        pe.wait_ge(ov_glo, o + 1)
                        down(12 * o + 8, ov_lo, ov_used)
                        stand(pe, ov_sent, 16 * (o + 1))



def kernel(**inputs):
    import concourse.bacc as _bacc
    from concourse.bass_utils import run_bass_kernel_spmd as _run

    a = {k: np.asarray(v) for k, v in inputs.items()}
    col = lambda v: np.ascontiguousarray(v.reshape(-1, P).T)
    cols = {
        "c": col(a["c"][0]), "g_pre": col(a["g_pre_mix"][0]), "b_ada": col(a["b_ada"][0, :2 * D]),
        "gam0": col(a["hgrn_gamma"][0]), "gam1": col(a["hgrn_gamma"][1]), "hg": col(a["hgrn_norm_g"][0]),
        "cw0": col(a["conv_w"][0, 0]), "cw1": col(a["conv_w"][0, 1]), "cw2": col(a["conv_w"][0, 2]), "cw3": col(a["conv_w"][0, 3]),
        "cb": col(a["conv_b"][0]), "br": col(a["rg_b_r"][0]), "bi": col(a["rg_b_i"][0]), "lam": col(a["rg_lambda"][0]),
        "rgg": col(a["rg_norm_g"][0]),
        "rbias": np.broadcast_to(np.concatenate([a["b_router_group"][0], a["b_router_expert"][0]]), (P, 36)),
    }
    params = np.concatenate([cols[n] for n in PARAM], axis=1)
    i128 = np.arange(P)
    const = {
        "ident": np.eye(P), "ones": np.ones((P, P)), "upper": (i128[:, None] < i128[None, :]),
        "iota128": np.broadcast_to(i128, (P, P)), "iota47": np.broadcast_to(np.arange(N_BLOCKS), (P, N_BLOCKS)),
        "iota32": np.broadcast_to(np.arange(NE), (P, NE)), "iota15": np.broadcast_to(np.arange(N_OVER), (P, N_OVER)),
        "tok": i128[:, None] + P * np.arange(2 * NT)[None, :] - UNUSED, "rev4": np.broadcast_to(np.arange(4, 0, -1), (P, 4)),
        "rev8": np.broadcast_to(np.arange(8, 0, -1), (P, 8)),
    }
    consts = np.concatenate([np.asarray(const[n], np.float32) for n in CONST], axis=1)
    s, t = i128[:, None], i128[None, :]
    mask = [(s // 2 == t // 2) & (s <= t)]
    for m in LEVELS:
        u = np.arange(64)[None, :]
        mask.append((s // (2 * m) == u // m) & ((s // m) % 2 == 0))
    masks = np.concatenate(mask, axis=1).astype(np.int32)
    g = {0: a["g_post_mix"][0], 2: a["g_pre_ffn"][0], 3: a["g_post_ffn"][0]}
    gain = np.concatenate([g.get(i, np.ones(D, np.float32)) for i in range(4)]).reshape(32, P)
    addend = np.zeros((32, P), np.float32)
    addend[16:24] = 1.0
    mod_rows = np.stack([a["b_ada"][0, 2 * D:].reshape(32, P), addend, gain], axis=1)
    w_route = np.concatenate([a["w_router_group"][0], a["w_router_expert"][0]], axis=1).reshape(KD, P, 36).transpose(1, 0, 2)
    arrays = {
        "x": a["x"][0], "x_t": a["x"][0].T, "params": params, "consts": consts, "masks": masks, "w_ada": a["w_ada"][0],
        "mod_rows": mod_rows, "w_in": a["w_in"][0], "w_r": a["rg_w_r"][0], "w_i": a["rg_w_i"][0], "w_out": a["w_out"][0],
        "w_route": w_route, "w1": a["w1"][0], "w3": a["w3"][0], "w2": a["w2"][0],
    }
    arrays = {f"in_{k}": np.ascontiguousarray(v) for k, v in arrays.items()}
    nc = _bacc.Bacc("TRN2", target_bir_lowering=False, num_devices=1)
    args = [nc.dram_tensor(k, v.shape, mybir.dt.from_np(v.dtype), kind="ExternalInput").ap() for k, v in arrays.items()]
    out = nc.dram_tensor("out_0", (T, D), F32, kind="ExternalOutput").ap()
    build(nc, *args, out)
    r = _run(nc, [arrays], core_ids=[0])
    return r.results[0]["out_0"].reshape(1, T, D)
```
